# Optimizing a Trainium2 kernel written in Bass

```python
import jax, jax.numpy as jnp
from jax import lax
import numpy as np

D_MODEL = 1024
BATCH = 1
SEQ = 1024
DEPTH = 1

CHUNK = 64
MIX_WIDTH = D_MODEL
HG_HEADS = 4
HG_DK = 128
HG_DV = 128
HG_WIDTH = HG_HEADS * HG_DV
SW_HEADS = 8
SW_KV_HEADS = 2
SW_GROUP = SW_HEADS // SW_KV_HEADS
SW_HEAD_DIM = 64
SW_WIDTH = SW_HEADS * SW_HEAD_DIM
SW_WINDOW = 128
SW_WIN_CHUNKS = SW_WINDOW // CHUNK
IN_SIZES = (HG_HEADS * HG_DK, HG_HEADS * HG_DK, HG_WIDTH, HG_WIDTH,
            SW_WIDTH, SW_KV_HEADS * SW_HEAD_DIM, SW_KV_HEADS * SW_HEAD_DIM)
IN_OFFS = tuple(int(v) for v in np.cumsum((0,) + IN_SIZES))
IN_COLS = IN_OFFS[-1]
PEER_HEADS = 8
PEER_NKEYS = 128
PEER_NEXP = PEER_NKEYS * PEER_NKEYS
PEER_DKEY = 256
PEER_HALF = PEER_DKEY // 2
PEER_TOPK = 16
PEER_BLOCK = 128
RMS_EPS = 1e-6

kernel_name = "hymba_hgrn2_swa_peer_block"

def _rmsnorm(x, g):
    xf = x.astype(jnp.float32)
    y = xf * lax.rsqrt(jnp.mean(xf * xf, axis=-1, keepdims=True) + RMS_EPS)
    return (y * g.astype(jnp.float32)).astype(x.dtype)

def _alibi_slopes(n):
    return 2.0 ** (-8.0 * (np.arange(1, n + 1, dtype=np.float32) / n))

def _to_chunks(t):
    B, S, H, D = t.shape
    return t.reshape(B, S // CHUNK, CHUNK, H, D).transpose(1, 0, 3, 2, 4)

def _hgrn2_scan(q, k, v, g):
    B, S, H, _ = q.shape
    qc, kc, vc, gc = _to_chunks(q), _to_chunks(k), _to_chunks(v), _to_chunks(g)
    causal = jnp.tril(jnp.ones((CHUNK, CHUNK), dtype=bool))[:, :, None]

    def step(state, inp):
        qb, kb, vb, gb = inp
        b = jnp.cumsum(gb, axis=2)
        o_inter = jnp.einsum('bhtd,bhde->bhte', qb * jnp.exp(b), state)
        diff = b[:, :, :, None, :] - b[:, :, None, :, :]
        decay = jnp.exp(jnp.where(causal, diff, -jnp.inf))
        attn = jnp.einsum('bhtd,bhsd,bhtsd->bhts', qb, kb, decay)
        o = o_inter + jnp.einsum('bhts,bhse->bhte', attn, vb)
        b_last = b[:, :, -1:, :]
        new_state = (jnp.exp(b_last[:, :, 0, :])[..., None] * state
                     + jnp.einsum('bhsd,bhse->bhde', kb * jnp.exp(b_last - b), vb))
        return new_state, o

    s0 = jnp.zeros((B, H, q.shape[-1], v.shape[-1]), jnp.float32)
    _, o = lax.scan(step, s0, (qc, kc, vc, gc))
    return o.transpose(1, 0, 3, 2, 4).reshape(B, S, H, v.shape[-1])

def _hgrn2_group(q_raw, f_raw, i_raw, gate_raw, lb, norm_g):
    B, S, _ = q_raw.shape
    dt = q_raw.dtype
    q = jax.nn.silu(q_raw.astype(jnp.float32)).reshape(B, S, HG_HEADS, HG_DK)
    z = f_raw.astype(jnp.float32).reshape(B, S, HG_HEADS, HG_DK)
    lbh = lb.astype(jnp.float32).reshape(HG_HEADS, HG_DK)
    log_f = jnp.logaddexp(jnp.log(lbh), jnp.log1p(-lbh) + jax.nn.log_sigmoid(z))
    k = (1.0 - lbh) * jax.nn.sigmoid(-z)
    v = i_raw.astype(jnp.float32).reshape(B, S, HG_HEADS, HG_DV)
    o = _hgrn2_scan(q, k, v, log_f)
    o = o * lax.rsqrt(jnp.mean(o * o, axis=-1, keepdims=True) + RMS_EPS)
    o = o.reshape(B, S, HG_WIDTH) * norm_g.astype(jnp.float32)
    o = o * jax.nn.silu(gate_raw.astype(jnp.float32))
    return o.astype(dt)

def _swa_group(q_raw, k_raw, v_raw, sinks):
    B, S, _ = q_raw.shape
    nC = S // CHUNK
    W = SW_WIN_CHUNKS
    L = W * CHUNK
    q = q_raw.reshape(B, nC, CHUNK, SW_KV_HEADS, SW_GROUP, SW_HEAD_DIM)
    k = k_raw.reshape(B, nC, CHUNK, SW_KV_HEADS, SW_HEAD_DIM)
    v = v_raw.reshape(B, nC, CHUNK, SW_KV_HEADS, SW_HEAD_DIM)
    pad = ((0, 0), (W - 1, 0), (0, 0), (0, 0), (0, 0))
    kp, vp = jnp.pad(k, pad), jnp.pad(v, pad)
    kw = jnp.concatenate([kp[:, j:j + nC] for j in range(W)], axis=2)
    vw = jnp.concatenate([vp[:, j:j + nC] for j in range(W)], axis=2)
    s = jnp.einsum('bcqkgd,bclkd->bckgql', q, kw).astype(jnp.float32) * (SW_HEAD_DIM ** -0.5)
    qi = jnp.arange(CHUNK)[:, None]
    lj = jnp.arange(L)[None, :]
    dist = jnp.abs(qi + (W - 1) * CHUNK - lj).astype(jnp.float32)
    slopes = jnp.asarray(_alibi_slopes(SW_HEADS)).reshape(SW_KV_HEADS, SW_GROUP)
    s = s - slopes[:, :, None, None] * dist
    key_chunk = jnp.arange(nC)[:, None] - (W - 1) + jnp.arange(L)[None, :] // CHUNK
    valid = (key_chunk >= 0)[None, :, None, None, None, :]
    s = jnp.where(valid, s, -jnp.inf)
    sink = sinks.astype(jnp.float32).reshape(SW_KV_HEADS, SW_GROUP)[None, None, :, :, None, None]
    m = jnp.maximum(jnp.max(s, axis=-1, keepdims=True), sink)
    p = jnp.exp(s - m)
    probs = p / (jnp.sum(p, axis=-1, keepdims=True) + jnp.exp(sink - m))
    o = jnp.einsum('bckgql,bclkd->bcqkgd', probs.astype(v.dtype), vw)
    return o.reshape(B, S, SW_WIDTH)

def _peer(h, wq, subkeys, u, v):
    B, S, D = h.shape
    T = B * S
    ht = h.reshape(T, D)
    q = (ht @ wq).reshape(T, PEER_HEADS, PEER_DKEY)
    s1 = jnp.einsum('thd,hnd->thn', q[..., :PEER_HALF], subkeys[:, 0])
    s2 = jnp.einsum('thd,hnd->thn', q[..., PEER_HALF:], subkeys[:, 1])
    v1, i1 = lax.top_k(s1, PEER_TOPK)
    v2, i2 = lax.top_k(s2, PEER_TOPK)
    cand = (v1[..., :, None] + v2[..., None, :]).reshape(T, PEER_HEADS, PEER_TOPK * PEER_TOPK)
    sc, ci = lax.top_k(cand, PEER_TOPK)
    e1 = jnp.take_along_axis(i1, ci // PEER_TOPK, axis=-1)
    e2 = jnp.take_along_axis(i2, ci % PEER_TOPK, axis=-1)
    idx = e1 * PEER_NKEYS + e2
    gates = jax.nn.softmax(sc.astype(jnp.float32), axis=-1)
    nblk = T // PEER_BLOCK

    def block(args):
        xb, ib, gb = args
        act = jax.nn.gelu(jnp.einsum('td,thkd->thk', xb, u[ib]).astype(jnp.float32), approximate=False)
        a = (act * gb).astype(xb.dtype)
        return jnp.einsum('thk,thkd->td', a, v[ib])

    y = lax.map(block, (ht.reshape(nblk, PEER_BLOCK, D),
                        idx.reshape(nblk, PEER_BLOCK, PEER_HEADS, PEER_TOPK),
                        gates.reshape(nblk, PEER_BLOCK, PEER_HEADS, PEER_TOPK)))
    return y.reshape(B, S, D)

def setup_inputs(seed: int = 0) -> dict:
    key = jax.random.key(seed)
    ks = jax.random.split(key, 13)
    f32 = jnp.float32
    nrm = lambda k, shp, sc: jax.random.normal(k, shp, f32) * sc
    return {
        "x": nrm(ks[0], (BATCH, SEQ, D_MODEL), 1.0),
        "norm1_g": 1.0 + nrm(ks[1], (DEPTH, D_MODEL), 0.02),
        "w_in": nrm(ks[2], (DEPTH, D_MODEL, IN_COLS), D_MODEL ** -0.5),
        "hg_lb_logits": nrm(ks[3], (DEPTH + 1, HG_HEADS * HG_DK), 1.0),
        "hg_norm_g": 1.0 + nrm(ks[4], (DEPTH, HG_WIDTH), 0.02),
        "sw_sinks": nrm(ks[5], (DEPTH, SW_HEADS), 0.5),
        "w_out": nrm(ks[6], (DEPTH, MIX_WIDTH, D_MODEL), MIX_WIDTH ** -0.5),
        "norm2_g": 1.0 + nrm(ks[7], (DEPTH, D_MODEL), 0.02),
        "peer_wq": nrm(ks[8], (DEPTH, D_MODEL, PEER_HEADS * PEER_DKEY), D_MODEL ** -0.5),
        "peer_subkeys": nrm(ks[9], (DEPTH, PEER_HEADS, 2, PEER_NKEYS, PEER_HALF), PEER_HALF ** -0.5),
        "peer_u": nrm(ks[10], (DEPTH, PEER_NEXP, D_MODEL), D_MODEL ** -0.5),
        "peer_v": nrm(ks[11], (DEPTH, PEER_NEXP, D_MODEL), PEER_HEADS ** -0.5),
        "final_norm_g": 1.0 + nrm(ks[12], (D_MODEL,), 0.02),
    }

def reference(x, norm1_g, w_in, hg_lb_logits, hg_norm_g, sw_sinks, w_out, norm2_g,
              peer_wq, peer_subkeys, peer_u, peer_v, final_norm_g):
    lb_all = jnp.cumsum(jax.nn.softmax(hg_lb_logits.astype(jnp.float32), axis=0), axis=0)
    o = IN_OFFS
    for l in range(DEPTH):
        h = _rmsnorm(x, norm1_g[l])
        proj = h @ w_in[l]
        hg_out = _hgrn2_group(proj[..., o[0]:o[1]], proj[..., o[1]:o[2]],
                              proj[..., o[2]:o[3]], proj[..., o[3]:o[4]],
                              lb_all[l], hg_norm_g[l])
        sw_out = _swa_group(proj[..., o[4]:o[5]], proj[..., o[5]:o[6]],
                            proj[..., o[6]:o[7]], sw_sinks[l])
        mixed = jnp.concatenate([hg_out, sw_out], axis=-1)
        x = x + mixed @ w_out[l]
        x = x + _peer(_rmsnorm(x, norm2_g[l]), peer_wq[l], peer_subkeys[l], peer_u[l], peer_v[l])
    return _rmsnorm(x, final_norm_g)


_drawn_inputs = setup_inputs


def setup_inputs(seed=0):
    import zlib

    import numpy as np

    out = dict(_drawn_inputs(seed))
    spreads = {}
    factors = {'hg_norm_g': 9.397, 'sw_sinks': 24.164, 'final_norm_g': 24.101, 'norm2_g': 11.208}
    for name, (base, spread) in spreads.items():
        noise = np.random.default_rng([zlib.crc32(name.encode()), seed]).standard_normal(out[name].shape)
        drawn = base * np.exp(spread * noise) if base else spread * noise
        out[name] = __import__('jax').numpy.asarray(drawn.astype(out[name].dtype))
    for name, factor in factors.items():
        out[name] = (out[name] * factor).astype(out[name].dtype)
    return out
```

```python
from contextlib import ExitStack

import numpy as np
import concourse.bass as bass
from concourse import mybir

P = 128
F32 = mybir.dt.float32
F32R = mybir.dt.float32r
BF16 = mybir.dt.bfloat16
U32 = mybir.dt.uint32
ALU = mybir.AluOpType
ACT = mybir.ActivationFunctionType
AX_X = mybir.AxisListType.X

D = 1024
SEQ = 1024
DC = D // P
NB = SEQ // P
HG = 4
HW = HG * P
SW_HEADS, SW_KV, HD, CHUNK = 8, 2, 64, 64
GROUP = SW_HEADS // SW_KV
IN_COLS = 4 * HW + SW_HEADS * HD + 2 * SW_KV * HD
WIN = 2 * CHUNK
LEVELS = 7
PH, NKEYS, TOPK = 8, 128, 16
PQ = PH * 2 * P
NHK = PH * TOPK
EPS = 1e-6
LOG_FLOOR = 1e-18
ARG_CAP = 80.0
NEG = -3.0e38
HALF = 64
NG = SEQ // HALF

INPUTS = ["x", "norm1_g", "w_in", "hg_lb_logits", "hg_norm_g", "sw_sinks", "w_out", "norm2_g",
          "peer_wq", "peer_subkeys", "peer_u", "peer_v", "final_norm_g"]


def shape_constants():
    t = np.arange(P)
    ident = np.eye(P, dtype=np.float32)
    upto = (t[:, None] <= t[None, :]).astype(np.float32)
    level = np.zeros((P, LEVELS + 1, P), np.float32)
    for n in range(LEVELS):
        w = P >> (n + 1)
        same = (t[:, None] // (2 * w)) == (t[None, :] // (2 * w))
        level[:, n] = same & ((t[:, None] // w) % 2 == 0) & ((t[None, :] // w) % 2 == 1)
    level[:, LEVELS] = ident
    slopes = 2.0 ** (-8.0 * (np.arange(1, SW_HEADS + 1, dtype=np.float32) / SW_HEADS))
    alibi = np.zeros((P, SW_HEADS, WIN), np.float32)
    q = np.arange(CHUNK)[:, None]
    j = np.arange(WIN)[None, :]
    own_first = np.where(j < CHUNK, np.abs(q - j), q + WIN - j)
    in_order = np.abs(q + CHUNK - j)
    for h in range(SW_HEADS):
        alibi[:CHUNK, h] = -slopes[h] * own_first
        alibi[CHUNK:, h] = -slopes[h] * in_order
    alibi0 = alibi.copy()
    alibi0[:CHUNK, :, CHUNK:] = -1e30
    iota = np.tile(t.astype(np.float32), (P, 1))
    return {"c_ident": ident, "c_upto": upto, "c_level": level, "c_alibi": alibi, "c_alibi0": alibi0,
            "c_iota": iota}


class Steps:

    def __init__(self, eng, sem, per_turn=0, turn=0):
        self.eng, self.sem, self.base, self.n = eng, sem, turn * per_turn, 0

    def mark(self, ins):
        self.n += 1
        ins.then_inc(self.sem, 1)
        return self.n

    def until(self, n):
        self.eng.wait_ge(self.sem, self.base + n)

    def step(self, ins):
        self.until(self.mark(ins))


def row(ap, width):
    return ap.rearrange("(o n) -> o n", o=1).broadcast_to([P, width])


def inverse_root(nc, dve, s, r, x, tmp):
    s.step(nc.vector.tensor_tensor(tmp, r, r, ALU.mult))
    s.step(nc.vector.tensor_tensor(tmp, tmp, x, ALU.mult))
    s.step(nc.vector.tensor_scalar(tmp, tmp, -0.5, 1.5, ALU.mult, ALU.add))
    s.step(nc.vector.tensor_tensor(r, r, tmp, ALU.mult))


def mixer_phase(nc, a, mix_dram):
    with ExitStack() as ctx:
        def sb(name, shape, dt=F32):
            return ctx.enter_context(nc.sbuf_tensor("m_" + name, shape, dt))

        def sem(name):
            return ctx.enter_context(nc.semaphore("m_" + name))

        w_in = sb("w_in", [P, DC, IN_COLS])
        ident = sb("ident", [P, P])
        upto = sb("upto", [P, P])
        level = sb("level", [P, LEVELS + 1, P], BF16)
        alibi = sb("alibi", [P, SW_HEADS, WIN])
        alibi_prev = sb("alibi_prev", [CHUNK, SW_HEADS, CHUNK])
        g1 = sb("g1", [P, D])
        lb2 = sb("lb2", [P, 2, HW])
        hgn = sb("hgn", [P, HW])
        sink = sb("sink", [P, SW_HEADS])
        tiny = sb("tiny", [P, 1])
        xb = sb("xb", [P, D])
        xn = sb("xn", [P, D])
        stat = sb("stat", [P, 4])
        pT = sb("pT", [P, SW_HEADS, P])
        swq = sb("swq", [P, GROUP, SW_KV, HD])
        swk = sb("swk", [P, SW_KV * HD])
        swv = sb("swv", [P, SW_KV * HD])
        swv_mix = sb("swv_mix", [P, SW_KV * HD])
        swqT = sb("swqT", [P, GROUP, P])
        swkT = sb("swkT", [P, P])
        swkT_mix = sb("swkT_mix", [P, P])
        ex = sb("ex", [P, 3, HW])
        sg = sb("sg", [P, 3, HW])
        st_flat = sb("st", [P, SW_HEADS * (WIN + 1)])
        ssum = sb("ssum", [P, 2, SW_HEADS])
        mixS = sb("mixS", [P, HG, P])
        qT = sb("qT", [P, 2, HG, P])
        kT = sb("kT", [P, 2, HG, P])
        bT = sb("bT", [P, 2, HG, P])
        eb = sb("eb", [P, 2, HG, P])
        vv = sb("vv", [P, 2, HW])
        gate = sb("gate", [P, 2, HW])
        dec = sb("dec", [P, 2, LEVELS, P])
        ke = sb("ke", [P, 2, LEVELS, P])
        dlast = sb("dlast", [P, HG, P])
        qb = sb("qb", [P, HG, P])
        kd = sb("kd", [P, HG, P])
        kdT = sb("kdT", [P, HG, P])
        attn = sb("attn", [P, HG, P])
        pick = sb("pick", [P, LEVELS + 1, P])
        oS = sb("oS", [P, HG, P])
        ostat = sb("ostat", [P, 3, HG])
        mixH = sb("mixH", [P, HG, P])
        state = sb("state", [P, HG, P])
        ps = ctx.enter_context(nc.psum_tensor("m_ps", [P, 8, 512], F32))

        st = st_flat[:].rearrange("p (h w) -> p h w", h=SW_HEADS)
        hT = pT
        lmax = vv[:, 0, :]
        qs, kk = ex[:, 0, :], ex[:, 2, :]
        ff = swq[:].rearrange("p i g d -> p (i g d)")

        def bank(n, k=1, heads=None):
            v = ps[:, n:n + k, :].rearrange("p a b -> p (a b)")
            return v if heads is None else v.rearrange("p (h t) -> p h t", h=heads)

        B_SWQ, B_SWKV, B_Q, B_Z, B_GATE, B_I = 2, 3, 0, 1, 3, 2
        B_SWQT, B_SWKT, B_QT, B_KT, B_CUM, B_OT = 2, 1, 0, 3, 0, 1
        B_SW = (2, 1)
        B_PT = (2, 3)
        B_LEVELS, B_O, B_ONT, B_KDT, B_U = 6, 4, 4, 5, 5

        consts, x_in = sem("consts"), sem("x_in")
        mix_out = [sem(f"mix_out{n}") for n in range(2)]
        tab, ready, lexp = sem("tab"), sem("ready"), sem("lexp")
        names = ("ss ms rs xn hT_ps hT old q_ps z_ps gate_ps i_ps swq_ps swkv_ps swq swkv swT kqT mix sc e v ex f logf qkT "
                 "qkTs b bS s p pn pT pTs oT oTs Dl E QK KDT kdT hs at O U oS oms ors on onT mixT s_free h_free passed").split()
        S = {n: sem(n) for n in names}
        act_steps, dve_steps = sem("act_steps"), sem("dve_steps")
        NCONST = 11

        block = ctx.enter_context(nc.Block())

        def turns(turn, eng):
            with eng.Fori(0, NB // 2 - 1) as i:
                for k in range(2):
                    turn(i * 2 + k, k)
            turn(NB - 2, 0)
            turn(NB - 1, 1, last=True)

        @block.sync
        def _(sp):
            x_h = a["x"][0].rearrange("(b p) d -> b p d", p=P)
            sp.dma_start(xb[:], x_h[0]).then_inc(x_in, 16)
            sp.dma_start(ident[:], a["c_ident"]).then_inc(consts, 16)
            sp.dma_start(g1[:], row(a["norm1_g"][0], D)).then_inc(consts, 16)
            for k in range(2):
                sp.dma_start(lb2[:, k, :], row(a["hg_lb_logits"][k], HW)).then_inc(consts, 16)
            sp.dma_start(hgn[:], row(a["hg_norm_g"][0], HW)).then_inc(consts, 16)
            sp.dma_start(sink[:], row(a["sw_sinks"][0], SW_HEADS)).then_inc(consts, 16)
            sp.dma_start(w_in[:], a["w_in"][0].rearrange("(c p) n -> p c n", p=P)).then_inc(consts, 16)
            sp.dma_start(upto[:], a["c_upto"]).then_inc(consts, 16)
            sp.dma_start(pick[:], a["c_level"]).then_inc(consts, 16)
            sp.dma_start(alibi[:], a["c_alibi0"]).then_inc(consts, 16)
            sp.dma_start(alibi_prev[:], a["c_alibi"][0:CHUNK, :, CHUNK:WIN]).then_inc(consts, 16)
            sp.sem_inc(S["s_free"], 1)
            sp.sem_inc(S["h_free"], 1)

            def store_window(n):
                sp.wait_ge(S["oTs"], n + 1)
                sp.dma_start(mix_dram[n, :, HG:, :], mixS[:]).then_inc(mix_out[0], 16)
                sp.wait_ge(mix_out[0], n * 16 + 16)
                sp.sem_inc(S["s_free"], 1)

            def turn(b, k, last=False):
                if not last:
                    sp.wait_ge(S["xn"], b + 1)
                    sp.dma_start(xb[:], x_h[b + 1]).then_inc(x_in, 16)
                    store_window(b + 1)
                sp.wait_ge(S["mixT"], b + 1)
                sp.dma_start(mix_dram[b, :, :HG, :], mixH[:]).then_inc(mix_out[1], 16)
                sp.wait_ge(mix_out[1], b * 16 + 16)
                sp.sem_inc(S["h_free"], 1)

            store_window(0)
            turns(turn, sp)

        @block.vector
        def _(dve):
            s = Steps(dve, dve_steps)
            s.step(nc.vector.memset(tiny[:], LOG_FLOOR))
            nc.vector.memset(state[:], 0.0)
            nc.vector.memset(swv[:], 0.0)
            s.step(nc.vector.memset(swkT[:], 0.0))
            dve.wait_ge(consts, 16 * NCONST)
            s.step(nc.vector.tensor_copy(level[:], pick[:]))
            s.step(nc.vector.tensor_tensor(lmax, lb2[:, 0, :], lb2[:, 1, :], ALU.max))
            s.step(nc.vector.tensor_tensor(lb2[:], lb2[:], lmax.unsqueeze(1).broadcast_to([P, 2, HW]), ALU.subtract))
            dve.sem_inc(tab, 1)
            dve.wait_ge(lexp, 1)
            s.step(nc.vector.tensor_tensor(lmax, lb2[:, 0, :], lb2[:, 1, :], ALU.add))
            s.step(nc.vector.reciprocal(lmax, lmax))
            s.step(nc.vector.tensor_tensor(lb2[:], lb2[:], lmax.unsqueeze(1).broadcast_to([P, 2, HW]), ALU.mult))
            lb, omlb = lb2[:, 0, :], lb2[:, 1, :]
            dve.sem_inc(ready, 1)

            def norm(s, n):
                dve.wait_ge(S["ss"], n + 1)
                s.step(nc.vector.tensor_scalar(stat[:, 1:2], stat[:, 0:1], 1.0 / D, EPS, ALU.mult, ALU.add))
                dve.sem_inc(S["ms"], 1)
                dve.wait_ge(S["rs"], n + 1)
                inverse_root(nc, dve, s, stat[:, 2:3], stat[:, 1:2], stat[:, 3:4])
                nc.vector.scalar_tensor_tensor(xn[:], xb[:], stat[:, 2:3], g1[:], ALU.mult, ALU.mult).then_inc(S["xn"], 1)
                s.step(nc.vector.tensor_copy(swv_mix[CHUNK:, :], swv[CHUNK:, :]))
                s.step(nc.vector.tensor_copy(swkT_mix[:, CHUNK:], swkT[:, CHUNK:]))
                dve.sem_inc(S["old"], 1)

            def cap_q(n):
                dve.wait_ge(S["q_ps"], n + 1)
                nc.vector.tensor_scalar(ex[:, 0, :], bank(B_Q), -ARG_CAP, -1.0, ALU.max, ALU.mult)

            def cap_rest(n):
                dve.wait_ge(S["z_ps"], n + 1)
                nc.vector.tensor_scalar(ex[:, 1, :], bank(B_Z), ARG_CAP, None, ALU.min)
                dve.wait_ge(S["gate_ps"], n + 1)
                nc.vector.tensor_scalar(ex[:, 2, :], bank(B_GATE), -ARG_CAP, -1.0, ALU.max, ALU.mult).then_inc(S["e"], 1)

            def own_keys(s, n):
                dve.wait_ge(S["kqT"], n + 1)
                s.step(nc.vector.tensor_copy(swv_mix[:CHUNK, :], swv[:CHUNK, :]))
                s.step(nc.vector.tensor_copy(swkT_mix[:, :CHUNK], swkT[:, :CHUNK]))
                dve.sem_inc(S["mix"], 1)

            def sigmoids(s, n, m):
                dve.wait_ge(S["ex"], n + 1)
                s.step(nc.vector.tensor_scalar(sg[:], ex[:], 1.0, None, ALU.add))
                s.step(nc.vector.reciprocal(sg[:], sg[:]))
                s.step(nc.vector.tensor_tensor(kk, sg[:, 1, :], omlb, ALU.mult))
                nc.vector.tensor_tensor(qs, bank(B_Q), sg[:, 0, :], ALU.mult)
                s.step(nc.vector.tensor_tensor(ff, ex[:, 1, :], kk, ALU.mult))
                nc.vector.tensor_tensor(gate[:, m], bank(B_GATE), sg[:, 2, :], ALU.mult)
                s.step(nc.vector.tensor_tensor(ff, ff, lb, ALU.add))
                dve.sem_inc(S["f"], 1)
                s.step(nc.vector.tensor_tensor(gate[:, m], gate[:, m], hgn[:], ALU.mult))

            def window_scores(s, n):
                nc.vector.tensor_copy(st[:, :, WIN:WIN + 1], sink[:].unsqueeze(2))
                dve.wait_ge(S["sc"], n + 1)
                for g in range(SW_KV):
                    hs = slice(g * GROUP, (g + 1) * GROUP)
                    s.step(nc.vector.scalar_tensor_tensor(st[:, hs, 0:WIN], bank(B_SW[g], 1, GROUP), HD ** -0.5,
                                                          alibi[:, hs, :], ALU.mult, ALU.add))
                s.step(nc.vector.tensor_copy(alibi[:CHUNK, :, CHUNK:], alibi_prev[:]))
                s.step(nc.vector.reduce_max(ssum[:, 0, :], st, AX_X))
                s.step(nc.vector.tensor_tensor(st, st, ssum[:, 0, :].unsqueeze(2).broadcast_to([P, SW_HEADS, WIN + 1]),
                                               ALU.subtract))
                dve.sem_inc(S["s"], 1)

            def window_probs(s, n):
                dve.wait_ge(S["p"], n + 1)
                s.step(nc.vector.reduce_sum(ssum[:, 0, :], st, AX_X))
                s.step(nc.vector.reciprocal(ssum[:, 1, :], ssum[:, 0, :]))
                s.step(nc.vector.tensor_tensor(st, st, ssum[:, 1, :].unsqueeze(2).broadcast_to([P, SW_HEADS, WIN + 1]),
                                               ALU.mult))
                dve.sem_inc(S["pn"], 1)

            def log_decays(s, b, k, h):
                if h >= 2:
                    dve.wait_ge(S["hs"], b * HG + h - 1)
                if h == 0:
                    dve.wait_ge(S["bS"], b + 1)
                    nc.vector.tensor_tensor(dlast[:], bT[:, k, :, P - 1:P].broadcast_to([P, HG, P]), bT[:, k], ALU.subtract)
                for n in range(LEVELS):
                    w = P >> (n + 1)
                    bv = bT[:, k, h, :].rearrange("p (m w) -> p m w", w=2 * w)
                    dv = dec[:, h % 2, n].rearrange("p (m w) -> p m w", w=2 * w)
                    ref = bv[:, :, w - 1:w].broadcast_to([P, P // (2 * w), w])
                    nc.vector.tensor_tensor(dv[:, :, w:], bv[:, :, w:], ref, ALU.subtract)
                    done = nc.vector.tensor_tensor(dv[:, :, :w], ref, bv[:, :, :w], ALU.subtract)
                done.then_inc(S["Dl"], 1)

            def decayed(s, b, k, h):
                dve.wait_ge(S["E"], b * HG + h + 1)
                if h == 0:
                    nc.vector.tensor_tensor(qb[:], qT[:, k], eb[:, k], ALU.mult)
                    nc.vector.tensor_tensor(kd[:], kT[:, k], dlast[:], ALU.mult)
                d = dec[:, h % 2]
                s.step(nc.vector.tensor_tensor(ke[:, h % 2], d, kT[:, k, h, :].unsqueeze(1).broadcast_to([P, LEVELS, P]), ALU.mult))
                nc.vector.tensor_tensor(d, d, qT[:, k, h, :].unsqueeze(1).broadcast_to([P, LEVELS, P]),
                                        ALU.mult).then_inc(S["QK"], 1)

            def weights(s, b, h):
                dve.wait_ge(S["hs"], b * HG + h + 1)
                s.step(nc.vector.tensor_tensor(pick[:], bank(B_LEVELS, 2, LEVELS + 1), level[:], ALU.mult))
                nc.vector.reduce_sum(attn[:, h, :], pick[:].rearrange("p l t -> p t l"), AX_X).then_inc(S["at"], 1)

            def outputs(s, b, k):
                dve.wait_ge(S["U"], b + 1)
                for h in range(HG):
                    done = nc.vector.scalar_tensor_tensor(state[:, h, :], state[:, h, :], eb[:, k, h, P - 1:P],
                                                          bank(B_U, 1, HG)[:, h, :], ALU.mult, ALU.add)
                s.step(done)
                dve.wait_ge(S["oS"], b + 1)
                sq = pick[:, 0:HG, :]
                s.step(nc.vector.tensor_tensor(sq, oS[:], oS[:], ALU.mult))
                s.step(nc.vector.reduce_sum(ostat[:, 0, :], sq, AX_X))
                s.step(nc.vector.tensor_scalar(ostat[:, 0, :], ostat[:, 0, :], 1.0 / P, EPS, ALU.mult, ALU.add))
                dve.sem_inc(S["oms"], 1)
                s.step(nc.vector.tensor_tensor(oS[:], oS[:], gate[:, k].rearrange("p (h t) -> p h t", h=HG), ALU.mult))
                dve.wait_ge(S["ors"], b + 1)
                inverse_root(nc, dve, s, ostat[:, 1, :], ostat[:, 0, :], ostat[:, 2, :])
                s.step(nc.vector.tensor_tensor(oS[:], oS[:], ostat[:, 1, :].unsqueeze(2).broadcast_to([P, HG, P]), ALU.mult))
                dve.sem_inc(S["on"], 1)

            def turn(b, k, one=True, two=True, last=False):
                n, m, one = b + 1, 1 - k, one and not last
                dve.sem_clear(dve_steps)
                s = Steps(dve, dve_steps)
                if two:
                    log_decays(s, b, k, 0)
                if one:
                    norm(s, n)
                if two:
                    decayed(s, b, k, 0)
                    log_decays(s, b, k, 1)
                    decayed(s, b, k, 1)
                    weights(s, b, 0)
                    log_decays(s, b, k, 2)
                if one:
                    cap_q(n)
                if two:
                    decayed(s, b, k, 2)
                    weights(s, b, 1)
                    log_decays(s, b, k, 3)
                if one:
                    cap_rest(n)
                if two:
                    decayed(s, b, k, 3)
                if one:
                    own_keys(s, n)
                if two:
                    weights(s, b, 2)
                if one:
                    sigmoids(s, n, m)
                    window_scores(s, n)
                if two:
                    weights(s, b, 3)
                if one:
                    window_probs(s, n)
                if two:
                    outputs(s, b, k)

            turn(-1, 1, two=False)
            turns(turn, dve)

        @block.scalar
        def _(act):
            act.wait_ge(tab, 1)
            nc.scalar.activation(lb2[:], lb2[:], ACT.Exp).then_inc(lexp, 1)
            act.wait_ge(ready, 1)

            def decays(s, b, h):
                act.wait_ge(S["Dl"], b * HG + h + 1)
                if h == 0:
                    s.step(nc.scalar.activation(dlast[:], dlast[:], ACT.Exp))
                nc.scalar.activation(dec[:, h % 2], dec[:, h % 2], ACT.Exp).then_inc(S["E"], 1)

            def turn(b, k, one=True, two=True, last=False):
                n, m, one = b + 1, 1 - k, one and not last
                act.sem_clear(act_steps)
                s = Steps(act, act_steps)
                if one:
                    act.wait_ge(x_in, n * 16 + 16)
                    nc.scalar.activation(xn[:], xb[:], ACT.Square, accum_out=stat[:, 0:1]).then_inc(S["ss"], 1)
                if two:
                    decays(s, b, 0)
                if one:
                    act.wait_ge(S["ms"], n + 1)
                    s.step(nc.scalar.activation(stat[:, 2:3], stat[:, 1:2], ACT.Ln))
                    nc.scalar.activation(stat[:, 2:3], stat[:, 2:3], ACT.Exp, scale=-0.5).then_inc(S["rs"], 1)
                    act.wait_ge(S["hT_ps"], n + 1)
                    for c in range(2):
                        done = nc.scalar.copy(hT[:, 4 * c:4 * c + 4, :], bank(c, 1, 4))
                    done.then_inc(S["hT"], 1)
                if two:
                    decays(s, b, 1)
                if one:
                    act.wait_ge(S["swq_ps"], n + 1)
                    nc.scalar.copy(swq[:].rearrange("p i g d -> p g i d"),
                                   bank(B_SWQ).rearrange("p (g i d) -> p g i d", g=SW_KV, i=GROUP)).then_inc(S["swq"], 1)
                    act.wait_ge(S["swkv_ps"], n + 1)
                    act.wait_ge(S["old"], n + 1)
                    nc.scalar.copy(swk[:], bank(B_SWKV)[:, 0:SW_KV * HD])
                    nc.scalar.copy(swv[:], bank(B_SWKV)[:, SW_KV * HD:2 * SW_KV * HD]).then_inc(S["swkv"], 1)
                if two:
                    act.wait_ge(S["KDT"], b + 1)
                    nc.scalar.copy(kdT[:], bank(B_KDT, 1, HG)).then_inc(S["kdT"], 1)
                    decays(s, b, 2)
                    decays(s, b, 3)
                if one:
                    act.wait_ge(S["e"], n + 1)
                    nc.scalar.activation(ex[:], ex[:], ACT.Exp).then_inc(S["ex"], 1)
                    act.wait_ge(S["i_ps"], n + 1)
                    nc.scalar.copy(vv[:, m], bank(B_I)).then_inc(S["v"], 1)
                    act.wait_ge(S["swT"], n + 1)
                    nc.scalar.copy(swqT[:], bank(B_SWQT, 1, GROUP))
                    nc.scalar.copy(swkT[:], bank(B_SWKT)[:, 0:P]).then_inc(S["kqT"], 1)
                    act.wait_ge(S["f"], n + 1)
                    nc.scalar.activation(ff, ff, ACT.Ln, bias=tiny[:]).then_inc(S["logf"], 1)
                    act.wait_ge(S["qkT"], n + 1)
                    nc.scalar.copy(qT[:, m], bank(B_QT, 1, HG))
                    nc.scalar.copy(kT[:, m], bank(B_KT, 1, HG)).then_inc(S["qkTs"], 1)
                    act.wait_ge(S["s"], n + 1)
                    nc.scalar.activation(st, st, ACT.Exp).then_inc(S["p"], 1)
                    act.wait_ge(S["b"], n + 1)
                    nc.scalar.copy(bT[:, m], bank(B_CUM, 1, HG))
                    nc.scalar.activation(eb[:, m], bank(B_CUM, 1, HG), ACT.Exp).then_inc(S["bS"], 1)
                    act.wait_ge(S["pT"], n + 1)
                    for c in range(2):
                        done = nc.scalar.copy(pT[:, 4 * c:4 * c + 4, :], bank(B_PT[c], 1, 4))
                    done.then_inc(S["pTs"], 1)
                if two:
                    act.wait_ge(S["O"], b + 1)
                    nc.scalar.copy(oS[:], bank(B_O, 1, HG)).then_inc(S["oS"], 1)
                if one:
                    act.wait_ge(S["s_free"], n + 1)
                    act.wait_ge(S["oT"], n + 1)
                    nc.scalar.copy(mixS[:], bank(B_OT, 1, 4)).then_inc(S["oTs"], 1)
                if two:
                    act.wait_ge(S["oms"], b + 1)
                    s.step(nc.scalar.activation(ostat[:, 1, :], ostat[:, 0, :], ACT.Ln))
                    nc.scalar.activation(ostat[:, 1, :], ostat[:, 1, :], ACT.Exp, scale=-0.5).then_inc(S["ors"], 1)
                    act.wait_ge(S["h_free"], b + 1)
                    act.wait_ge(S["onT"], b + 1)
                    nc.scalar.copy(mixH[:], bank(B_ONT, 1, 4)).then_inc(S["mixT"], 1)

            turn(-1, 1, two=False)
            turns(turn, act)

        @block.tensor
        def _(pe):
            mm, tr = nc.tensor.matmul, nc.tensor.transpose
            pe.wait_ge(consts, 16 * NCONST)

            def project(n, to, at, width, done_sem):
                for c in range(DC):
                    done = mm(bank(to)[:, 0:width], hT[:, c, :], w_in[:, c, at:at + width],
                              start=(c == 0), stop=(c == DC - 1))
                done.then_inc(S[done_sem], 1)

            def level_scores(b, k, h):
                pe.wait_ge(S["QK"], b * HG + h + 1)
                if h == 0:
                    for j in range(HG):
                        done = tr(bank(B_KDT, 1, HG)[:, j, :], kd[:, j, :], ident[:])
                    done.then_inc(S["KDT"], 1)
                else:
                    pe.wait_ge(S["at"], b * HG + h)
                sc = bank(B_LEVELS, 2, LEVELS + 1)
                for n in range(LEVELS):
                    mm(sc[:, n, :], ke[:, h % 2, n, :], dec[:, h % 2, n, :], start=True, stop=True)
                mm(sc[:, LEVELS, :], kT[:, k, h, :], qT[:, k, h, :], start=True, stop=True).then_inc(S["hs"], 1)

            def turn(b, k, one=True, two=True, last=False):
                n, m, one = b + 1, 1 - k, one and not last
                if one:
                    pe.wait_ge(S["xn"], n + 1)
                    for c in range(DC):
                        done = tr(bank(c // 4, 1, 4)[:, c % 4, :], xn[:, c * P:(c + 1) * P], ident[:])
                    done.then_inc(S["hT_ps"], 1)
                    pe.wait_ge(S["hT"], n + 1)
                    project(n, B_SWQ, 4 * HW, SW_HEADS * HD, "swq_ps")
                    project(n, B_SWKV, 4 * HW + SW_HEADS * HD, 2 * SW_KV * HD, "swkv_ps")
                    project(n, B_Q, 0, HW, "q_ps")
                if two:
                    level_scores(b, k, 0)
                if one:
                    project(n, B_Z, HW, HW, "z_ps")
                if two:
                    level_scores(b, k, 1)
                if one:
                    pe.wait_ge(S["swkv"], n + 1)
                    project(n, B_GATE, 3 * HW, HW, "gate_ps")
                    pe.wait_ge(S["swq"], n + 1)
                    project(n, B_I, 2 * HW, HW, "i_ps")
                    pe.wait_ge(S["v"], n + 1)
                    for i in range(GROUP):
                        tr(bank(B_SWQT, 1, GROUP)[:, i, :], swq[:, i].rearrange("p g d -> p (g d)"), ident[:])
                    pe.wait_ge(S["e"], n + 1)
                    tr(bank(B_SWKT)[:, 0:P], swk[:], ident[:]).then_inc(S["swT"], 1)
                if two:
                    level_scores(b, k, 2)
                if one:
                    pe.wait_ge(S["kqT"], n + 1)
                    pe.wait_ge(S["mix"], n + 1)
                    pe.sem_inc(S["passed"], 1)
                    for c in range(2):
                        keys = swkT_mix if c == 0 else swkT
                        for i in range(GROUP):
                            for g in range(SW_KV):
                                done = mm(ps[c * CHUNK:(c + 1) * CHUNK, B_SW[g], i * WIN:(i + 1) * WIN],
                                          swqT[g * HD:(g + 1) * HD, i, c * CHUNK:(c + 1) * CHUNK],
                                          keys[g * HD:(g + 1) * HD, :], start=True, stop=True)
                    done.then_inc(S["sc"], 1)
                    pe.wait_ge(S["f"], n + 1)
                    for h in range(HG):
                        tr(bank(B_QT, 1, HG)[:, h, :], qs[:, h * P:(h + 1) * P], ident[:])
                    for h in range(HG):
                        done = tr(bank(B_KT, 1, HG)[:, h, :], kk[:, h * P:(h + 1) * P], ident[:])
                    done.then_inc(S["qkT"], 1)
                    pe.wait_ge(S["logf"], n + 1)
                    pe.wait_ge(S["qkTs"], n + 1)
                    for h in range(HG):
                        done = mm(bank(B_CUM, 1, HG)[:, h, :], ff[:, h * P:(h + 1) * P], upto[:], start=True, stop=True)
                    done.then_inc(S["b"], 1)
                if two:
                    level_scores(b, k, 3)
                if one:
                    pe.wait_ge(S["pn"], n + 1)
                    for h in range(SW_HEADS):
                        done = tr(bank(B_PT[h // 4], 1, 4)[:, h % 4, :], st[:, h, 0:WIN], ident[:])
                    done.then_inc(S["pT"], 1)
                if two:
                    pe.wait_ge(S["kdT"], b + 1)
                    o = bank(B_O, 1, HG)
                    for h in range(HG):
                        pe.wait_ge(S["at"], b * HG + h + 1)
                        mm(o[:, h, :], attn[:, h, :], vv[:, k, h * P:(h + 1) * P], start=True, stop=False)
                        done = mm(o[:, h, :], qb[:, h, :], state[:, h, :], start=False, stop=True)
                    done.then_inc(S["O"], 1)
                    for h in range(HG):
                        done = mm(bank(B_U, 1, HG)[:, h, :], kdT[:, h, :], vv[:, k, h * P:(h + 1) * P], start=True, stop=True)
                    done.then_inc(S["U"], 1)
                if one:
                    pe.wait_ge(S["pTs"], n + 1)
                    for h in range(SW_HEADS):
                        g, half = h // GROUP, (h % 2) * HD
                        for c in range(2):
                            vals = swv_mix if c == 0 else swv
                            done = mm(ps[half:half + HD, B_OT, (h // 2) * P + c * CHUNK:(h // 2) * P + (c + 1) * CHUNK],
                                      vals[:, g * HD:(g + 1) * HD], pT[:, h, c * CHUNK:(c + 1) * CHUNK],
                                      start=True, stop=True)
                    done.then_inc(S["oT"], 1)
                if two:
                    pe.wait_ge(S["on"], b + 1)
                    for h in range(HG):
                        done = tr(bank(B_ONT, 1, HG)[:, h, :], oS[:, h, :], ident[:])
                    done.then_inc(S["onT"], 1)

            turn(-1, 1, two=False)
            turns(turn, pe)


def output_phase(nc, a, mix_dram, x1_dram, wq, wq_in):
    with ExitStack() as ctx:
        def sb(name, shape, dt=F32):
            return ctx.enter_context(nc.sbuf_tensor("o_" + name, shape, dt))

        def sem(name):
            return ctx.enter_context(nc.semaphore("o_" + name))

        w_raw = sb("w_raw", [P, DC, D])
        w_hi = sb("w_hi", [P, DC, D], F32R)
        w_lo = sb("w_lo", [P, DC, D], F32R)
        xb = sb("xb", [P, 2, D])
        mixT = sb("mixT", [P, 2, D])
        m_hi = sb("m_hi", [P, 2, D], F32R)
        m_lo = sb("m_lo", [P, 2, D], F32R)
        ps = ctx.enter_context(nc.psum_tensor("o_ps", [P, 2, 2, 512], F32))
        w_in, m_in, x_in, x1_out = sem("w_in"), *([sem(f"{n}{k}") for k in range(2)] for n in ("m_in", "x_in", "x1_out"))
        S = {n: sem(n) for n in "w_hi w_lo m_hi m_lo out x1 stored".split()}
        block = ctx.enter_context(nc.Block())

        @block.sync
        def _(sp):
            x_h = a["x"][0].rearrange("(b p) d -> b p d", p=P)

            def load(b, k):
                sp.dma_start(mixT[:, k, :], mix_dram[b].rearrange("p c t -> p (c t)")).then_inc(m_in[k], 16)
                sp.dma_start(xb[:, k, :], x_h[b]).then_inc(x_in[k], 16)

            sp.dma_start(w_raw[:], a["w_out"][0].rearrange("(c p) n -> p c n", p=P)).then_inc(w_in, 16)
            load(0, 0)
            load(1, 1)
            sp.dma_start(wq[:], a["peer_wq"][0].rearrange("(c p) n -> p c n", p=P)).then_inc(wq_in, 16)

            def turn(i, k, last=False):
                b = i * 2 + k
                sp.wait_ge(S["x1"], b + 1)
                sp.dma_start(x1_dram[b], xb[:, k, :]).then_inc(x1_out[k], 16)
                sp.wait_ge(x1_out[k], i * 16 + 16)
                sp.sem_inc(S["stored"], 1)
                if not last:
                    load(b + 2, k)

            with sp.Fori(0, NB // 2 - 1) as i:
                for k in range(2):
                    turn(i, k)
            for k in range(2):
                turn(NB // 2 - 1, k, last=True)

        @block.scalar
        def _(act):
            act.wait_ge(w_in, 16)
            for c in range(DC):
                nc.scalar.copy(w_hi[:, c, :], w_raw[:, c, :]).then_inc(S["w_hi"], 1)
            act.sem_inc(S["out"], 2)
            with act.Fori(0, NB // 2) as i:
                for k in range(2):
                    b = i * 2 + k
                    act.wait_ge(m_in[k], i * 16 + 16)
                    act.wait_ge(S["out"], b + 1)
                    nc.scalar.copy(m_hi[:, k, :], mixT[:, k, :]).then_inc(S["m_hi"], 1)

        @block.vector
        def _(dve):
            for c in range(DC):
                dve.wait_ge(S["w_hi"], c + 1)
                nc.vector.tensor_tensor(w_lo[:, c, :], w_raw[:, c, :], w_hi[:, c, :].bitcast(F32), ALU.subtract).then_inc(S["w_lo"], 1)

            def split(b, k):
                dve.wait_ge(S["m_hi"], b + 1)
                nc.vector.tensor_tensor(m_lo[:, k, :], mixT[:, k, :], m_hi[:, k, :].bitcast(F32), ALU.subtract).then_inc(S["m_lo"], 1)

            def add(i, k):
                dve.wait_ge(x_in[k], i * 16 + 16)
                dve.wait_ge(S["out"], i * 2 + k + 3)
                nc.vector.tensor_tensor(xb[:, k, :], xb[:, k, :], ps[:, k].rearrange("p a b -> p (a b)"),
                                        ALU.add).then_inc(S["x1"], 1)

            split(0, 0)
            with dve.Fori(0, NB // 2 - 1) as i:
                for k in range(2):
                    split(i * 2 + k + 1, 1 - k)
                    add(i, k)
            split(NB - 1, 1)
            add(NB // 2 - 1, 0)
            add(NB // 2 - 1, 1)

        @block.tensor
        def _(pe):
            pe.wait_ge(S["w_lo"], DC)

            def turn(b, k, first=False):
                pe.wait_ge(S["m_lo"], b + 1)
                if not first:
                    pe.wait_ge(S["x1"], b - 1)
                for half in range(2):
                    for c in range(DC):
                        for m, (mv, wv) in enumerate(((m_hi, w_hi), (m_hi, w_lo), (m_lo, w_hi))):
                            done = nc.tensor.matmul(ps[:, k, half, :], mv[:, k, c * P:(c + 1) * P],
                                                    wv[:, c, half * 512:(half + 1) * 512],
                                                    start=(c == 0 and m == 0), stop=(c == DC - 1 and m == 2))
                done.then_inc(S["out"], 1)

            turn(0, 0, first=True)
            turn(1, 1, first=True)
            with pe.Fori(1, NB // 2) as i:
                for k in range(2):
                    turn(i * 2 + k, k)


def score_phase(nc, a, x1_dram, s_dram, wq, wq_in, h_hi, h_lo):
    with ExitStack() as ctx:
        def sb(name, shape, dt=F32):
            return ctx.enter_context(nc.sbuf_tensor("s_" + name, shape, dt))

        def sem(name):
            return ctx.enter_context(nc.semaphore("s_" + name))

        skT = sb("skT", [P, 2 * PH, NKEYS])
        ident = sb("ident", [P, P])
        g2 = sb("g2", [P, D])
        xb = sb("xb", [P, D])
        xn = sb("xn", [P, D])
        squares = sb("squares", [P, D])
        stat = sb("stat", [P, 4])
        hT = sb("hT", [P, DC, P])
        qq = sb("qq", [P, 2, D])
        qT = sb("qT", [P, 2, D])
        ss = sb("ss", [P, 2, D])
        ps = ctx.enter_context(nc.psum_tensor("s_ps", [P, 8, 512], F32))
        subkeys = qq[:].rearrange("p j d -> p (j d)").rearrange("p (k d) -> p k d", d=P)

        def bank(n, k=1, parts=None):
            v = ps[:, n:n + k, :].rearrange("p a b -> p (a b)")
            return v if parts is None else v.rearrange("p (h t) -> p h t", h=parts)

        Q_BANKS, H_BANKS, QT_BANKS = (0, 2), 4, 6
        names = "ss ms rs xn hT_ps hT h_hi h_lo q_ps q_sb qT_ps qT_sb s_ps s_sb skT_ps skT".split()
        S = {n: sem(n) for n in names}
        consts, x1_in, s_out = sem("consts"), sem("x1_in"), sem("s_out")
        act_steps, dve_steps = sem("act_steps"), sem("dve_steps")
        NC = 3
        block = ctx.enter_context(nc.Block())

        def turns(turn, eng):
            with eng.Fori(0, NB - 1) as b:
                turn(b)
            turn(NB - 1, last=True)

        @block.sync
        def _(sp):
            sp.dma_start(xb[:], x1_dram[0]).then_inc(x1_in, 16)
            sp.dma_start(ident[:], a["c_ident"]).then_inc(consts, 16)
            sp.dma_start(subkeys, a["peer_subkeys"][0].rearrange("h c n d -> n (h c) d")).then_inc(consts, 16)
            sp.dma_start(g2[:], row(a["norm2_g"][0], D)).then_inc(consts, 16)
            sp.wait_ge(S["xn"], 1)
            sp.dma_start(xb[:], x1_dram[1]).then_inc(x1_in, 16)

            def store(b):
                sp.wait_ge(S["s_sb"], b * 2 + 4)
                sp.dma_start(s_dram[b], ss[:]).then_inc(s_out, 16)

            with sp.Fori(0, NB - 2) as b:
                sp.wait_ge(S["xn"], b + 2)
                sp.dma_start(xb[:], x1_dram[b + 2]).then_inc(x1_in, 16)
                store(b)
            store(NB - 2)
            store(NB - 1)
            sp.wait_ge(s_out, NB * 16 + 1)

        @block.vector
        def _(dve):
            dve.wait_ge(consts, 16 * NC)

            def norm(b):
                s = Steps(dve, dve_steps)
                dve.wait_ge(S["ss"], b + 1)
                s.step(nc.vector.tensor_scalar(stat[:, 1:2], stat[:, 0:1], 1.0 / D, EPS, ALU.mult, ALU.add))
                dve.sem_inc(S["ms"], 1)
                dve.wait_ge(S["rs"], b + 1)
                inverse_root(nc, dve, s, stat[:, 2:3], stat[:, 1:2], stat[:, 3:4])
                nc.vector.scalar_tensor_tensor(xn[:], xb[:], stat[:, 2:3], g2[:], ALU.mult, ALU.mult).then_inc(S["xn"], 1)

            def split(b):
                dve.wait_ge(S["h_hi"], b + 1)
                at = bass.ds(b * P, P)
                nc.vector.tensor_tensor(h_lo[:, :, at], bank(H_BANKS, 2, DC), h_hi[:, :, at].bitcast(F32),
                                        ALU.subtract).then_inc(S["h_lo"], 1)

            norm(0)
            split(0)
            with dve.Fori(0, NB - 1) as b:
                dve.sem_clear(dve_steps)
                norm(b + 1)
                split(b + 1)

        @block.scalar
        def _(act):
            act.sem_inc(s_out, 1)
            act.wait_ge(S["skT_ps"], 1)
            for c in range(4):
                done = nc.scalar.copy(skT[:, 4 * c:4 * c + 4, :], bank(c, 1, 4))
            done.then_inc(S["skT"], 1)
            act.sem_inc(S["s_sb"], 2)

            def norm(b):
                s = Steps(act, act_steps)
                act.wait_ge(x1_in, b * 16 + 16)
                nc.scalar.activation(squares[:], xb[:], ACT.Square, accum_out=stat[:, 0:1]).then_inc(S["ss"], 1)
                act.wait_ge(S["ms"], b + 1)
                s.step(nc.scalar.activation(stat[:, 2:3], stat[:, 1:2], ACT.Ln))
                nc.scalar.activation(stat[:, 2:3], stat[:, 2:3], ACT.Exp, scale=-0.5).then_inc(S["rs"], 1)

            def features(b):
                act.wait_ge(S["hT_ps"], b + 1)
                nc.scalar.copy(hT[:], bank(H_BANKS, 2, DC)).then_inc(S["hT"], 1)
                nc.scalar.copy(h_hi[:, :, bass.ds(b * P, P)], bank(H_BANKS, 2, DC)).then_inc(S["h_hi"], 1)

            def q_features(b, j):
                act.wait_ge(S["qT_ps"], b * 2 + j + 1)
                nc.scalar.copy(qT[:, j, :], bank(QT_BANKS, 2)).then_inc(S["qT_sb"], 1)

            def scores(b, j):
                act.wait_ge(S["s_ps"], b * 2 + j + 1)
                nc.scalar.copy(ss[:, j, :], bank(Q_BANKS[j], 2)).then_inc(S["s_sb"], 1)

            def turn(b, last=False):
                if not last:
                    act.sem_clear(act_steps)
                    norm(b + 1)
                for j in range(2):
                    act.wait_ge(S["q_ps"], b * 2 + j + 1)
                    nc.scalar.copy(qq[:, j, :], bank(Q_BANKS[j], 2)).then_inc(S["q_sb"], 1)
                q_features(b, 0)
                if not last:
                    features(b + 1)
                act.wait_ge(s_out, b * 16 + 1)
                scores(b, 0)
                q_features(b, 1)
                scores(b, 1)

            norm(0)
            features(0)
            turns(turn, act)

        @block.tensor
        def _(pe):
            mm, tr = nc.tensor.matmul, nc.tensor.transpose
            pe.wait_ge(consts, 16 * NC)
            for c in range(2 * PH):
                done = tr(bank(c // 4, 1, 4)[:, c % 4, :], subkeys[:, c, :], ident[:])
            done.then_inc(S["skT_ps"], 1)

            def features(b):
                pe.wait_ge(S["xn"], b + 1)
                for c in range(DC):
                    done = tr(bank(H_BANKS, 2, DC)[:, c, :], xn[:, c * P:(c + 1) * P], ident[:])
                done.then_inc(S["hT_ps"], 1)

            def q_features(b, j):
                pe.wait_ge(S["q_sb"], b * 2 + j + 1)
                for c in range(DC):
                    done = tr(bank(QT_BANKS, 2, DC)[:, c, :], qq[:, j, c * P:(c + 1) * P], ident[:])
                done.then_inc(S["qT_ps"], 1)

            def scores(b, j):
                pe.wait_ge(S["qT_sb"], b * 2 + j + 1)
                for c in range(DC):
                    done = mm(bank(Q_BANKS[j], 2, DC)[:, c, :], qT[:, j, c * P:(c + 1) * P], skT[:, j * DC + c, :],
                              start=True, stop=True)
                done.then_inc(S["s_ps"], 1)

            def turn(b, last=False):
                pe.wait_ge(S["hT"], b + 1)
                for j in range(2):
                    pe.wait_ge(S["s_sb"], b * 2 + j + 1)
                    for n in range(2):
                        for c in range(DC):
                            at = (2 * j + n) * 512
                            done = mm(bank(Q_BANKS[j] + n), hT[:, c, :], wq[:, c, at:at + 512], start=(c == 0), stop=(c == DC - 1))
                    done.then_inc(S["q_ps"], 1)
                q_features(b, 0)
                if not last:
                    pe.wait_ge(S["h_lo"], b + 1)
                    features(b + 1)
                scores(b, 0)
                q_features(b, 1)
                scores(b, 1)

            features(0)
            pe.wait_ge(S["skT"], 1)
            pe.wait_ge(wq_in, 16)
            turns(turn, pe)


def choose_phase(nc, a, s_dram, act_dram, g_dram, h_hi, h_lo):
    with ExitStack() as ctx:
        def sb(name, shape, dt=F32):
            return ctx.enter_context(nc.sbuf_tensor("k_" + name, shape, dt))

        def sem(name):
            return ctx.enter_context(nc.semaphore("k_" + name))

        SLOTS = NKEYS // NB
        SET = P // SLOTS
        SPH = HALF // SET
        u_raw = sb("u_raw", [P, 2, D])
        uT_hi = sb("uT_hi", [P, 2, DC, P], F32R)
        uT_lo = sb("uT_lo", [P, 2, DC, P], F32R)
        ga = sb("ga", [P, 2, SEQ])
        ident = sb("ident", [P, P])
        iota = sb("iota", [P, P])
        ss = sb("ss", [P, 2, D])
        v12 = sb("v12", [P, 2, PH, TOPK])
        i12 = sb("i12", [P, 2, PH, TOPK], U32)
        i12f = sb("i12f", [P, 2, PH, TOPK])
        cand = sb("cand", [P, PH, TOPK * TOPK])
        ci = sb("ci", [P, PH, TOPK], U32)
        onehot = sb("onehot", [P, NHK, TOPK])
        zsum = sb("zsum", [P, 2, PH])
        eg = sb("eg", [P, 3, PH, TOPK])
        egT = sb("egT", [P, 3, P])
        oh1 = sb("oh1", [P, 2, SET, P])
        oh2 = sb("oh2", [P, 2, SET, P])
        gs = sb("gs", [P, 2, NKEYS, HALF])
        ps = ctx.enter_context(nc.psum_tensor("k_ps", [P, 8, 512], F32))
        rest = onehot[:].rearrange("p a b -> p (a b)")[:, 0:4 * P].rearrange("p (n w) -> p n w", n=2)

        sc = v12[:, 0]
        c12 = i12
        c12f = cand[:, 0, :].rearrange("p (c h k) -> p c h k", c=2, h=PH)

        def bank(n, k=1, parts=None):
            v = ps[:, n:n + k, :].rearrange("p a b -> p (a b)")
            return v if parts is None else v.rearrange("p (h t) -> p h t", h=parts)

        TPS, UPS, GPS = 0, 2, 6
        names = ("uT_ps uT_hi uT_lo act_ps ga ss_read sx gx eg egT_ps egT oh weighed g_ps gs_sb passed").split()
        S = {n: sem(n) for n in names}
        consts, ss_in = sem("consts"), sem("ss_in")
        u_in, act_out, g_out = ([sem(f"{n}{k}") for k in range(2)] for n in ("u_in", "act_out", "g_out"))
        dve_steps = sem("dve_steps")
        block = ctx.enter_context(nc.Block())

        def turns(turn, eng):
            turn(0, gates=False)
            with eng.Fori(1, NB - 1) as b:
                turn(b)
            turn(NB - 1)
            turn(NB, slices=False)

        @block.sync
        def _(sp):
            for k in range(2):
                sp.sem_inc(act_out[k], 1)
                sp.sem_inc(g_out[k], 1)
            sp.dma_start(ident[:], a["c_ident"]).then_inc(consts, 16)
            sp.dma_start(iota[:], a["c_iota"]).then_inc(consts, 16)

            def store_gates(b, half):
                sp.wait_ge(S["gs_sb"], (b - 1) * SLOTS + (half + 1) * SPH)
                sp.dma_start(g_dram[(b - 1) * 2 + half], gs[:, half]).then_inc(g_out[half], 16)

            def turn(b, gates=True, slices=True):
                for j in range(SLOTS):
                    e = b * SLOTS + j
                    if slices:
                        sp.wait_ge(S["ga"], e + 1)
                        sp.dma_start(act_dram[e], ga[:, j % 2, :]).then_inc(act_out[j % 2], 16)
                    if gates and j == SPH:
                        store_gates(b, 0)
                if gates:
                    store_gates(b, 1)

            turns(turn, sp)
            for k in range(2):
                sp.wait_ge(act_out[k], NKEYS // 2 * 16 + 1)
                sp.wait_ge(g_out[k], NB * 16 + 1)

        @block.gpsimd
        def _(pool):
            u_h = a["peer_u"][0].rearrange("(e p) d -> e p d", p=P)
            for k in range(2):
                pool.dma_start(u_raw[:, k, :], u_h[k]).then_inc(u_in[k], 16)
            pool.dma_start(ss[:], s_dram[0]).then_inc(ss_in, 16)

            def turn(b, last=False):
                for j in range(SLOTS):
                    e = b * SLOTS + j
                    if not (last and j >= SLOTS - 2):
                        pool.wait_ge(S["uT_ps"], e + 1)
                        pool.dma_start(u_raw[:, j % 2, :], u_h[e + 2]).then_inc(u_in[j % 2], 16)
                    if j == PH and not last:
                        pool.wait_ge(S["ss_read"], b + 1)
                        pool.dma_start(ss[:], s_dram[b + 1]).then_inc(ss_in, 16)

            with pool.Fori(0, NB - 1) as b:
                turn(b)
            turn(NB - 1, last=True)

        @block.vector
        def _(dve):
            dve.wait_ge(consts, 32)

            def u_lo(e, k):
                dve.wait_ge(S["uT_hi"], e + 1)
                nc.vector.tensor_tensor(uT_lo[:, k].rearrange("p c t -> p (c t)"), bank(TPS, 2),
                                        uT_hi[:, k].rearrange("p c t -> p (c t)").bitcast(F32),
                                        ALU.subtract).then_inc(S["uT_lo"], 1)

            def rows(b, j):
                if j == 0:
                    dve.wait_ge(S["egT"], b)
                dve.wait_ge(S["g_ps"], (b - 1) * SLOTS + j + 1)
                ts = slice(j * SET, (j + 1) * SET)
                for n, oh in ((1, oh2), (0, oh1)):
                    made = nc.vector.tensor_tensor(
                        oh[:, j % 2], iota[:].unsqueeze(1).broadcast_to([P, SET, P]),
                        egT[:, n, ts].unsqueeze(2).broadcast_to([P, SET, P]), ALU.is_equal)
                made.then_inc(S["oh"], 1)

            def top16(s, pair, width):
                scr = [rest[:, n, 0:width] for n in range(2)]
                first = [s.mark(nc.vector.max(vals[:, 0:8], src)) for src, vals, _ in pair]
                replaced = []
                for n, (src, vals, idx) in enumerate(pair):
                    s.until(first[n])
                    nc.vector.max_index(idx[:, 0:8], vals[:, 0:8], src)
                    replaced.append(s.mark(nc.vector.match_replace(scr[n], vals[:, 0:8], src, NEG)))
                second = []
                for n, (src, vals, idx) in enumerate(pair):
                    s.until(replaced[n])
                    second.append(s.mark(nc.vector.max(vals[:, 8:16], scr[n])))
                for n, (src, vals, idx) in enumerate(pair):
                    s.until(second[n])
                    found = s.mark(nc.vector.max_index(idx[:, 8:16], vals[:, 8:16], scr[n]))
                s.until(found)

            def best_keys(s, h):
                keys = ss[:, h // 4, (h % 4) * 2 * P:((h % 4) * 2 + 2) * P].rearrange("p (c n) -> p c n", c=2)
                top16(s, [(keys[:, c, :], v12[:, c, h, :], i12[:, c, h, :]) for c in range(2)], NKEYS)

            def sums(s):
                s.step(nc.vector.tensor_copy(i12f[:], i12[:]))
                s.step(nc.vector.tensor_tensor(
                    cand[:].rearrange("p h (m n) -> p h m n", m=TOPK),
                    v12[:, 0].unsqueeze(3).broadcast_to([P, PH, TOPK, TOPK]),
                    v12[:, 1].unsqueeze(2).broadcast_to([P, PH, TOPK, TOPK]), ALU.add))

            def best_sums(s, h):
                top16(s, [(cand[:, n, :], sc[:, n, :], ci[:, n, :]) for n in (h, h + 1)], TOPK * TOPK)

            def shifted(s):
                s.step(nc.vector.tensor_tensor(eg[:, 2], sc, sc[:, :, 0:1].broadcast_to([P, PH, TOPK]), ALU.subtract))
                dve.sem_inc(S["sx"], 1)
                nc.vector.tensor_scalar(c12[:, 0], ci[:], 4, None, ALU.logical_shift_right)
                s.step(nc.vector.tensor_scalar(c12[:, 1], ci[:], TOPK - 1, None, ALU.bitwise_and))
                s.step(nc.vector.tensor_copy(c12f, c12[:]))

            def keys_of(s, c):
                s.step(nc.vector.tensor_tensor(
                    onehot[:], c12f[:, c].rearrange("p h k -> p (h k)").unsqueeze(2).broadcast_to([P, NHK, TOPK]),
                    iota[:, 0:TOPK].unsqueeze(1).broadcast_to([P, NHK, TOPK]), ALU.is_equal))
                oh4 = onehot[:].rearrange("p (h k) j -> p h k j", h=PH)
                s.step(nc.vector.tensor_tensor(
                    oh4, oh4, i12f[:, c].unsqueeze(2).broadcast_to([P, PH, TOPK, TOPK]), ALU.mult))
                s.step(nc.vector.reduce_sum(eg[:, c].rearrange("p h k -> p (h k)"), onehot[:], AX_X))

            def normalised(s, b):
                dve.wait_ge(S["gx"], b + 1)
                s.step(nc.vector.reduce_sum(zsum[:, 0, :], eg[:, 2], AX_X))
                s.step(nc.vector.reciprocal(zsum[:, 1, :], zsum[:, 0, :]))
                s.step(nc.vector.tensor_tensor(eg[:, 2], eg[:, 2], zsum[:, 1, :].unsqueeze(2).broadcast_to([P, PH, TOPK]), ALU.mult))
                dve.sem_inc(S["eg"], 1)

            def choose(s, b, j):
                if j == 0:
                    dve.wait_ge(ss_in, b * 16 + 16)
                    dve.sem_inc(S["passed"], 1)
                if j < PH:
                    best_keys(s, j)
                    if j == PH - 1:
                        dve.sem_inc(S["ss_read"], 1)
                elif j == PH:
                    sums(s)
                elif j <= PH + PH // 2:
                    best_sums(s, 2 * (j - PH - 1))
                elif j == PH + PH // 2 + 1:
                    shifted(s)
                    keys_of(s, 0)
                elif j == PH + PH // 2 + 2:
                    keys_of(s, 1)
                elif j == PH + PH // 2 + 3:
                    normalised(s, b)

            def turn(b, gates=True, slices=True):
                if slices:
                    dve.sem_clear(dve_steps)
                s = Steps(dve, dve_steps)
                for j in range(SLOTS):
                    e = b * SLOTS + j
                    if gates:
                        rows(b, j)
                    if slices:
                        if not (isinstance(b, int) and e == NKEYS - 1):
                            u_lo(e + 1, (j + 1) % 2)
                        choose(s, b, j)

            u_lo(0, 0)
            turns(turn, dve)

        @block.scalar
        def _(act):
            def u_hi(e, k):
                act.wait_ge(S["uT_ps"], e + 1)
                act.wait_ge(S["act_ps"], e + 1)
                nc.scalar.copy(uT_hi[:, k].rearrange("p c t -> p (c t)"), bank(TPS, 2)).then_inc(S["uT_hi"], 1)

            def weigh(b, j):
                act.wait_ge(S["oh"], (b - 1) * SLOTS + j + 1)
                for t in range(SET):
                    done = nc.scalar.activation(oh1[:, j % 2, t, :], oh1[:, j % 2, t, :], ACT.Copy,
                                                scale=egT[:, 2, j * SET + t:j * SET + t + 1])
                done.then_inc(S["weighed"], 1)

            def stage(b, j):
                half, at = j // SPH, j % SPH * SET
                if j % SPH == 0:
                    act.wait_ge(g_out[half], (b - 1) * 16 + 1)
                act.wait_ge(S["g_ps"], (b - 1) * SLOTS + j + 3)
                for n in range(2):
                    done = nc.scalar.copy(gs[:, half, :, at + n * 4:at + n * 4 + 4],
                                          bank(GPS + n, 1, 4).rearrange("p t e -> p e t"))
                done.then_inc(S["gs_sb"], 1)

            def turn(b, gates=True, slices=True):
                for j in range(SLOTS):
                    e = b * SLOTS + j
                    if slices and not (isinstance(b, int) and e == NKEYS - 1):
                        u_hi(e + 1, (j + 1) % 2)
                    if gates:
                        if j > 0:
                            stage(b, j - 1)
                        else:
                            act.wait_ge(S["egT_ps"], b)
                            nc.scalar.copy(egT[:], bank(GPS, 1, 4)[:, 0:3, :]).then_inc(S["egT"], 1)
                        weigh(b, j)
                    if slices:
                        if j == PH + PH // 2 + 2:
                            act.wait_ge(S["sx"], b + 1)
                            nc.scalar.activation(eg[:, 2], eg[:, 2], ACT.Exp).then_inc(S["gx"], 1)
                        act.wait_ge(S["act_ps"], e + 3)
                        act.wait_ge(act_out[j % 2], (b * (SLOTS // 2) + j // 2) * 16 + 1)
                        nc.scalar.activation(ga[:, j % 2, :], bank(UPS + 2 * (j % 2), 2), ACT.Gelu).then_inc(S["ga"], 1)
                if gates:
                    stage(b, SLOTS - 1)

            u_hi(0, 0)
            turns(turn, act)

        @block.tensor
        def _(pe):
            mm, tr = nc.tensor.matmul, nc.tensor.transpose
            pe.sem_inc(S["g_ps"], 2)
            pe.sem_inc(S["act_ps"], 2)
            pe.wait_ge(consts, 32)

            def transpose_u(e, k, loads):
                pe.wait_ge(u_in[k], loads * 16 + 16)
                for c in range(DC):
                    last = tr(bank(TPS, 2, DC)[:, c, :], u_raw[:, k, c * P:(c + 1) * P], ident[:])
                last.then_inc(S["uT_ps"], 1)

            def product_h(k, half):
                ts = slice(half * 512, (half + 1) * 512)
                for c in range(DC):
                    for m, (uv, hv) in enumerate(((uT_hi, h_hi), (uT_hi, h_lo), (uT_lo, h_hi))):
                        done = mm(bank(UPS + 2 * k + half), uv[:, k, c, :], hv[:, c, ts],
                                  start=(c == 0 and m == 0), stop=(c == DC - 1 and m == 2))
                return done

            def by_rank(b):
                pe.wait_ge(S["eg"], b)
                if not (isinstance(b, int) and b < 2):
                    pe.wait_ge(S["gs_sb"], (b - 1) * SLOTS)
                for c in range(3):
                    done = tr(bank(GPS, 1, 4)[:, c, :], eg[:, c].rearrange("p h k -> p (h k)"), ident[:])
                done.then_inc(S["egT_ps"], 1)

            def gate_products(b, j):
                pe.wait_ge(S["weighed"], (b - 1) * SLOTS + j + 1)
                if j > 0:
                    pe.wait_ge(S["gs_sb"], (b - 1) * SLOTS + j)
                for t in range(SET):
                    done = mm(bank(GPS + t // 4, 1, 4)[:, t % 4, :], oh2[:, j % 2, t, :], oh1[:, j % 2, t, :], start=True, stop=True)
                done.then_inc(S["g_ps"], 1)

            def turn(b, gates=True, slices=True):
                for j in range(SLOTS):
                    e, k = b * SLOTS + j, j % 2
                    if slices:
                        pe.wait_ge(S["uT_lo"], e + 1)
                        if not (isinstance(b, int) and e == NKEYS - 1):
                            transpose_u(e + 1, 1 - k, b * (SLOTS // 2) + (j + 1) // 2)
                        if not (isinstance(b, int) and e < 2):
                            pe.wait_ge(S["ga"], e - 1)
                        product_h(k, 0)
                    if gates and j == 0:
                        by_rank(b)
                    if slices:
                        product_h(k, 1).then_inc(S["act_ps"], 1)
                    if gates:
                        gate_products(b, j)

            transpose_u(0, 0, 0)
            turns(turn, pe)


def value_phase(nc, a, x1_dram, act_dram, g_dram):
    with ExitStack() as ctx:
        def sb(name, shape, dt=F32):
            return ctx.enter_context(nc.sbuf_tensor("v_" + name, shape, dt))

        def sem(name):
            return ctx.enter_context(nc.semaphore("v_" + name))

        GR = 4
        NGR = NKEYS // GR
        y = sb("y", [P, NB, D])
        v_raw = sb("v_raw", [P, 2, D])
        ga = sb("ga", [P, GR, SEQ])
        g_raw = sb("g_raw", [P, 2, NG, 2, HALF])
        a_hi = sb("a_hi", [P, 2, GR, SEQ], F32R)
        a_lo = sb("a_lo", [P, 2, GR, SEQ], F32R)
        v_hi = sb("v_hi", [P, 2, GR, D], F32R)
        v_lo = sb("v_lo", [P, 2, GR, D], F32R)
        stat = sb("stat", [P, 4, NB])
        ps = ctx.enter_context(nc.psum_tensor("v_ps", [P, 8, 512], F32))
        grow = ga[:, 0, :]
        YS = 4
        x1_in, out_sem, gf_in = sem("x1_in"), sem("out"), sem("gf_in")
        v_in, g_in = ([sem(f"{n}_in{k}") for k in range(2)] for n in "vg")
        a_in = [sem(f"a_in{j}") for j in range(GR)]
        names = "am a_hi a_lo v_hi v_lo y_ps y_ad ss2 ms2 rs2 fin".split()
        S = {n: sem(n) for n in names}
        act_steps, dve_steps = sem("act_steps"), sem("dve_steps")
        block = ctx.enter_context(nc.Block())

        def groups(body, eng):
            for s in range(2):
                body(0, s, first=True)
            with eng.Fori(1, NGR // 2 - 1) as i:
                for s in range(2):
                    body(i, s)
            for s in range(2):
                body(NGR // 2 - 1, s, last=True)

        @block.sync
        def _(sp):
            g_h = g_dram.rearrange("j p e t -> p j e t")

            def body(i, s, first=False, last=False):
                for j in range(GR):
                    e = (i * 2 + s) * GR + j
                    if j % 2 == 0:
                        if not (first and s == 0):
                            sp.wait_ge(S["am"], e - 2)
                        sp.dma_start(g_raw[:, j // 2], g_h[:, :, bass.ds(e, 2), :]).then_inc(g_in[j // 2], 16)
                    if not (first and s == 0):
                        sp.wait_ge(S["a_lo"], e - GR + 1)
                    sp.dma_start(ga[:, j, :], act_dram[e]).then_inc(a_in[j], 16)
                if first and s == 0:
                    sp.dma_start(y[:], x1_dram.rearrange("b p d -> p b d")).then_inc(x1_in, 16)

            groups(body, sp)
            sp.wait_ge(S["a_lo"], NKEYS)
            sp.dma_start(grow, row(a["final_norm_g"], D)).then_inc(gf_in, 16)
            out_h = a["out"][0].rearrange("(b p) d -> b p d", p=P)
            with sp.Fori(0, NB) as b:
                sp.wait_ge(S["fin"], b + 1)
                sp.dma_start(out_h[b], y[:, b, :]).then_inc(out_sem, 16)
            sp.wait_ge(out_sem, 16 * NB)

        @block.gpsimd
        def _(pool):
            v_h = a["peer_v"][0].rearrange("(e p) d -> e p d", p=P)

            def body(i, s, first=False, last=False):
                for j in range(GR):
                    e = (i * 2 + s) * GR + j
                    if not (first and s == 0 and j < 2):
                        pool.wait_ge(S["v_lo"], e - 1)
                    pool.dma_start(v_raw[:, j % 2, :], v_h[e]).then_inc(v_in[j % 2], 16)

            groups(body, pool)

        @block.tensor
        def _(pe):
            def body(i, s, first=False, last=False):
                g = i * 2 + s
                pe.wait_ge(S["a_lo"], g * GR + GR)
                pe.wait_ge(S["v_lo"], g * GR + GR)
                for b in range(NB):
                    if not (first and s == 0 and b < YS):
                        pe.wait_ge(S["y_ad"], g * NB + b - YS + 1)
                    for half in range(2):
                        ds = slice(half * 512, (half + 1) * 512)
                        ts = slice(b * P, (b + 1) * P)
                        for j in range(GR):
                            for m, (av, vv) in enumerate(((a_hi, v_hi), (a_hi, v_lo), (a_lo, v_hi))):
                                done = nc.tensor.matmul(ps[:, 2 * (b % YS) + half, :], av[:, s, j, ts], vv[:, s, j, ds],
                                                        start=(j == 0 and m == 0), stop=(j == GR - 1 and m == 2))
                    done.then_inc(S["y_ps"], 1)

            groups(body, pe)

        @block.scalar
        def _(act):
            def body(i, s, first=False, last=False):
                g = i * 2 + s
                for j in range(GR):
                    e = g * GR + j
                    if j == 0 and not first:
                        act.wait_ge(S["y_ps"], g * NB - NB)
                    act.wait_ge(v_in[j % 2], g * (GR // 2) * 16 + (j // 2) * 16 + 16)
                    nc.scalar.copy(v_hi[:, s, j, :], v_raw[:, j % 2, :]).then_inc(S["v_hi"], 1)
                    act.wait_ge(S["am"], e + 1)
                    nc.scalar.copy(a_hi[:, s, j, :], ga[:, j, :]).then_inc(S["a_hi"], 1)

            groups(body, act)
            st = Steps(act, act_steps)
            act.wait_ge(S["y_ad"], NGR * NB)
            for b in range(NB):
                st.step(nc.scalar.activation(ga[:, 1, :], y[:, b, :], ACT.Square, accum_out=stat[:, 0, b:b + 1]))
            act.sem_inc(S["ss2"], 1)
            act.wait_ge(S["ms2"], 1)
            st.step(nc.scalar.activation(stat[:, 2, :], stat[:, 1, :], ACT.Ln))
            nc.scalar.activation(stat[:, 2, :], stat[:, 2, :], ACT.Exp, scale=-0.5).then_inc(S["rs2"], 1)

        @block.vector
        def _(dve):
            def prepare(i, s, j):
                g = i * 2 + s
                e = g * GR + j
                if j % 2 == 0:
                    dve.wait_ge(g_in[j // 2], g * 16 + 16)
                dve.wait_ge(a_in[j], g * 16 + 16)
                v = ga[:, j, :].rearrange("p (j t) -> p j t", j=NG)
                nc.vector.tensor_tensor(v, v, g_raw[:, j // 2, :, j % 2, :], ALU.mult).then_inc(S["am"], 1)
                dve.wait_ge(S["v_hi"], e + 1)
                nc.vector.tensor_tensor(v_lo[:, s, j, :], v_raw[:, j % 2, :], v_hi[:, s, j, :].bitcast(F32),
                                        ALU.subtract).then_inc(S["v_lo"], 1)

            def rest_of_a(i, s, j):
                e = (i * 2 + s) * GR + j
                dve.wait_ge(S["a_hi"], e + 1)
                nc.vector.tensor_tensor(a_lo[:, s, j, :], ga[:, j, :], a_hi[:, s, j, :].bitcast(F32),
                                        ALU.subtract).then_inc(S["a_lo"], 1)

            def add(g, b):
                dve.wait_ge(S["y_ps"], g * NB + b + 1)
                nc.vector.tensor_tensor(y[:, b, :], y[:, b, :],
                                        ps[:, 2 * (b % YS):2 * (b % YS) + 2, :].rearrange("p a b -> p (a b)"),
                                        ALU.add).then_inc(S["y_ad"], 1)

            def body(i, s, first=False, last=False):
                g = i * 2 + s
                for j in range(GR):
                    prepare(i, s, j)
                    if not (first and s == 0):
                        for b in (2 * j, 2 * j + 1):
                            add(g - 1, b)
                            if b == 2 * j:
                                rest_of_a(i, s, j)
                    else:
                        rest_of_a(i, s, j)
                        if j == 0:
                            dve.wait_ge(x1_in, 16)

            groups(body, dve)
            for b in range(NB):
                add(NGR - 1, b)
            st = Steps(dve, dve_steps)
            dve.wait_ge(S["ss2"], 1)
            st.step(nc.vector.tensor_scalar(stat[:, 1, :], stat[:, 0, :], 1.0 / D, EPS, ALU.mult, ALU.add))
            dve.sem_inc(S["ms2"], 1)
            dve.wait_ge(S["rs2"], 1)
            inverse_root(nc, dve, st, stat[:, 2, :], stat[:, 1, :], stat[:, 3, :])
            dve.wait_ge(gf_in, 16)
            with dve.Fori(0, NB) as b:
                nc.vector.scalar_tensor_tensor(y[:, b, :], y[:, b, :], stat[:, 2, bass.ds(b, 1)], grow,
                                               ALU.mult, ALU.mult).then_inc(S["fin"], 1)


def build(nc, a):
    x1_dram = nc.dram_tensor("x1_scratch", [NB, P, D], F32).ap()
    g_dram = nc.dram_tensor("g_scratch", [NG, P, NKEYS, HALF], F32).ap()
    mix_dram = nc.dram_tensor("mix_scratch", [NB, P, DC, P], F32).ap()
    s_dram = nc.dram_tensor("score_scratch", [NB, P, 2, D], F32).ap()
    act_dram = nc.dram_tensor("act_scratch", [NKEYS, P, SEQ], F32).ap()
    mixer_phase(nc, a, mix_dram)
    with ExitStack() as h_space:
        with nc.sbuf_tensor("wq", [P, DC, PQ], F32, side="right") as wq, nc.semaphore("wq_in") as wq_in:
            output_phase(nc, a, mix_dram, x1_dram, wq, wq_in)
            h_hi, h_lo = (h_space.enter_context(nc.sbuf_tensor(n, [P, DC, SEQ], F32R)) for n in ("h_hi", "h_lo"))
            score_phase(nc, a, x1_dram, s_dram, wq, wq_in, h_hi, h_lo)
        choose_phase(nc, a, s_dram, act_dram, g_dram, h_hi, h_lo)
    value_phase(nc, a, x1_dram, act_dram, g_dram)


def kernel(**inputs):
    import concourse.bacc as bacc
    from concourse.bass_utils import run_bass_kernel_spmd

    nc = bacc.Bacc("TRN2", target_bir_lowering=False, num_devices=1)
    arrays = {name: np.ascontiguousarray(inputs[name]) for name in INPUTS}
    arrays.update(shape_constants())
    a = {name: nc.dram_tensor(name, v.shape, mybir.dt.from_np(v.dtype), kind="ExternalInput").ap()
         for name, v in arrays.items()}
    a["out"] = nc.dram_tensor("out", (1, SEQ, D), F32, kind="ExternalOutput").ap()
    build(nc, a)
    result = run_bass_kernel_spmd(nc, [arrays], core_ids=[0])
    return result.results[0]["out"]
```

```python
from contextlib import ExitStack

import numpy as np
import concourse.bass as bass
from concourse import mybir

P = 128
F32 = mybir.dt.float32
F32R = mybir.dt.float32r
BF16 = mybir.dt.bfloat16
U32 = mybir.dt.uint32
ALU = mybir.AluOpType
ACT = mybir.ActivationFunctionType
AX_X = mybir.AxisListType.X

D = 1024
SEQ = 1024
DC = D // P
NB = SEQ // P
HG = 4
HW = HG * P
SW_HEADS, SW_KV, HD, CHUNK = 8, 2, 64, 64
GROUP = SW_HEADS // SW_KV
IN_COLS = 4 * HW + SW_HEADS * HD + 2 * SW_KV * HD
WIN = 2 * CHUNK
LEVELS = 7
PH, NKEYS, TOPK = 8, 128, 16
PQ = PH * 2 * P
NHK = PH * TOPK
EPS = 1e-6
LOG_FLOOR = 1e-18
ARG_CAP = 80.0
NEG = -3.0e38
HALF = 64
NG = SEQ // HALF

INPUTS = ["x", "norm1_g", "w_in", "hg_lb_logits", "hg_norm_g", "sw_sinks", "w_out", "norm2_g",
          "peer_wq", "peer_subkeys", "peer_u", "peer_v", "final_norm_g"]


def shape_constants():
    t = np.arange(P)
    ident = np.eye(P, dtype=np.float32)
    upto = (t[:, None] <= t[None, :]).astype(np.float32)
    level = np.zeros((P, LEVELS + 1, P), np.float32)
    for n in range(LEVELS):
        w = P >> (n + 1)
        same = (t[:, None] // (2 * w)) == (t[None, :] // (2 * w))
        level[:, n] = same & ((t[:, None] // w) % 2 == 0) & ((t[None, :] // w) % 2 == 1)
    level[:, LEVELS] = ident
    slopes = 2.0 ** (-8.0 * (np.arange(1, SW_HEADS + 1, dtype=np.float32) / SW_HEADS))
    alibi = np.zeros((P, SW_HEADS, WIN), np.float32)
    q = np.arange(CHUNK)[:, None]
    j = np.arange(WIN)[None, :]
    own_first = np.where(j < CHUNK, np.abs(q - j), q + WIN - j)
    in_order = np.abs(q + CHUNK - j)
    for h in range(SW_HEADS):
        alibi[:CHUNK, h] = -slopes[h] * own_first
        alibi[CHUNK:, h] = -slopes[h] * in_order
    alibi0 = alibi.copy()
    alibi0[:CHUNK, :, CHUNK:] = -1e30
    iota = np.tile(t.astype(np.float32), (P, 1))
    return {"c_ident": ident, "c_upto": upto, "c_level": level, "c_alibi": alibi, "c_alibi0": alibi0,
            "c_iota": iota}


class Steps:

    def __init__(self, eng, sem, per_turn=0, turn=0):
        self.eng, self.sem, self.base, self.n = eng, sem, turn * per_turn, 0

    def mark(self, ins):
        self.n += 1
        ins.then_inc(self.sem, 1)
        return self.n

    def until(self, n):
        self.eng.wait_ge(self.sem, self.base + n)

    def step(self, ins):
        self.until(self.mark(ins))


def row(ap, width):
    return ap.rearrange("(o n) -> o n", o=1).broadcast_to([P, width])


def inverse_root(nc, dve, s, r, x, tmp):
    s.step(nc.vector.tensor_tensor(tmp, r, r, ALU.mult))
    s.step(nc.vector.tensor_tensor(tmp, tmp, x, ALU.mult))
    s.step(nc.vector.tensor_scalar(tmp, tmp, -0.5, 1.5, ALU.mult, ALU.add))
    s.step(nc.vector.tensor_tensor(r, r, tmp, ALU.mult))


def mixer_phase(nc, a, mix_dram):
    with ExitStack() as ctx:
        def sb(name, shape, dt=F32):
            return ctx.enter_context(nc.sbuf_tensor("m_" + name, shape, dt))

        def sem(name):
            return ctx.enter_context(nc.semaphore("m_" + name))

        w_in = sb("w_in", [P, DC, IN_COLS])
        ident = sb("ident", [P, P])
        upto = sb("upto", [P, P])
        level = sb("level", [P, LEVELS + 1, P], BF16)
        alibi = sb("alibi", [P, SW_HEADS, WIN])
        alibi_prev = sb("alibi_prev", [CHUNK, SW_HEADS, CHUNK])
        g1 = sb("g1", [P, D])
        lb2 = sb("lb2", [P, 2, HW])
        hgn = sb("hgn", [P, HW])
        sink = sb("sink", [P, SW_HEADS])
        tiny = sb("tiny", [P, 1])
        xb = sb("xb", [P, D])
        xn = sb("xn", [P, D])
        stat = sb("stat", [P, 4])
        hT = sb("hT", [P, DC, P])
        qr = sb("qr", [P, HW])
        zr = sb("zr", [P, HW])
        gr = sb("gr", [P, HW])
        ir = sb("ir", [P, HW])
        swq = sb("swq", [P, GROUP, SW_KV, HD])
        swkv = sb("swkv", [P, 2, SW_KV * HD])
        pT = sb("pT", [P, SW_HEADS, P])
        swv = sb("swv", [P, SW_KV * HD])
        swv_mix = sb("swv_mix", [P, SW_KV * HD])
        swqT = sb("swqT", [P, GROUP, P])
        swkT = sb("swkT", [P, P])
        swkT_mix = sb("swkT_mix", [P, P])
        ex = sb("ex", [P, 3, HW])
        kk = sb("kk", [P, HW])
        st_flat = sb("st", [P, SW_HEADS * (WIN + 1)])
        ssum = sb("ssum", [P, 2, SW_HEADS])
        qT = sb("qT", [P, 2, HG, P])
        kT = sb("kT", [P, 2, HG, P])
        bT = sb("bT", [P, 2, HG, P])
        eb = sb("eb", [P, 2, HG, P])
        vv = sb("vv", [P, 2, HW])
        gate = sb("gate", [P, 2, HW])
        dec = sb("dec", [P, 2, LEVELS, P])
        ke = sb("ke", [P, 2, LEVELS, P])
        dlast = sb("dlast", [P, HG, P])
        qb = sb("qb", [P, HG, P])
        kd = sb("kd", [P, HG, P])
        kdT = sb("kdT", [P, HG, P])
        attn = sb("attn", [P, HG, P])
        pick = sb("pick", [P, LEVELS + 1, P])
        oS = sb("oS", [P, HG, P])
        ostat = sb("ostat", [P, 3, HG])
        state = sb("state", [P, HG, P])
        ps = ctx.enter_context(nc.psum_tensor("m_ps", [P, 8, 512], F32))

        st = st_flat[:].rearrange("p (h w) -> p h w", h=SW_HEADS)
        mixS = st_flat[:, 0:HW].rearrange("p (h t) -> p h t", h=HG)
        mixH = oS
        lmax = vv[:, 0, :]
        qs, ff = ex[:, 0, :], ex[:, 2, :]

        def bank(n, k=1, heads=None):
            v = ps[:, n:n + k, :].rearrange("p a b -> p (a b)")
            return v if heads is None else v.rearrange("p (h t) -> p h t", h=heads)

        B_SWQ, B_SWKV, B_Q, B_Z, B_GATE, B_I = 0, 1, 0, 1, 0, 1
        B_SWQT, B_SWKT, B_QT, B_KT, B_CUM, B_OT = 2, 3, 2, 3, 2, 2
        B_SW = B_PT = (2, 3)
        B_LEVELS, B_O, B_ONT, B_KDT, B_U = 6, 4, 4, 5, 5

        consts, x_in = sem("consts"), sem("x_in")
        mix_out = [sem(f"mix_out{n}") for n in range(2)]
        tab, ready, lexp = sem("tab"), sem("ready"), sem("lexp")
        names = ("ss ms rs xn hT_ps hT old q_ps z_ps gate_ps i_ps swq_ps swkv_ps swq swkv qr zr gr ir swT kqT kept mix "
                 "sc e ex f logf qkT qkTs b bS s p pn pT pTs oT oTs Dl E QK KDT kdT hs at O U oS oms ors on onT mixT "
                 "passed").split()
        S = {n: sem(n) for n in names}
        act_steps, dve_steps, pool_steps = sem("act_steps"), sem("dve_steps"), sem("pool_steps")
        NCONST = 11
        pro_steps, pro_steps_act = sem("pro_steps"), sem("pro_steps_act")

        block = ctx.enter_context(nc.Block())

        def turns(turn, eng):
            turn(-2, 0, second=False, third=False, out=False)
            turn(-1, 1, third=False, out=False)
            turn(0, 0, out=False)
            with eng.Fori(0, (NB - 4) // 2) as i:
                for k in (1, 2):
                    turn(i * 2 + k, k % 2)
            turn(NB - 3, 1, norm=False)
            turn(NB - 2, 0, norm=False, first=False)
            turn(NB - 1, 1, norm=False, first=False, second=False)
            turn(NB, 0, norm=False, first=False, second=False, third=False)

        @block.sync
        def _(sp):
            x_h = a["x"][0].rearrange("(b p) d -> b p d", p=P)
            sp.dma_start(xb[:], x_h[0]).then_inc(x_in, 16)
            sp.dma_start(ident[:], a["c_ident"]).then_inc(consts, 16)
            sp.dma_start(g1[:], row(a["norm1_g"][0], D)).then_inc(consts, 16)
            for k in range(2):
                sp.dma_start(lb2[:, k, :], row(a["hg_lb_logits"][k], HW)).then_inc(consts, 16)
            sp.dma_start(hgn[:], row(a["hg_norm_g"][0], HW)).then_inc(consts, 16)
            sp.dma_start(sink[:], row(a["sw_sinks"][0], SW_HEADS)).then_inc(consts, 16)
            sp.dma_start(w_in[:], a["w_in"][0].rearrange("(c p) n -> p c n", p=P)).then_inc(consts, 16)
            sp.dma_start(upto[:], a["c_upto"]).then_inc(consts, 16)
            sp.dma_start(pick[:], a["c_level"]).then_inc(consts, 16)
            sp.dma_start(alibi[:], a["c_alibi0"]).then_inc(consts, 16)
            sp.dma_start(alibi_prev[:], a["c_alibi"][0:CHUNK, :, CHUNK:WIN]).then_inc(consts, 16)


            def turn(c, k, norm=True, first=True, second=True, third=True, out=True):
                if norm:
                    sp.wait_ge(S["xn"], c + 3)
                    sp.dma_start(xb[:], x_h[c + 3]).then_inc(x_in, 16)
                if out:
                    sp.wait_ge(S["mixT"], c)
                    sp.dma_start(mix_dram[c - 1, :, :HG, :], mixH[:]).then_inc(mix_out[1], 16)
                if second:
                    sp.wait_ge(S["oTs"], c + 2)
                    sp.dma_start(mix_dram[c + 1, :, HG:, :], mixS).then_inc(mix_out[0], 16)

            turns(turn, sp)
            for n in range(2):
                sp.wait_ge(mix_out[n], NB * 16)

        @block.gpsimd
        def _(pool):
            pool.wait_ge(ready, 1)

            def turn(c, k, norm=True, first=True, second=True, third=True, out=True):
                if not second:
                    return
                n, m = c + 1, 1 - k
                pool.sem_clear(pool_steps)
                s = Steps(pool, pool_steps)
                if not (isinstance(c, int) and c < 0):
                    pool.wait_ge(S["oT"], n)
                    pool.sem_inc(S["passed"], 1)
                s.step(nc.gpsimd.tensor_copy(swv_mix[CHUNK:, :], swv[CHUNK:, :]))
                s.step(nc.gpsimd.tensor_copy(swkT_mix[:, CHUNK:], swkT[:, CHUNK:]))
                pool.sem_inc(S["old"], 1)
                pool.wait_ge(S["swkv"], n + 1)
                pool.sem_inc(S["passed"], 1)
                s.step(nc.gpsimd.tensor_copy(swv[:], swkv[:, 1]))
                s.step(nc.gpsimd.tensor_copy(swv_mix[:CHUNK, :], swkv[:CHUNK, 1]))
                pool.wait_ge(S["ir"], n + 1)
                if not (isinstance(c, int) and c < 1):
                    pool.wait_ge(S["U"], c)
                pool.sem_inc(S["passed"], 1)
                s.step(nc.gpsimd.tensor_copy(vv[:, m], ir[:]))
                pool.sem_inc(S["kept"], 1)
                pool.wait_ge(S["kqT"], n + 1)
                pool.sem_inc(S["passed"], 1)
                nc.gpsimd.tensor_copy(swkT_mix[:, :CHUNK], swkT[:, :CHUNK]).then_inc(S["mix"], 1)

            turns(turn, pool)

        @block.vector
        def _(dve):
            s = Steps(dve, dve_steps)
            s.step(nc.vector.memset(tiny[:], LOG_FLOOR))
            nc.vector.memset(state[:], 0.0)
            nc.vector.memset(swv[:], 0.0)
            s.step(nc.vector.memset(swkT[:], 0.0))
            dve.wait_ge(consts, 16 * NCONST)
            s.step(nc.vector.tensor_copy(level[:], pick[:]))
            s.step(nc.vector.tensor_tensor(lmax, lb2[:, 0, :], lb2[:, 1, :], ALU.max))
            s.step(nc.vector.tensor_tensor(lb2[:], lb2[:], lmax.unsqueeze(1).broadcast_to([P, 2, HW]), ALU.subtract))
            dve.sem_inc(tab, 1)
            dve.wait_ge(lexp, 1)
            s.step(nc.vector.tensor_tensor(lmax, lb2[:, 0, :], lb2[:, 1, :], ALU.add))
            s.step(nc.vector.reciprocal(lmax, lmax))
            s.step(nc.vector.tensor_tensor(lb2[:], lb2[:], lmax.unsqueeze(1).broadcast_to([P, 2, HW]), ALU.mult))
            lb, omlb = lb2[:, 0, :], lb2[:, 1, :]
            dve.sem_inc(ready, 1)

            def normed(s, n):
                dve.wait_ge(S["ss"], n + 1)
                s.step(nc.vector.tensor_scalar(stat[:, 1:2], stat[:, 0:1], 1.0 / D, EPS, ALU.mult, ALU.add))
                dve.sem_inc(S["ms"], 1)
                dve.wait_ge(S["rs"], n + 1)
                inverse_root(nc, dve, s, stat[:, 2:3], stat[:, 1:2], stat[:, 3:4])
                nc.vector.scalar_tensor_tensor(xn[:], xb[:], stat[:, 2:3], g1[:], ALU.mult, ALU.mult).then_inc(S["xn"], 1)

            def caps(n, first):
                dve.wait_ge(S["ir"], n + 1)
                if not first:
                    dve.wait_ge(S["b"], n)
                nc.vector.tensor_scalar(ex[:, 0, :], qr[:], -ARG_CAP, -1.0, ALU.max, ALU.mult)
                nc.vector.tensor_scalar(ex[:, 1, :], gr[:], -ARG_CAP, -1.0, ALU.max, ALU.mult)
                nc.vector.tensor_scalar(ex[:, 2, :], zr[:], ARG_CAP, None, ALU.min).then_inc(S["e"], 1)

            def sigmoids(s, n, m):
                dve.wait_ge(S["ex"], n + 1)
                qg = ex[:, 0:2, :]
                nc.vector.tensor_scalar(qg, qg, 1.0, None, ALU.add)
                s.step(nc.vector.tensor_scalar(kk[:], ex[:, 2, :], 1.0, None, ALU.add))
                nc.vector.reciprocal(qg, qg)
                s.step(nc.vector.reciprocal(kk[:], kk[:]))
                s.step(nc.vector.tensor_tensor(kk[:], kk[:], omlb, ALU.mult))
                nc.vector.tensor_tensor(qs, qr[:], qs, ALU.mult)
                s.step(nc.vector.tensor_tensor(ff, ff, kk[:], ALU.mult))
                nc.vector.tensor_tensor(gate[:, m], gr[:], ex[:, 1, :], ALU.mult)
                s.step(nc.vector.tensor_tensor(ff, ff, lb, ALU.add))
                dve.sem_inc(S["f"], 1)
                s.step(nc.vector.tensor_tensor(gate[:, m], gate[:, m], hgn[:], ALU.mult))

            def window_scores(s, n, first):
                if not first:
                    dve.wait_ge(mix_out[0], n * 16)
                nc.vector.tensor_copy(st[:, :, WIN:WIN + 1], sink[:].unsqueeze(2))
                dve.wait_ge(S["sc"], n + 1)
                for g in range(SW_KV):
                    hs = slice(g * GROUP, (g + 1) * GROUP)
                    s.step(nc.vector.scalar_tensor_tensor(st[:, hs, 0:WIN], bank(B_SW[g], 1, GROUP), HD ** -0.5,
                                                          alibi[:, hs, :], ALU.mult, ALU.add))
                s.step(nc.vector.tensor_copy(alibi[:CHUNK, :, CHUNK:], alibi_prev[:]))
                s.step(nc.vector.reduce_max(ssum[:, 0, :], st, AX_X))
                s.step(nc.vector.tensor_tensor(st, st, ssum[:, 0, :].unsqueeze(2).broadcast_to([P, SW_HEADS, WIN + 1]),
                                               ALU.subtract))
                dve.sem_inc(S["s"], 1)

            def window_probs(s, n):
                dve.wait_ge(S["p"], n + 1)
                s.step(nc.vector.reduce_sum(ssum[:, 0, :], st, AX_X))
                s.step(nc.vector.reciprocal(ssum[:, 1, :], ssum[:, 0, :]))
                s.step(nc.vector.tensor_tensor(st, st, ssum[:, 1, :].unsqueeze(2).broadcast_to([P, SW_HEADS, WIN + 1]),
                                               ALU.mult))
                dve.sem_inc(S["pn"], 1)

            def log_decays(s, b, k, h):
                if h >= 2:
                    dve.wait_ge(S["hs"], b * HG + h - 1)
                if h == 0:
                    dve.wait_ge(S["bS"], b + 1)
                    nc.vector.tensor_tensor(dlast[:], bT[:, k, :, P - 1:P].broadcast_to([P, HG, P]), bT[:, k], ALU.subtract)
                for n in range(LEVELS):
                    w = P >> (n + 1)
                    bv = bT[:, k, h, :].rearrange("p (m w) -> p m w", w=2 * w)
                    dv = dec[:, h % 2, n].rearrange("p (m w) -> p m w", w=2 * w)
                    ref = bv[:, :, w - 1:w].broadcast_to([P, P // (2 * w), w])
                    nc.vector.tensor_tensor(dv[:, :, w:], bv[:, :, w:], ref, ALU.subtract)
                    done = nc.vector.tensor_tensor(dv[:, :, :w], ref, bv[:, :, :w], ALU.subtract)
                done.then_inc(S["Dl"], 1)

            def decayed(s, b, k, h):
                dve.wait_ge(S["E"], b * HG + h + 1)
                if h == 0:
                    nc.vector.tensor_tensor(qb[:], qT[:, k], eb[:, k], ALU.mult)
                    nc.vector.tensor_tensor(kd[:], kT[:, k], dlast[:], ALU.mult)
                d = dec[:, h % 2]
                s.step(nc.vector.tensor_tensor(ke[:, h % 2], d, kT[:, k, h, :].unsqueeze(1).broadcast_to([P, LEVELS, P]), ALU.mult))
                nc.vector.tensor_tensor(d, d, qT[:, k, h, :].unsqueeze(1).broadcast_to([P, LEVELS, P]),
                                        ALU.mult).then_inc(S["QK"], 1)

            def weights(s, b, h):
                dve.wait_ge(S["hs"], b * HG + h + 1)
                s.step(nc.vector.tensor_tensor(pick[:], bank(B_LEVELS, 2, LEVELS + 1), level[:], ALU.mult))
                nc.vector.reduce_sum(attn[:, h, :], pick[:].rearrange("p l t -> p t l"), AX_X).then_inc(S["at"], 1)

            def outputs(s, b, k):
                dve.wait_ge(S["U"], b + 1)
                for h in range(HG):
                    done = nc.vector.scalar_tensor_tensor(state[:, h, :], state[:, h, :], eb[:, k, h, P - 1:P],
                                                          bank(B_U, 1, HG)[:, h, :], ALU.mult, ALU.add)
                s.step(done)
                dve.wait_ge(S["oS"], b + 1)
                sq = pick[:, 0:HG, :]
                s.step(nc.vector.tensor_tensor(sq, oS[:], oS[:], ALU.mult))
                s.step(nc.vector.reduce_sum(ostat[:, 0, :], sq, AX_X))
                s.step(nc.vector.tensor_scalar(ostat[:, 0, :], ostat[:, 0, :], 1.0 / P, EPS, ALU.mult, ALU.add))
                dve.sem_inc(S["oms"], 1)
                s.step(nc.vector.tensor_tensor(oS[:], oS[:], gate[:, k].rearrange("p (h t) -> p h t", h=HG), ALU.mult))
                dve.wait_ge(S["ors"], b + 1)
                inverse_root(nc, dve, s, ostat[:, 1, :], ostat[:, 0, :], ostat[:, 2, :])
                s.step(nc.vector.tensor_tensor(oS[:], oS[:], ostat[:, 1, :].unsqueeze(2).broadcast_to([P, HG, P]), ALU.mult))
                dve.sem_inc(S["on"], 1)

            def turn(c, k, norm=True, first=True, second=True, third=True, out=True):
                n, m = c + 1, 1 - k
                start = isinstance(c, int) and c < 0
                dve.sem_clear(dve_steps)
                s = Steps(dve, dve_steps)
                if third:
                    log_decays(s, c, k, 0)
                if second:
                    caps(n, start)
                if third:
                    log_decays(s, c, k, 1)
                    decayed(s, c, k, 0)
                    decayed(s, c, k, 1)
                    weights(s, c, 0)
                    log_decays(s, c, k, 2)
                if second:
                    sigmoids(s, n, m)
                if third:
                    decayed(s, c, k, 2)
                    weights(s, c, 1)
                    log_decays(s, c, k, 3)
                if second:
                    window_scores(s, n, start)
                if third:
                    decayed(s, c, k, 3)
                    weights(s, c, 2)
                if norm:
                    normed(s, c + 3)
                if second:
                    window_probs(s, n)
                if third:
                    weights(s, c, 3)
                    outputs(s, c, k)

            normed(Steps(dve, pro_steps), 0)
            turns(turn, dve)

        @block.scalar
        def _(act):
            act.wait_ge(tab, 1)
            nc.scalar.activation(lb2[:], lb2[:], ACT.Exp).then_inc(lexp, 1)
            act.wait_ge(ready, 1)

            def decays(s, b, h):
                act.wait_ge(S["Dl"], b * HG + h + 1)
                if h == 0:
                    s.step(nc.scalar.activation(dlast[:], dlast[:], ACT.Exp))
                nc.scalar.activation(dec[:, h % 2], dec[:, h % 2], ACT.Exp).then_inc(S["E"], 1)

            def evacuate(to, frm, done_sem, a_):
                act.wait_ge(S[done_sem + "_ps"], a_ + 1)
                return nc.scalar.copy(to, frm)

            def squares(n):
                act.wait_ge(x_in, n * 16 + 16)
                nc.scalar.activation(xn[:], xb[:], ACT.Square, accum_out=stat[:, 0:1]).then_inc(S["ss"], 1)

            def root(s, n):
                act.wait_ge(S["ms"], n + 1)
                s.step(nc.scalar.activation(stat[:, 2:3], stat[:, 1:2], ACT.Ln))
                nc.scalar.activation(stat[:, 2:3], stat[:, 2:3], ACT.Exp, scale=-0.5).then_inc(S["rs"], 1)

            def features(n):
                act.wait_ge(S["hT_ps"], n + 1)
                for c in range(2):
                    done = nc.scalar.copy(hT[:, 4 * c:4 * c + 4, :], bank(c, 1, 4))
                done.then_inc(S["hT"], 1)

            def turn(c, k, norm=True, first=True, second=True, third=True, out=True):
                p, n, m = c + 2, c + 1, 1 - k
                act.sem_clear(act_steps)
                s = Steps(act, act_steps)
                if third:
                    decays(s, c, 0)
                if second:
                    act.wait_ge(S["swT"], n + 1)
                    act.wait_ge(S["old"], n + 1)
                    nc.scalar.copy(swqT[:], bank(B_SWQT, 1, GROUP))
                    nc.scalar.copy(swkT[:], bank(B_SWKT)[:, 0:P]).then_inc(S["kqT"], 1)
                    act.wait_ge(S["e"], n + 1)
                    nc.scalar.activation(ex[:], ex[:], ACT.Exp).then_inc(S["ex"], 1)
                if third:
                    decays(s, c, 1)
                if out:
                    act.wait_ge(S["onT"], c)
                    nc.scalar.copy(mixH[:], bank(B_ONT, 1, 4)).then_inc(S["mixT"], 1)
                if third:
                    act.wait_ge(S["KDT"], c + 1)
                    nc.scalar.copy(kdT[:], bank(B_KDT, 1, HG)).then_inc(S["kdT"], 1)
                if first:
                    evacuate(swq[:].rearrange("p i g d -> p g i d"),
                             bank(B_SWQ).rearrange("p (g i d) -> p g i d", g=SW_KV, i=GROUP), "swq", p).then_inc(S["swq"], 1)
                    if second:
                        act.wait_ge(S["kept"], n + 1)
                    evacuate(swkv[:].rearrange("p n d -> p (n d)"), bank(B_SWKV)[:, 0:2 * SW_KV * HD], "swkv", p).then_inc(S["swkv"], 1)
                if third:
                    decays(s, c, 2)
                if second:
                    act.wait_ge(S["f"], n + 1)
                    nc.scalar.activation(ff, ff, ACT.Ln, bias=tiny[:]).then_inc(S["logf"], 1)
                if first:
                    evacuate(qr[:], bank(B_Q), "q", p).then_inc(S["qr"], 1)
                if third:
                    decays(s, c, 3)
                if first:
                    evacuate(zr[:], bank(B_Z), "z", p).then_inc(S["zr"], 1)
                if norm:
                    squares(c + 3)
                if second:
                    act.wait_ge(S["s"], n + 1)
                    nc.scalar.activation(st, st, ACT.Exp).then_inc(S["p"], 1)
                    act.wait_ge(S["qkT"], n + 1)
                    nc.scalar.copy(qT[:, m], bank(B_QT, 1, HG))
                    nc.scalar.copy(kT[:, m], bank(B_KT, 1, HG)).then_inc(S["qkTs"], 1)
                if norm:
                    root(s, c + 3)
                if first:
                    evacuate(gr[:], bank(B_GATE), "gate", p).then_inc(S["gr"], 1)
                if second:
                    act.wait_ge(S["b"], n + 1)
                    nc.scalar.copy(bT[:, m], bank(B_CUM, 1, HG))
                    nc.scalar.activation(eb[:, m], bank(B_CUM, 1, HG), ACT.Exp).then_inc(S["bS"], 1)
                if first:
                    evacuate(ir[:], bank(B_I), "i", p).then_inc(S["ir"], 1)
                if third:
                    if out:
                        act.wait_ge(mix_out[1], c * 16)
                    act.wait_ge(S["O"], c + 1)
                    nc.scalar.copy(oS[:], bank(B_O, 1, HG)).then_inc(S["oS"], 1)
                if second:
                    act.wait_ge(S["pT"], n + 1)
                    for g in range(2):
                        done = nc.scalar.copy(pT[:, 4 * g:4 * g + 4, :], bank(B_PT[g], 1, 4))
                    done.then_inc(S["pTs"], 1)
                if norm:
                    features(c + 3)
                if third:
                    act.wait_ge(S["oms"], c + 1)
                    s.step(nc.scalar.activation(ostat[:, 1, :], ostat[:, 0, :], ACT.Ln))
                    nc.scalar.activation(ostat[:, 1, :], ostat[:, 1, :], ACT.Exp, scale=-0.5).then_inc(S["ors"], 1)
                if second:
                    act.wait_ge(S["oT"], n + 1)
                    nc.scalar.copy(mixS, bank(B_OT, 1, 4)).then_inc(S["oTs"], 1)

            squares(0)
            root(Steps(act, pro_steps_act), 0)
            features(0)
            turns(turn, act)

        @block.tensor
        def _(pe):
            mm, tr = nc.tensor.matmul, nc.tensor.transpose
            pe.wait_ge(consts, 16 * NCONST)

            def project(n, to, at, width, done_sem):
                for c in range(DC):
                    done = mm(bank(to)[:, 0:width], hT[:, c, :], w_in[:, c, at:at + width],
                              start=(c == 0), stop=(c == DC - 1))
                done.then_inc(S[done_sem], 1)

            def level_scores(b, k, h):
                pe.wait_ge(S["QK"], b * HG + h + 1)
                if h == 0:
                    for j in range(HG):
                        done = tr(bank(B_KDT, 1, HG)[:, j, :], kd[:, j, :], ident[:])
                    done.then_inc(S["KDT"], 1)
                else:
                    pe.wait_ge(S["at"], b * HG + h)
                sc = bank(B_LEVELS, 2, LEVELS + 1)
                for n in range(LEVELS):
                    mm(sc[:, n, :], ke[:, h % 2, n, :], dec[:, h % 2, n, :], start=True, stop=True)
                mm(sc[:, LEVELS, :], kT[:, k, h, :], qT[:, k, h, :], start=True, stop=True).then_inc(S["hs"], 1)

            def features(n):
                pe.wait_ge(S["xn"], n + 1)
                for c in range(DC):
                    done = tr(bank(c // 4, 1, 4)[:, c % 4, :], xn[:, c * P:(c + 1) * P], ident[:])
                done.then_inc(S["hT_ps"], 1)

            def turn(c, k, norm=True, first=True, second=True, third=True, out=True):
                p, n, m = c + 2, c + 1, 1 - k
                if second:
                    if not (isinstance(c, int) and c < 0):
                        pe.wait_ge(S["oTs"], n)
                    pe.wait_ge(S["swkv"], n + 1)
                    for i in range(GROUP):
                        tr(bank(B_SWQT, 1, GROUP)[:, i, :], swq[:, i].rearrange("p g d -> p (g d)"), ident[:])
                    tr(bank(B_SWKT)[:, 0:P], swkv[:, 0], ident[:]).then_inc(S["swT"], 1)
                if first:
                    pe.wait_ge(S["hT"], p + 1)
                    project(p, B_SWQ, 4 * HW, SW_HEADS * HD, "swq_ps")
                    project(p, B_SWKV, 4 * HW + SW_HEADS * HD, 2 * SW_KV * HD, "swkv_ps")
                if out:
                    pe.wait_ge(S["on"], c)
                    for h in range(HG):
                        done = tr(bank(B_ONT, 1, HG)[:, h, :], oS[:, h, :], ident[:])
                    done.then_inc(S["onT"], 1)
                if third:
                    level_scores(c, k, 0)
                if second:
                    pe.wait_ge(S["kqT"], n + 1)
                    pe.wait_ge(S["mix"], n + 1)
                    pe.sem_inc(S["passed"], 1)
                    for g2 in range(2):
                        keys = swkT_mix if g2 == 0 else swkT
                        for i in range(GROUP):
                            for g in range(SW_KV):
                                done = mm(ps[g2 * CHUNK:(g2 + 1) * CHUNK, B_SW[g], i * WIN:(i + 1) * WIN],
                                          swqT[g * HD:(g + 1) * HD, i, g2 * CHUNK:(g2 + 1) * CHUNK],
                                          keys[g * HD:(g + 1) * HD, :], start=True, stop=True)
                    done.then_inc(S["sc"], 1)
                if first:
                    pe.wait_ge(S["swq"], p + 1)
                    project(p, B_Q, 0, HW, "q_ps")
                if third:
                    level_scores(c, k, 1)
                if first:
                    pe.wait_ge(S["swkv"], p + 1)
                    project(p, B_Z, HW, HW, "z_ps")
                if third:
                    level_scores(c, k, 2)
                if second:
                    pe.wait_ge(S["f"], n + 1)
                    pe.wait_ge(S["s"], n + 1)
                    for h in range(HG):
                        tr(bank(B_QT, 1, HG)[:, h, :], qs[:, h * P:(h + 1) * P], ident[:])
                    for h in range(HG):
                        done = tr(bank(B_KT, 1, HG)[:, h, :], kk[:, h * P:(h + 1) * P], ident[:])
                    done.then_inc(S["qkT"], 1)
                if first:
                    pe.wait_ge(S["qr"], p + 1)
                    project(p, B_GATE, 3 * HW, HW, "gate_ps")
                if second:
                    pe.wait_ge(S["logf"], n + 1)
                    pe.wait_ge(S["qkTs"], n + 1)
                    for h in range(HG):
                        done = mm(bank(B_CUM, 1, HG)[:, h, :], ff[:, h * P:(h + 1) * P], upto[:], start=True, stop=True)
                    done.then_inc(S["b"], 1)
                if third:
                    level_scores(c, k, 3)
                if first:
                    pe.wait_ge(S["zr"], p + 1)
                    project(p, B_I, 2 * HW, HW, "i_ps")
                if third:
                    pe.wait_ge(S["kdT"], c + 1)
                    pe.wait_ge(S["kept"], c + 1)
                    if out:
                        pe.wait_ge(S["mixT"], c)
                    o = bank(B_O, 1, HG)
                    for h in range(HG):
                        pe.wait_ge(S["at"], c * HG + h + 1)
                        mm(o[:, h, :], attn[:, h, :], vv[:, k, h * P:(h + 1) * P], start=True, stop=False)
                        done = mm(o[:, h, :], qb[:, h, :], state[:, h, :], start=False, stop=True)
                    done.then_inc(S["O"], 1)
                    for h in range(HG):
                        done = mm(bank(B_U, 1, HG)[:, h, :], kdT[:, h, :], vv[:, k, h * P:(h + 1) * P], start=True, stop=True)
                    done.then_inc(S["U"], 1)
                if second:
                    pe.wait_ge(S["pn"], n + 1)
                    pe.wait_ge(S["bS"], n + 1)
                    for h in range(SW_HEADS):
                        done = tr(bank(B_PT[h // 4], 1, 4)[:, h % 4, :], st[:, h, 0:WIN], ident[:])
                    done.then_inc(S["pT"], 1)
                if norm:
                    pe.wait_ge(S["gr"], p + 1)
                    pe.wait_ge(S["ir"], p + 1)
                    features(c + 3)
                if second:
                    pe.wait_ge(S["pTs"], n + 1)
                    for h in range(SW_HEADS):
                        g, half = h // GROUP, (h % 2) * HD
                        for g2 in range(2):
                            vals = swv_mix if g2 == 0 else swv
                            done = mm(ps[half:half + HD, B_OT, (h // 2) * P + g2 * CHUNK:(h // 2) * P + (g2 + 1) * CHUNK],
                                      vals[:, g * HD:(g + 1) * HD], pT[:, h, g2 * CHUNK:(g2 + 1) * CHUNK],
                                      start=True, stop=True)
                    done.then_inc(S["oT"], 1)

            features(0)
            turns(turn, pe)


def output_phase(nc, a, mix_dram, x1_dram, wq, wq_in):
    with ExitStack() as ctx:
        def sb(name, shape, dt=F32):
            return ctx.enter_context(nc.sbuf_tensor("o_" + name, shape, dt))

        def sem(name):
            return ctx.enter_context(nc.semaphore("o_" + name))

        w_raw = sb("w_raw", [P, DC, D])
        w_hi = sb("w_hi", [P, DC, D], F32R)
        w_lo = sb("w_lo", [P, DC, D], F32R)
        xb = sb("xb", [P, 2, D])
        mixT = sb("mixT", [P, 2, D])
        m_hi = sb("m_hi", [P, 2, D], F32R)
        m_lo = sb("m_lo", [P, 2, D], F32R)
        ps = ctx.enter_context(nc.psum_tensor("o_ps", [P, 2, 2, 512], F32))
        w_in, m_in, x_in, x1_out = sem("w_in"), *([sem(f"{n}{k}") for k in range(2)] for n in ("m_in", "x_in", "x1_out"))
        S = {n: sem(n) for n in "w_hi w_lo m_hi m_lo out x1 stored".split()}
        block = ctx.enter_context(nc.Block())

        @block.sync
        def _(sp):
            x_h = a["x"][0].rearrange("(b p) d -> b p d", p=P)

            def load(b, k):
                sp.dma_start(mixT[:, k, :], mix_dram[b].rearrange("p c t -> p (c t)")).then_inc(m_in[k], 16)
                sp.dma_start(xb[:, k, :], x_h[b]).then_inc(x_in[k], 16)

            sp.dma_start(w_raw[:], a["w_out"][0].rearrange("(c p) n -> p c n", p=P)).then_inc(w_in, 16)
            load(0, 0)
            load(1, 1)
            sp.dma_start(wq[:], a["peer_wq"][0].rearrange("(c p) n -> p c n", p=P)).then_inc(wq_in, 16)

            def turn(i, k, last=False):
                b = i * 2 + k
                sp.wait_ge(S["x1"], b + 1)
                sp.dma_start(x1_dram[b], xb[:, k, :]).then_inc(x1_out[k], 16)
                sp.wait_ge(x1_out[k], i * 16 + 16)
                sp.sem_inc(S["stored"], 1)
                if not last:
                    load(b + 2, k)

            with sp.Fori(0, NB // 2 - 1) as i:
                for k in range(2):
                    turn(i, k)
            for k in range(2):
                turn(NB // 2 - 1, k, last=True)

        @block.scalar
        def _(act):
            act.wait_ge(w_in, 16)
            for c in range(DC):
                nc.scalar.copy(w_hi[:, c, :], w_raw[:, c, :]).then_inc(S["w_hi"], 1)
            act.sem_inc(S["out"], 2)
            with act.Fori(0, NB // 2) as i:
                for k in range(2):
                    b = i * 2 + k
                    act.wait_ge(m_in[k], i * 16 + 16)
                    act.wait_ge(S["out"], b + 1)
                    nc.scalar.copy(m_hi[:, k, :], mixT[:, k, :]).then_inc(S["m_hi"], 1)

        @block.vector
        def _(dve):
            for c in range(DC):
                dve.wait_ge(S["w_hi"], c + 1)
                nc.vector.tensor_tensor(w_lo[:, c, :], w_raw[:, c, :], w_hi[:, c, :].bitcast(F32), ALU.subtract).then_inc(S["w_lo"], 1)

            def split(b, k):
                dve.wait_ge(S["m_hi"], b + 1)
                nc.vector.tensor_tensor(m_lo[:, k, :], mixT[:, k, :], m_hi[:, k, :].bitcast(F32), ALU.subtract).then_inc(S["m_lo"], 1)

            def add(i, k):
                dve.wait_ge(x_in[k], i * 16 + 16)
                dve.wait_ge(S["out"], i * 2 + k + 3)
                nc.vector.tensor_tensor(xb[:, k, :], xb[:, k, :], ps[:, k].rearrange("p a b -> p (a b)"),
                                        ALU.add).then_inc(S["x1"], 1)

            split(0, 0)
            with dve.Fori(0, NB // 2 - 1) as i:
                for k in range(2):
                    split(i * 2 + k + 1, 1 - k)
                    add(i, k)
            split(NB - 1, 1)
            add(NB // 2 - 1, 0)
            add(NB // 2 - 1, 1)

        @block.tensor
        def _(pe):
            pe.wait_ge(S["w_lo"], DC)

            def turn(b, k, first=False):
                pe.wait_ge(S["m_lo"], b + 1)
                if not first:
                    pe.wait_ge(S["x1"], b - 1)
                for half in range(2):
                    for c in range(DC):
                        for m, (mv, wv) in enumerate(((m_hi, w_hi), (m_hi, w_lo), (m_lo, w_hi))):
                            done = nc.tensor.matmul(ps[:, k, half, :], mv[:, k, c * P:(c + 1) * P],
                                                    wv[:, c, half * 512:(half + 1) * 512],
                                                    start=(c == 0 and m == 0), stop=(c == DC - 1 and m == 2))
                done.then_inc(S["out"], 1)

            turn(0, 0, first=True)
            turn(1, 1, first=True)
            with pe.Fori(1, NB // 2) as i:
                for k in range(2):
                    turn(i * 2 + k, k)


def score_phase(nc, a, x1_dram, s_dram, wq, wq_in, h_hi, h_lo):
    with ExitStack() as ctx:
        def sb(name, shape, dt=F32):
            return ctx.enter_context(nc.sbuf_tensor("s_" + name, shape, dt))

        def sem(name):
            return ctx.enter_context(nc.semaphore("s_" + name))

        skT = sb("skT", [P, 2 * PH, NKEYS])
        ident = sb("ident", [P, P])
        g2 = sb("g2", [P, D])
        xb = sb("xb", [P, D])
        xn = sb("xn", [P, D])
        squares = sb("squares", [P, D])
        stat = sb("stat", [P, 4])
        hT = sb("hT", [P, DC, P])
        qq = sb("qq", [P, 2, D])
        qT = sb("qT", [P, 2, D])
        ss = sb("ss", [P, 2, D])
        ps = ctx.enter_context(nc.psum_tensor("s_ps", [P, 8, 512], F32))
        subkeys = qq[:].rearrange("p j d -> p (j d)").rearrange("p (k d) -> p k d", d=P)

        def bank(n, k=1, parts=None):
            v = ps[:, n:n + k, :].rearrange("p a b -> p (a b)")
            return v if parts is None else v.rearrange("p (h t) -> p h t", h=parts)

        Q_BANKS, H_BANKS, QT_BANKS = (0, 2), 4, 6
        names = "ss ms rs xn hT_ps hT h_hi h_lo q_ps q_sb qT_ps qT_sb s_ps s_sb skT_ps skT".split()
        S = {n: sem(n) for n in names}
        consts, x1_in, s_out = sem("consts"), sem("x1_in"), sem("s_out")
        act_steps, dve_steps = sem("act_steps"), sem("dve_steps")
        NC = 3
        block = ctx.enter_context(nc.Block())

        def turns(turn, eng):
            with eng.Fori(0, NB - 1) as b:
                turn(b)
            turn(NB - 1, last=True)

        @block.sync
        def _(sp):
            sp.dma_start(xb[:], x1_dram[0]).then_inc(x1_in, 16)
            sp.dma_start(ident[:], a["c_ident"]).then_inc(consts, 16)
            sp.dma_start(subkeys, a["peer_subkeys"][0].rearrange("h c n d -> n (h c) d")).then_inc(consts, 16)
            sp.dma_start(g2[:], row(a["norm2_g"][0], D)).then_inc(consts, 16)
            sp.wait_ge(S["xn"], 1)
            sp.dma_start(xb[:], x1_dram[1]).then_inc(x1_in, 16)

            def store(b):
                sp.wait_ge(S["s_sb"], b * 2 + 4)
                sp.dma_start(s_dram[b], ss[:]).then_inc(s_out, 16)

            with sp.Fori(0, NB - 2) as b:
                sp.wait_ge(S["xn"], b + 2)
                sp.dma_start(xb[:], x1_dram[b + 2]).then_inc(x1_in, 16)
                store(b)
            store(NB - 2)
            store(NB - 1)
            sp.wait_ge(s_out, NB * 16 + 1)

        @block.vector
        def _(dve):
            dve.wait_ge(consts, 16 * NC)

            def norm(b):
                s = Steps(dve, dve_steps)
                dve.wait_ge(S["ss"], b + 1)
                s.step(nc.vector.tensor_scalar(stat[:, 1:2], stat[:, 0:1], 1.0 / D, EPS, ALU.mult, ALU.add))
                dve.sem_inc(S["ms"], 1)
                dve.wait_ge(S["rs"], b + 1)
                inverse_root(nc, dve, s, stat[:, 2:3], stat[:, 1:2], stat[:, 3:4])
                nc.vector.scalar_tensor_tensor(xn[:], xb[:], stat[:, 2:3], g2[:], ALU.mult, ALU.mult).then_inc(S["xn"], 1)

            def split(b):
                dve.wait_ge(S["h_hi"], b + 1)
                at = bass.ds(b * P, P)
                nc.vector.tensor_tensor(h_lo[:, :, at], bank(H_BANKS, 2, DC), h_hi[:, :, at].bitcast(F32),
                                        ALU.subtract).then_inc(S["h_lo"], 1)

            norm(0)
            split(0)
            with dve.Fori(0, NB - 1) as b:
                dve.sem_clear(dve_steps)
                norm(b + 1)
                split(b + 1)

        @block.scalar
        def _(act):
            act.sem_inc(s_out, 1)
            act.wait_ge(S["skT_ps"], 1)
            for c in range(4):
                done = nc.scalar.copy(skT[:, 4 * c:4 * c + 4, :], bank(c, 1, 4))
            done.then_inc(S["skT"], 1)
            act.sem_inc(S["s_sb"], 2)

            def norm(b):
                s = Steps(act, act_steps)
                act.wait_ge(x1_in, b * 16 + 16)
                nc.scalar.activation(squares[:], xb[:], ACT.Square, accum_out=stat[:, 0:1]).then_inc(S["ss"], 1)
                act.wait_ge(S["ms"], b + 1)
                s.step(nc.scalar.activation(stat[:, 2:3], stat[:, 1:2], ACT.Ln))
                nc.scalar.activation(stat[:, 2:3], stat[:, 2:3], ACT.Exp, scale=-0.5).then_inc(S["rs"], 1)

            def features(b):
                act.wait_ge(S["hT_ps"], b + 1)
                nc.scalar.copy(hT[:], bank(H_BANKS, 2, DC)).then_inc(S["hT"], 1)
                nc.scalar.copy(h_hi[:, :, bass.ds(b * P, P)], bank(H_BANKS, 2, DC)).then_inc(S["h_hi"], 1)

            def q_features(b, j):
                act.wait_ge(S["qT_ps"], b * 2 + j + 1)
                nc.scalar.copy(qT[:, j, :], bank(QT_BANKS, 2)).then_inc(S["qT_sb"], 1)

            def scores(b, j):
                act.wait_ge(S["s_ps"], b * 2 + j + 1)
                nc.scalar.copy(ss[:, j, :], bank(Q_BANKS[j], 2)).then_inc(S["s_sb"], 1)

            def turn(b, last=False):
                if not last:
                    act.sem_clear(act_steps)
                    norm(b + 1)
                for j in range(2):
                    act.wait_ge(S["q_ps"], b * 2 + j + 1)
                    nc.scalar.copy(qq[:, j, :], bank(Q_BANKS[j], 2)).then_inc(S["q_sb"], 1)
                q_features(b, 0)
                if not last:
                    features(b + 1)
                act.wait_ge(s_out, b * 16 + 1)
                scores(b, 0)
                q_features(b, 1)
                scores(b, 1)

            norm(0)
            features(0)
            turns(turn, act)

        @block.tensor
        def _(pe):
            mm, tr = nc.tensor.matmul, nc.tensor.transpose
            pe.wait_ge(consts, 16 * NC)
            for c in range(2 * PH):
                done = tr(bank(c // 4, 1, 4)[:, c % 4, :], subkeys[:, c, :], ident[:])
            done.then_inc(S["skT_ps"], 1)

            def features(b):
                pe.wait_ge(S["xn"], b + 1)
                for c in range(DC):
                    done = tr(bank(H_BANKS, 2, DC)[:, c, :], xn[:, c * P:(c + 1) * P], ident[:])
                done.then_inc(S["hT_ps"], 1)

            def q_features(b, j):
                pe.wait_ge(S["q_sb"], b * 2 + j + 1)
                for c in range(DC):
                    done = tr(bank(QT_BANKS, 2, DC)[:, c, :], qq[:, j, c * P:(c + 1) * P], ident[:])
                done.then_inc(S["qT_ps"], 1)

            def scores(b, j):
                pe.wait_ge(S["qT_sb"], b * 2 + j + 1)
                for c in range(DC):
                    done = mm(bank(Q_BANKS[j], 2, DC)[:, c, :], qT[:, j, c * P:(c + 1) * P], skT[:, j * DC + c, :],
                              start=True, stop=True)
                done.then_inc(S["s_ps"], 1)

            def turn(b, last=False):
                pe.wait_ge(S["hT"], b + 1)
                for j in range(2):
                    pe.wait_ge(S["s_sb"], b * 2 + j + 1)
                    for n in range(2):
                        for c in range(DC):
                            at = (2 * j + n) * 512
                            done = mm(bank(Q_BANKS[j] + n), hT[:, c, :], wq[:, c, at:at + 512], start=(c == 0), stop=(c == DC - 1))
                    done.then_inc(S["q_ps"], 1)
                q_features(b, 0)
                if not last:
                    pe.wait_ge(S["h_lo"], b + 1)
                    features(b + 1)
                scores(b, 0)
                q_features(b, 1)
                scores(b, 1)

            features(0)
            pe.wait_ge(S["skT"], 1)
            pe.wait_ge(wq_in, 16)
            turns(turn, pe)


def choose_phase(nc, a, s_dram, act_dram, g_dram, h_hi, h_lo):
    with ExitStack() as ctx:
        def sb(name, shape, dt=F32):
            return ctx.enter_context(nc.sbuf_tensor("k_" + name, shape, dt))

        def sem(name):
            return ctx.enter_context(nc.semaphore("k_" + name))

        SLOTS = NKEYS // NB
        SET = P // SLOTS
        SPH = HALF // SET
        u_raw = sb("u_raw", [P, 2, D])
        uT_hi = sb("uT_hi", [P, 2, DC, P], F32R)
        uT_lo = sb("uT_lo", [P, 2, DC, P], F32R)
        ga = sb("ga", [P, 2, SEQ])
        ident = sb("ident", [P, P])
        iota = sb("iota", [P, P])
        ss = sb("ss", [P, 2, D])
        v12 = sb("v12", [P, 2, PH, TOPK])
        i12 = sb("i12", [P, 2, PH, TOPK], U32)
        i12f = sb("i12f", [P, 2, PH, TOPK])
        cand = sb("cand", [P, PH, TOPK * TOPK])
        ci = sb("ci", [P, PH, TOPK], U32)
        onehot = sb("onehot", [P, NHK, TOPK])
        zsum = sb("zsum", [P, 2, PH])
        eg = sb("eg", [P, 3, PH, TOPK])
        egT = sb("egT", [P, 3, P])
        oh1 = sb("oh1", [P, 2, SET, P])
        oh2 = sb("oh2", [P, 2, SET, P])
        gs = sb("gs", [P, 2, NKEYS, HALF])
        ps = ctx.enter_context(nc.psum_tensor("k_ps", [P, 8, 512], F32))
        rest = onehot[:].rearrange("p a b -> p (a b)")[:, 0:4 * P].rearrange("p (n w) -> p n w", n=2)

        sc = v12[:, 0]
        c12 = i12
        c12f = cand[:, 0, :].rearrange("p (c h k) -> p c h k", c=2, h=PH)

        def bank(n, k=1, parts=None):
            v = ps[:, n:n + k, :].rearrange("p a b -> p (a b)")
            return v if parts is None else v.rearrange("p (h t) -> p h t", h=parts)

        TPS, UPS, GPS = 0, 2, 6
        names = ("uT_ps uT_hi uT_lo act_ps ga ss_read sx gx eg egT_ps egT oh weighed g_ps gs_sb passed").split()
        S = {n: sem(n) for n in names}
        consts, ss_in = sem("consts"), sem("ss_in")
        u_in, act_out, g_out = ([sem(f"{n}{k}") for k in range(2)] for n in ("u_in", "act_out", "g_out"))
        dve_steps = sem("dve_steps")
        block = ctx.enter_context(nc.Block())

        def turns(turn, eng):
            turn(0, gates=False)
            with eng.Fori(1, NB - 1) as b:
                turn(b)
            turn(NB - 1)
            turn(NB, slices=False)

        @block.sync
        def _(sp):
            for k in range(2):
                sp.sem_inc(act_out[k], 1)
                sp.sem_inc(g_out[k], 1)
            sp.dma_start(ident[:], a["c_ident"]).then_inc(consts, 16)
            sp.dma_start(iota[:], a["c_iota"]).then_inc(consts, 16)

            def store_gates(b, half):
                sp.wait_ge(S["gs_sb"], (b - 1) * SLOTS + (half + 1) * SPH)
                sp.dma_start(g_dram[(b - 1) * 2 + half], gs[:, half]).then_inc(g_out[half], 16)

            def turn(b, gates=True, slices=True):
                for j in range(SLOTS):
                    e = b * SLOTS + j
                    if slices:
                        sp.wait_ge(S["ga"], e + 1)
                        sp.dma_start(act_dram[e], ga[:, j % 2, :]).then_inc(act_out[j % 2], 16)
                    if gates and j == SPH:
                        store_gates(b, 0)
                if gates:
                    store_gates(b, 1)

            turns(turn, sp)
            for k in range(2):
                sp.wait_ge(act_out[k], NKEYS // 2 * 16 + 1)
                sp.wait_ge(g_out[k], NB * 16 + 1)

        @block.gpsimd
        def _(pool):
            u_h = a["peer_u"][0].rearrange("(e p) d -> e p d", p=P)
            for k in range(2):
                pool.dma_start(u_raw[:, k, :], u_h[k]).then_inc(u_in[k], 16)
            pool.dma_start(ss[:], s_dram[0]).then_inc(ss_in, 16)

            def turn(b, last=False):
                for j in range(SLOTS):
                    e = b * SLOTS + j
                    if not (last and j >= SLOTS - 2):
                        pool.wait_ge(S["uT_ps"], e + 1)
                        pool.dma_start(u_raw[:, j % 2, :], u_h[e + 2]).then_inc(u_in[j % 2], 16)
                    if j == PH and not last:
                        pool.wait_ge(S["ss_read"], b + 1)
                        pool.dma_start(ss[:], s_dram[b + 1]).then_inc(ss_in, 16)

            with pool.Fori(0, NB - 1) as b:
                turn(b)
            turn(NB - 1, last=True)

        @block.vector
        def _(dve):
            dve.wait_ge(consts, 32)

            def u_lo(e, k):
                dve.wait_ge(S["uT_hi"], e + 1)
                nc.vector.tensor_tensor(uT_lo[:, k].rearrange("p c t -> p (c t)"), bank(TPS, 2),
                                        uT_hi[:, k].rearrange("p c t -> p (c t)").bitcast(F32),
                                        ALU.subtract).then_inc(S["uT_lo"], 1)

            def rows(b, j):
                if j == 0:
                    dve.wait_ge(S["egT"], b)
                dve.wait_ge(S["g_ps"], (b - 1) * SLOTS + j + 1)
                ts = slice(j * SET, (j + 1) * SET)
                for n, oh in ((1, oh2), (0, oh1)):
                    made = nc.vector.tensor_tensor(
                        oh[:, j % 2], iota[:].unsqueeze(1).broadcast_to([P, SET, P]),
                        egT[:, n, ts].unsqueeze(2).broadcast_to([P, SET, P]), ALU.is_equal)
                made.then_inc(S["oh"], 1)

            def top16(s, pair, width):
                scr = [rest[:, n, 0:width] for n in range(2)]
                first = [s.mark(nc.vector.max(vals[:, 0:8], src)) for src, vals, _ in pair]
                replaced = []
                for n, (src, vals, idx) in enumerate(pair):
                    s.until(first[n])
                    nc.vector.max_index(idx[:, 0:8], vals[:, 0:8], src)
                    replaced.append(s.mark(nc.vector.match_replace(scr[n], vals[:, 0:8], src, NEG)))
                second = []
                for n, (src, vals, idx) in enumerate(pair):
                    s.until(replaced[n])
                    second.append(s.mark(nc.vector.max(vals[:, 8:16], scr[n])))
                for n, (src, vals, idx) in enumerate(pair):
                    s.until(second[n])
                    found = s.mark(nc.vector.max_index(idx[:, 8:16], vals[:, 8:16], scr[n]))
                s.until(found)

            def best_keys(s, h):
                keys = ss[:, h // 4, (h % 4) * 2 * P:((h % 4) * 2 + 2) * P].rearrange("p (c n) -> p c n", c=2)
                top16(s, [(keys[:, c, :], v12[:, c, h, :], i12[:, c, h, :]) for c in range(2)], NKEYS)

            def sums(s):
                s.step(nc.vector.tensor_copy(i12f[:], i12[:]))
                s.step(nc.vector.tensor_tensor(
                    cand[:].rearrange("p h (m n) -> p h m n", m=TOPK),
                    v12[:, 0].unsqueeze(3).broadcast_to([P, PH, TOPK, TOPK]),
                    v12[:, 1].unsqueeze(2).broadcast_to([P, PH, TOPK, TOPK]), ALU.add))

            def best_sums(s, h):
                top16(s, [(cand[:, n, :], sc[:, n, :], ci[:, n, :]) for n in (h, h + 1)], TOPK * TOPK)

            def shifted(s):
                s.step(nc.vector.tensor_tensor(eg[:, 2], sc, sc[:, :, 0:1].broadcast_to([P, PH, TOPK]), ALU.subtract))
                dve.sem_inc(S["sx"], 1)
                nc.vector.tensor_scalar(c12[:, 0], ci[:], 4, None, ALU.logical_shift_right)
                s.step(nc.vector.tensor_scalar(c12[:, 1], ci[:], TOPK - 1, None, ALU.bitwise_and))
                s.step(nc.vector.tensor_copy(c12f, c12[:]))

            def keys_of(s, c):
                s.step(nc.vector.tensor_tensor(
                    onehot[:], c12f[:, c].rearrange("p h k -> p (h k)").unsqueeze(2).broadcast_to([P, NHK, TOPK]),
                    iota[:, 0:TOPK].unsqueeze(1).broadcast_to([P, NHK, TOPK]), ALU.is_equal))
                oh4 = onehot[:].rearrange("p (h k) j -> p h k j", h=PH)
                s.step(nc.vector.tensor_tensor(
                    oh4, oh4, i12f[:, c].unsqueeze(2).broadcast_to([P, PH, TOPK, TOPK]), ALU.mult))
                s.step(nc.vector.reduce_sum(eg[:, c].rearrange("p h k -> p (h k)"), onehot[:], AX_X))

            def normalised(s, b):
                dve.wait_ge(S["gx"], b + 1)
                s.step(nc.vector.reduce_sum(zsum[:, 0, :], eg[:, 2], AX_X))
                s.step(nc.vector.reciprocal(zsum[:, 1, :], zsum[:, 0, :]))
                s.step(nc.vector.tensor_tensor(eg[:, 2], eg[:, 2], zsum[:, 1, :].unsqueeze(2).broadcast_to([P, PH, TOPK]), ALU.mult))
                dve.sem_inc(S["eg"], 1)

            def choose(s, b, j):
                if j == 0:
                    dve.wait_ge(ss_in, b * 16 + 16)
                    dve.sem_inc(S["passed"], 1)
                if j < PH:
                    best_keys(s, j)
                    if j == PH - 1:
                        dve.sem_inc(S["ss_read"], 1)
                elif j == PH:
                    sums(s)
                elif j <= PH + PH // 2:
                    best_sums(s, 2 * (j - PH - 1))
                elif j == PH + PH // 2 + 1:
                    shifted(s)
                    keys_of(s, 0)
                elif j == PH + PH // 2 + 2:
                    keys_of(s, 1)
                elif j == PH + PH // 2 + 3:
                    normalised(s, b)

            def turn(b, gates=True, slices=True):
                if slices:
                    dve.sem_clear(dve_steps)
                s = Steps(dve, dve_steps)
                for j in range(SLOTS):
                    e = b * SLOTS + j
                    if gates:
                        rows(b, j)
                    if slices:
                        if not (isinstance(b, int) and e == NKEYS - 1):
                            u_lo(e + 1, (j + 1) % 2)
                        choose(s, b, j)

            u_lo(0, 0)
            turns(turn, dve)

        @block.scalar
        def _(act):
            def u_hi(e, k):
                act.wait_ge(S["uT_ps"], e + 1)
                act.wait_ge(S["act_ps"], e + 1)
                nc.scalar.copy(uT_hi[:, k].rearrange("p c t -> p (c t)"), bank(TPS, 2)).then_inc(S["uT_hi"], 1)

            def weigh(b, j):
                act.wait_ge(S["oh"], (b - 1) * SLOTS + j + 1)
                for t in range(SET):
                    done = nc.scalar.activation(oh1[:, j % 2, t, :], oh1[:, j % 2, t, :], ACT.Copy,
                                                scale=egT[:, 2, j * SET + t:j * SET + t + 1])
                done.then_inc(S["weighed"], 1)

            def stage(b, j):
                half, at = j // SPH, j % SPH * SET
                if j % SPH == 0:
                    act.wait_ge(g_out[half], (b - 1) * 16 + 1)
                act.wait_ge(S["g_ps"], (b - 1) * SLOTS + j + 3)
                for n in range(2):
                    done = nc.scalar.copy(gs[:, half, :, at + n * 4:at + n * 4 + 4],
                                          bank(GPS + n, 1, 4).rearrange("p t e -> p e t"))
                done.then_inc(S["gs_sb"], 1)

            def turn(b, gates=True, slices=True):
                for j in range(SLOTS):
                    e = b * SLOTS + j
                    if slices and not (isinstance(b, int) and e == NKEYS - 1):
                        u_hi(e + 1, (j + 1) % 2)
                    if gates:
                        if j > 0:
                            stage(b, j - 1)
                        else:
                            act.wait_ge(S["egT_ps"], b)
                            nc.scalar.copy(egT[:], bank(GPS, 1, 4)[:, 0:3, :]).then_inc(S["egT"], 1)
                        weigh(b, j)
                    if slices:
                        if j == PH + PH // 2 + 2:
                            act.wait_ge(S["sx"], b + 1)
                            nc.scalar.activation(eg[:, 2], eg[:, 2], ACT.Exp).then_inc(S["gx"], 1)
                        act.wait_ge(S["act_ps"], e + 3)
                        act.wait_ge(act_out[j % 2], (b * (SLOTS // 2) + j // 2) * 16 + 1)
                        nc.scalar.activation(ga[:, j % 2, :], bank(UPS + 2 * (j % 2), 2), ACT.Gelu).then_inc(S["ga"], 1)
                if gates:
                    stage(b, SLOTS - 1)

            u_hi(0, 0)
            turns(turn, act)

        @block.tensor
        def _(pe):
            mm, tr = nc.tensor.matmul, nc.tensor.transpose
            pe.sem_inc(S["g_ps"], 2)
            pe.sem_inc(S["act_ps"], 2)
            pe.wait_ge(consts, 32)

            def transpose_u(e, k, loads):
                pe.wait_ge(u_in[k], loads * 16 + 16)
                for c in range(DC):
                    last = tr(bank(TPS, 2, DC)[:, c, :], u_raw[:, k, c * P:(c + 1) * P], ident[:])
                last.then_inc(S["uT_ps"], 1)

            def product_h(k, half):
                ts = slice(half * 512, (half + 1) * 512)
                for c in range(DC):
                    for m, (uv, hv) in enumerate(((uT_hi, h_hi), (uT_hi, h_lo), (uT_lo, h_hi))):
                        done = mm(bank(UPS + 2 * k + half), uv[:, k, c, :], hv[:, c, ts],
                                  start=(c == 0 and m == 0), stop=(c == DC - 1 and m == 2))
                return done

            def by_rank(b):
                pe.wait_ge(S["eg"], b)
                if not (isinstance(b, int) and b < 2):
                    pe.wait_ge(S["gs_sb"], (b - 1) * SLOTS)
                for c in range(3):
                    done = tr(bank(GPS, 1, 4)[:, c, :], eg[:, c].rearrange("p h k -> p (h k)"), ident[:])
                done.then_inc(S["egT_ps"], 1)

            def gate_products(b, j):
                pe.wait_ge(S["weighed"], (b - 1) * SLOTS + j + 1)
                if j > 0:
                    pe.wait_ge(S["gs_sb"], (b - 1) * SLOTS + j)
                for t in range(SET):
                    done = mm(bank(GPS + t // 4, 1, 4)[:, t % 4, :], oh2[:, j % 2, t, :], oh1[:, j % 2, t, :], start=True, stop=True)
                done.then_inc(S["g_ps"], 1)

            def turn(b, gates=True, slices=True):
                for j in range(SLOTS):
                    e, k = b * SLOTS + j, j % 2
                    if slices:
                        pe.wait_ge(S["uT_lo"], e + 1)
                        if not (isinstance(b, int) and e == NKEYS - 1):
                            transpose_u(e + 1, 1 - k, b * (SLOTS // 2) + (j + 1) // 2)
                        if not (isinstance(b, int) and e < 2):
                            pe.wait_ge(S["ga"], e - 1)
                        product_h(k, 0)
                    if gates and j == 0:
                        by_rank(b)
                    if slices:
                        product_h(k, 1).then_inc(S["act_ps"], 1)
                    if gates:
                        gate_products(b, j)

            transpose_u(0, 0, 0)
            turns(turn, pe)


def value_phase(nc, a, x1_dram, act_dram, g_dram):
    with ExitStack() as ctx:
        def sb(name, shape, dt=F32):
            return ctx.enter_context(nc.sbuf_tensor("v_" + name, shape, dt))

        def sem(name):
            return ctx.enter_context(nc.semaphore("v_" + name))

        GR = 4
        NGR = NKEYS // GR
        y = sb("y", [P, NB, D])
        v_raw = sb("v_raw", [P, 2, D])
        ga = sb("ga", [P, GR, SEQ])
        g_raw = sb("g_raw", [P, 2, NG, 2, HALF])
        a_hi = sb("a_hi", [P, 2, GR, SEQ], F32R)
        a_lo = sb("a_lo", [P, 2, GR, SEQ], F32R)
        v_hi = sb("v_hi", [P, 2, GR, D], F32R)
        v_lo = sb("v_lo", [P, 2, GR, D], F32R)
        stat = sb("stat", [P, 4, NB])
        ps = ctx.enter_context(nc.psum_tensor("v_ps", [P, 8, 512], F32))
        grow = ga[:, 0, :]
        YS = 4
        x1_in, out_sem, gf_in = sem("x1_in"), sem("out"), sem("gf_in")
        v_in, g_in = ([sem(f"{n}_in{k}") for k in range(2)] for n in "vg")
        a_in = [sem(f"a_in{j}") for j in range(GR)]
        names = "am a_hi a_lo v_hi v_lo y_ps y_ad ss2 ms2 rs2 fin".split()
        S = {n: sem(n) for n in names}
        act_steps, dve_steps = sem("act_steps"), sem("dve_steps")
        block = ctx.enter_context(nc.Block())

        def groups(body, eng):
            for s in range(2):
                body(0, s, first=True)
            with eng.Fori(1, NGR // 2 - 1) as i:
                for s in range(2):
                    body(i, s)
            for s in range(2):
                body(NGR // 2 - 1, s, last=True)

        @block.sync
        def _(sp):
            g_h = g_dram.rearrange("j p e t -> p j e t")

            def body(i, s, first=False, last=False):
                for j in range(GR):
                    e = (i * 2 + s) * GR + j
                    if j % 2 == 0:
                        if not (first and s == 0):
                            sp.wait_ge(S["am"], e - 2)
                        sp.dma_start(g_raw[:, j // 2], g_h[:, :, bass.ds(e, 2), :]).then_inc(g_in[j // 2], 16)
                    if not (first and s == 0):
                        sp.wait_ge(S["a_lo"], e - GR + 1)
                    sp.dma_start(ga[:, j, :], act_dram[e]).then_inc(a_in[j], 16)
                if first and s == 0:
                    sp.dma_start(y[:], x1_dram.rearrange("b p d -> p b d")).then_inc(x1_in, 16)

            groups(body, sp)
            sp.wait_ge(S["a_lo"], NKEYS)
            sp.dma_start(grow, row(a["final_norm_g"], D)).then_inc(gf_in, 16)
            out_h = a["out"][0].rearrange("(b p) d -> b p d", p=P)
            with sp.Fori(0, NB) as b:
                sp.wait_ge(S["fin"], b + 1)
                sp.dma_start(out_h[b], y[:, b, :]).then_inc(out_sem, 16)
            sp.wait_ge(out_sem, 16 * NB)

        @block.gpsimd
        def _(pool):
            v_h = a["peer_v"][0].rearrange("(e p) d -> e p d", p=P)

            def body(i, s, first=False, last=False):
                for j in range(GR):
                    e = (i * 2 + s) * GR + j
                    if not (first and s == 0 and j < 2):
                        pool.wait_ge(S["v_lo"], e - 1)
                    pool.dma_start(v_raw[:, j % 2, :], v_h[e]).then_inc(v_in[j % 2], 16)

            groups(body, pool)

        @block.tensor
        def _(pe):
            def body(i, s, first=False, last=False):
                g = i * 2 + s
                pe.wait_ge(S["a_lo"], g * GR + GR)
                pe.wait_ge(S["v_lo"], g * GR + GR)
                for b in range(NB):
                    if not (first and s == 0 and b < YS):
                        pe.wait_ge(S["y_ad"], g * NB + b - YS + 1)
                    for half in range(2):
                        ds = slice(half * 512, (half + 1) * 512)
                        ts = slice(b * P, (b + 1) * P)
                        for j in range(GR):
                            for m, (av, vv) in enumerate(((a_hi, v_hi), (a_hi, v_lo), (a_lo, v_hi))):
                                done = nc.tensor.matmul(ps[:, 2 * (b % YS) + half, :], av[:, s, j, ts], vv[:, s, j, ds],
                                                        start=(j == 0 and m == 0), stop=(j == GR - 1 and m == 2))
                    done.then_inc(S["y_ps"], 1)

            groups(body, pe)

        @block.scalar
        def _(act):
            def body(i, s, first=False, last=False):
                g = i * 2 + s
                for j in range(GR):
                    e = g * GR + j
                    if j == 0 and not first:
                        act.wait_ge(S["y_ps"], g * NB - NB)
                    act.wait_ge(v_in[j % 2], g * (GR // 2) * 16 + (j // 2) * 16 + 16)
                    nc.scalar.copy(v_hi[:, s, j, :], v_raw[:, j % 2, :]).then_inc(S["v_hi"], 1)
                    act.wait_ge(S["am"], e + 1)
                    nc.scalar.copy(a_hi[:, s, j, :], ga[:, j, :]).then_inc(S["a_hi"], 1)

            groups(body, act)
            st = Steps(act, act_steps)
            act.wait_ge(S["y_ad"], NGR * NB)
            for b in range(NB):
                st.step(nc.scalar.activation(ga[:, 1, :], y[:, b, :], ACT.Square, accum_out=stat[:, 0, b:b + 1]))
            act.sem_inc(S["ss2"], 1)
            act.wait_ge(S["ms2"], 1)
            st.step(nc.scalar.activation(stat[:, 2, :], stat[:, 1, :], ACT.Ln))
            nc.scalar.activation(stat[:, 2, :], stat[:, 2, :], ACT.Exp, scale=-0.5).then_inc(S["rs2"], 1)

        @block.vector
        def _(dve):
            def prepare(i, s, j):
                g = i * 2 + s
                e = g * GR + j
                if j % 2 == 0:
                    dve.wait_ge(g_in[j // 2], g * 16 + 16)
                dve.wait_ge(a_in[j], g * 16 + 16)
                v = ga[:, j, :].rearrange("p (j t) -> p j t", j=NG)
                nc.vector.tensor_tensor(v, v, g_raw[:, j // 2, :, j % 2, :], ALU.mult).then_inc(S["am"], 1)
                dve.wait_ge(S["v_hi"], e + 1)
                nc.vector.tensor_tensor(v_lo[:, s, j, :], v_raw[:, j % 2, :], v_hi[:, s, j, :].bitcast(F32),
                                        ALU.subtract).then_inc(S["v_lo"], 1)

            def rest_of_a(i, s, j):
                e = (i * 2 + s) * GR + j
                dve.wait_ge(S["a_hi"], e + 1)
                nc.vector.tensor_tensor(a_lo[:, s, j, :], ga[:, j, :], a_hi[:, s, j, :].bitcast(F32),
                                        ALU.subtract).then_inc(S["a_lo"], 1)

            def add(g, b):
                dve.wait_ge(S["y_ps"], g * NB + b + 1)
                nc.vector.tensor_tensor(y[:, b, :], y[:, b, :],
                                        ps[:, 2 * (b % YS):2 * (b % YS) + 2, :].rearrange("p a b -> p (a b)"),
                                        ALU.add).then_inc(S["y_ad"], 1)

            def body(i, s, first=False, last=False):
                g = i * 2 + s
                for j in range(GR):
                    prepare(i, s, j)
                    if not (first and s == 0):
                        for b in (2 * j, 2 * j + 1):
                            add(g - 1, b)
                            if b == 2 * j:
                                rest_of_a(i, s, j)
                    else:
                        rest_of_a(i, s, j)
                        if j == 0:
                            dve.wait_ge(x1_in, 16)

            groups(body, dve)
            for b in range(NB):
                add(NGR - 1, b)
            st = Steps(dve, dve_steps)
            dve.wait_ge(S["ss2"], 1)
            st.step(nc.vector.tensor_scalar(stat[:, 1, :], stat[:, 0, :], 1.0 / D, EPS, ALU.mult, ALU.add))
            dve.sem_inc(S["ms2"], 1)
            dve.wait_ge(S["rs2"], 1)
            inverse_root(nc, dve, st, stat[:, 2, :], stat[:, 1, :], stat[:, 3, :])
            dve.wait_ge(gf_in, 16)
            with dve.Fori(0, NB) as b:
                nc.vector.scalar_tensor_tensor(y[:, b, :], y[:, b, :], stat[:, 2, bass.ds(b, 1)], grow,
                                               ALU.mult, ALU.mult).then_inc(S["fin"], 1)


def build(nc, a):
    x1_dram = nc.dram_tensor("x1_scratch", [NB, P, D], F32).ap()
    g_dram = nc.dram_tensor("g_scratch", [NG, P, NKEYS, HALF], F32).ap()
    mix_dram = nc.dram_tensor("mix_scratch", [NB, P, DC, P], F32).ap()
    s_dram = nc.dram_tensor("score_scratch", [NB, P, 2, D], F32).ap()
    act_dram = nc.dram_tensor("act_scratch", [NKEYS, P, SEQ], F32).ap()
    mixer_phase(nc, a, mix_dram)
    with ExitStack() as h_space:
        with nc.sbuf_tensor("wq", [P, DC, PQ], F32, side="right") as wq, nc.semaphore("wq_in") as wq_in:
            output_phase(nc, a, mix_dram, x1_dram, wq, wq_in)
            h_hi, h_lo = (h_space.enter_context(nc.sbuf_tensor(n, [P, DC, SEQ], F32R)) for n in ("h_hi", "h_lo"))
            score_phase(nc, a, x1_dram, s_dram, wq, wq_in, h_hi, h_lo)
        choose_phase(nc, a, s_dram, act_dram, g_dram, h_hi, h_lo)
    value_phase(nc, a, x1_dram, act_dram, g_dram)


def kernel(**inputs):
    import concourse.bacc as bacc
    from concourse.bass_utils import run_bass_kernel_spmd

    nc = bacc.Bacc("TRN2", target_bir_lowering=False, num_devices=1)
    arrays = {name: np.ascontiguousarray(inputs[name]) for name in INPUTS}
    arrays.update(shape_constants())
    a = {name: nc.dram_tensor(name, v.shape, mybir.dt.from_np(v.dtype), kind="ExternalInput").ap()
         for name, v in arrays.items()}
    a["out"] = nc.dram_tensor("out", (1, SEQ, D), F32, kind="ExternalOutput").ap()
    build(nc, a)
    result = run_bass_kernel_spmd(nc, [arrays], core_ids=[0])
    return result.results[0]["out"]
```

```python
from contextlib import ExitStack

import numpy as np
import concourse.bass as bass
from concourse import mybir

P = 128
F32 = mybir.dt.float32
F32R = mybir.dt.float32r
BF16 = mybir.dt.bfloat16
U32 = mybir.dt.uint32
ALU = mybir.AluOpType
ACT = mybir.ActivationFunctionType
AX_X = mybir.AxisListType.X

D = 1024
SEQ = 1024
DC = D // P
NB = SEQ // P
HG = 4
HW = HG * P
SW_HEADS, SW_KV, HD, CHUNK = 8, 2, 64, 64
GROUP = SW_HEADS // SW_KV
IN_COLS = 4 * HW + SW_HEADS * HD + 2 * SW_KV * HD
WIN = 2 * CHUNK
LEVELS = 7
PH, NKEYS, TOPK = 8, 128, 16
PQ = PH * 2 * P
OUT_AT = IN_COLS - D
NHK = PH * TOPK
EPS = 1e-6
LOG_FLOOR = 1e-18
ARG_CAP = 80.0
LN_SCALE = 2.0 ** -52
NEG = -3.0e38
HALF = 64
NG = SEQ // HALF

INPUTS = ["x", "norm1_g", "w_in", "hg_lb_logits", "hg_norm_g", "sw_sinks", "w_out", "norm2_g",
          "peer_wq", "peer_subkeys", "peer_u", "peer_v", "final_norm_g"]


def shape_constants():
    t = np.arange(P)
    ident = np.eye(P, dtype=np.float32)
    upto = (t[:, None] <= t[None, :]).astype(np.float32)
    level = np.zeros((P, LEVELS + 1, P), np.float32)
    for n in range(LEVELS):
        w = P >> (n + 1)
        same = (t[:, None] // (2 * w)) == (t[None, :] // (2 * w))
        level[:, n] = same & ((t[:, None] // w) % 2 == 0) & ((t[None, :] // w) % 2 == 1)
    level[:, LEVELS] = ident
    slopes = 2.0 ** (-8.0 * (np.arange(1, SW_HEADS + 1, dtype=np.float32) / SW_HEADS))
    alibi = np.zeros((P, SW_HEADS, WIN), np.float32)
    q = np.arange(CHUNK)[:, None]
    j = np.arange(WIN)[None, :]
    own_first = np.where(j < CHUNK, np.abs(q - j), q + WIN - j)
    in_order = np.abs(q + CHUNK - j)
    for h in range(SW_HEADS):
        alibi[:CHUNK, h] = -slopes[h] * own_first
        alibi[CHUNK:, h] = -slopes[h] * in_order
    alibi0 = alibi.copy()
    alibi0[:CHUNK, :, CHUNK:] = -1e30
    iota = np.tile(t.astype(np.float32), (P, 1))
    return {"c_ident": ident, "c_upto": upto, "c_level": level, "c_alibi": alibi, "c_alibi0": alibi0,
            "c_iota": iota}


class Steps:

    def __init__(self, eng, sem, per_turn=0, turn=0):
        self.eng, self.sem, self.base, self.n = eng, sem, turn * per_turn, 0

    def mark(self, ins):
        self.n += 1
        ins.then_inc(self.sem, 1)
        return self.n

    def until(self, n):
        self.eng.wait_ge(self.sem, self.base + n)

    def step(self, ins):
        self.until(self.mark(ins))


def row(ap, width):
    return ap.rearrange("(o n) -> o n", o=1).broadcast_to([P, width])


def inverse_root(nc, dve, s, r, x, tmp):
    s.step(nc.vector.tensor_tensor(tmp, r, r, ALU.mult))
    s.step(nc.vector.tensor_tensor(tmp, tmp, x, ALU.mult))
    s.step(nc.vector.tensor_scalar(tmp, tmp, -0.5, 1.5, ALU.mult, ALU.add))
    s.step(nc.vector.tensor_tensor(r, r, tmp, ALU.mult))


def mixer_phase(nc, a, mix_dram, ident, w_in, w_out_in, wq_in, passed):
    with ExitStack() as ctx:
        def sb(name, shape, dt=F32):
            return ctx.enter_context(nc.sbuf_tensor("m_" + name, shape, dt))

        def sem(name):
            return ctx.enter_context(nc.semaphore("m_" + name))

        upto = sb("upto", [P, P])
        level = sb("level", [P, LEVELS + 1, P], BF16)
        alibi = sb("alibi", [P, SW_HEADS, WIN])
        alibi_prev = sb("alibi_prev", [CHUNK, SW_HEADS, CHUNK])
        g1 = sb("g1", [P, D])
        lb2 = sb("lb2", [P, 2, HW])
        hgn = sb("hgn", [P, HW])
        sink = sb("sink", [P, SW_HEADS])
        tiny = sb("tiny", [P, 1])
        unit = sb("unit", [P, 1])
        undo = sb("undo", [P, 1])
        xb = sb("xb", [P, D])
        xn = sb("xn", [P, D])
        stat = sb("stat", [P, 4])
        hT = sb("hT", [P, DC, P])
        qr = sb("qr", [P, HW])
        zr = sb("zr", [P, HW])
        gr = sb("gr", [P, HW])
        ir = sb("ir", [P, HW])
        swq = sb("swq", [P, GROUP, SW_KV, HD])
        swkv = sb("swkv", [P, 2, SW_KV * HD])
        pT = sb("pT", [P, SW_HEADS, P])
        swv = sb("swv", [P, SW_KV * HD])
        swv_mix = sb("swv_mix", [P, SW_KV * HD])
        swqT = sb("swqT", [P, GROUP, P])
        swkT = sb("swkT", [P, P])
        swkT_mix = sb("swkT_mix", [P, P])
        ex = sb("ex", [P, 3, HW])
        kk = sb("kk", [P, HW])
        st_flat = sb("st", [P, SW_HEADS * (WIN + 1)])
        ssum = sb("ssum", [P, 2, SW_HEADS])
        qT = sb("qT", [P, 2, HG, P])
        kT = sb("kT", [P, 2, HG, P])
        bT = sb("bT", [P, 2, HG, P])
        eb = sb("eb", [P, 2, HG, P])
        vv = sb("vv", [P, 2, HW])
        gate = sb("gate", [P, 2, HW])
        dec = sb("dec", [P, 2, LEVELS, P])
        ke = sb("ke", [P, 2, LEVELS, P])
        dlast = sb("dlast", [P, HG, P])
        qb = sb("qb", [P, HG, P])
        kd = sb("kd", [P, HG, P])
        kdT = sb("kdT", [P, HG, P])
        attn = sb("attn", [P, HG, P])
        pick = sb("pick", [P, LEVELS + 1, P])
        oS = sb("oS", [P, HG, P])
        ostat = sb("ostat", [P, 3, HG])
        state = sb("state", [P, HG, P])
        ps = ctx.enter_context(nc.psum_tensor("m_ps", [P, 8, 512], F32))

        st = st_flat[:].rearrange("p (h w) -> p h w", h=SW_HEADS)
        mixS = st_flat[:, 0:HW].rearrange("p (h t) -> p h t", h=HG)
        mixH = oS
        r_qg = pT[:].rearrange("p h t -> p (h t)").rearrange("p (n w) -> p n w", n=2)
        lmax = vv[:, 0, :]
        qs, ff = ex[:, 0, :], ex[:, 2, :]

        def bank(n, k=1, heads=None):
            v = ps[:, n:n + k, :].rearrange("p a b -> p (a b)")
            return v if heads is None else v.rearrange("p (h t) -> p h t", h=heads)

        B_SWQ, B_SWKV, B_Q, B_Z, B_GATE, B_I = 0, 1, 0, 1, 0, 1
        B_SWQT, B_SWKT, B_QT, B_KT, B_CUM, B_OT = 2, 3, 2, 3, 2, 2
        B_SW = B_PT = (2, 3)
        B_LEVELS, B_O, B_ONT, B_KDT, B_U = 6, 4, 4, 5, 5

        consts, x_in = sem("consts"), sem("x_in")
        mix_out = [sem(f"mix_out{n}") for n in range(2)]
        tab, ready, lexp = sem("tab"), sem("ready"), sem("lexp")
        names = ("ss ms rs xn hT_ps hT old q_ps z_ps gate_ps i_ps swq_ps swkv_ps swq swkv qr zr gr ir swT kqT kept mix "
                 "sc e ex f logf qkT qkTs b bS s p pn pT pTs oT oTs Dl E QK KDT kdT hs at O U oS oms ors on onT mixT").split()
        S = {n: sem(n) for n in names}
        act_steps, dve_steps, pool_steps = sem("act_steps"), sem("dve_steps"), sem("pool_steps")
        PARTS = {"swq": (4 * HW, SW_HEADS * HD), "swkv": (4 * HW + SW_HEADS * HD, 2 * SW_KV * HD), "q": (0, HW),
                 "z": (HW, HW), "gate": (3 * HW, HW), "i": (2 * HW, HW)}
        w_part = {n: sem("w_" + n) for n in PARTS}
        tables = sem("tables")
        NCONST = 6

        block = ctx.enter_context(nc.Block())

        def turns(turn, eng):
            turn(-2, 0, second=False, third=False, out=False)
            turn(-1, 1, third=False, out=False)
            turn(0, 0, out=False)
            with eng.Fori(0, (NB - 4) // 2) as i:
                for k in (1, 2):
                    turn(i * 2 + k, k % 2)
            turn(NB - 3, 1, norm=False)
            turn(NB - 2, 0, norm=False, first=False)
            turn(NB - 1, 1, norm=False, first=False, second=False)
            turn(NB, 0, norm=False, first=False, second=False, third=False)

        @block.sync
        def _(sp):
            x_h = a["x"][0].rearrange("(b p) d -> b p d", p=P)
            sp.dma_start(xb[:], x_h[0]).then_inc(x_in, 16)
            sp.dma_start(ident[:], a["c_ident"]).then_inc(tables, 16)
            sp.dma_start(g1[:], row(a["norm1_g"][0], D)).then_inc(tables, 16)
            for k in range(2):
                sp.dma_start(lb2[:, k, :], row(a["hg_lb_logits"][k], HW)).then_inc(tables, 16)
            w_h = a["w_in"][0].rearrange("(c p) n -> p c n", p=P)
            for n, (at, width) in PARTS.items():
                sp.dma_start(w_in[:, :, at:at + width], w_h[:, :, at:at + width]).then_inc(w_part[n], 16)
            sp.dma_start(sink[:], row(a["sw_sinks"][0], SW_HEADS)).then_inc(consts, 16)
            sp.dma_start(alibi[:], a["c_alibi0"]).then_inc(consts, 16)
            sp.dma_start(hgn[:], row(a["hg_norm_g"][0], HW)).then_inc(consts, 16)
            sp.dma_start(upto[:], a["c_upto"]).then_inc(consts, 16)
            sp.dma_start(pick[:], a["c_level"]).then_inc(consts, 16)
            sp.dma_start(alibi_prev[:], a["c_alibi"][0:CHUNK, :, CHUNK:WIN]).then_inc(consts, 16)

            def turn(c, k, norm=True, first=True, second=True, third=True, out=True):
                if norm:
                    sp.wait_ge(S["xn"], c + 3)
                    sp.dma_start(xb[:], x_h[c + 3]).then_inc(x_in, 16)
                if out:
                    sp.wait_ge(S["mixT"], c)
                    sp.dma_start(mix_dram[c - 1, :, :HG, :], mixH[:]).then_inc(mix_out[1], 16)
                if third and not first and second:
                    sp.wait_ge(S["i_ps"], NB)
                    sp.dma_start(w_in[:, :, OUT_AT:OUT_AT + D], a["w_out"][0].rearrange("(c p) n -> p c n", p=P)).then_inc(w_out_in, 16)
                    sp.dma_start(w_in[:, :, 0:OUT_AT], a["peer_wq"][0].rearrange("(c p) n -> p c n", p=P)[:, :, 0:OUT_AT]).then_inc(wq_in, 16)
                if second:
                    sp.wait_ge(S["oTs"], c + 2)
                    sp.dma_start(mix_dram[c + 1, :, HG:, :], mixS).then_inc(mix_out[0], 16)

            turns(turn, sp)
            for n in range(2):
                sp.wait_ge(mix_out[n], NB * 16)

        @block.gpsimd
        def _(pool):
            pool.wait_ge(ready, 1)

            def turn(c, k, norm=True, first=True, second=True, third=True, out=True):
                if not second:
                    return
                n, m = c + 1, 1 - k
                pool.sem_clear(pool_steps)
                s = Steps(pool, pool_steps)
                if not (isinstance(c, int) and c < 0):
                    pool.wait_ge(S["oT"], n)
                    pool.sem_inc(passed, 1)
                s.step(nc.gpsimd.tensor_copy(swv_mix[CHUNK:, :], swv[CHUNK:, :]))
                s.step(nc.gpsimd.tensor_copy(swkT_mix[:, CHUNK:], swkT[:, CHUNK:]))
                pool.sem_inc(S["old"], 1)
                pool.wait_ge(S["swkv"], n + 1)
                pool.sem_inc(passed, 1)
                s.step(nc.gpsimd.tensor_copy(swv[:], swkv[:, 1]))
                s.step(nc.gpsimd.tensor_copy(swv_mix[:CHUNK, :], swkv[:CHUNK, 1]))
                pool.wait_ge(S["ir"], n + 1)
                if not (isinstance(c, int) and c < 1):
                    pool.wait_ge(S["U"], c)
                pool.sem_inc(passed, 1)
                s.step(nc.gpsimd.tensor_copy(vv[:, m], ir[:]))
                pool.sem_inc(S["kept"], 1)
                pool.wait_ge(S["kqT"], n + 1)
                pool.sem_inc(passed, 1)
                nc.gpsimd.tensor_copy(swkT_mix[:, :CHUNK], swkT[:, :CHUNK]).then_inc(S["mix"], 1)

            turns(turn, pool)

        @block.vector
        def _(dve):
            def normed(s, n):
                dve.wait_ge(S["ss"], n + 1)
                s.step(nc.vector.tensor_scalar(stat[:, 1:2], stat[:, 0:1], 1.0 / D, EPS, ALU.mult, ALU.add))
                dve.sem_inc(S["ms"], 1)
                dve.wait_ge(S["rs"], n + 1)
                inverse_root(nc, dve, s, stat[:, 2:3], stat[:, 1:2], stat[:, 3:4])
                nc.vector.scalar_tensor_tensor(xn[:], xb[:], stat[:, 2:3], g1[:], ALU.mult, ALU.mult).then_inc(S["xn"], 1)

            dve.wait_ge(tables, 64)
            s = Steps(dve, dve_steps)
            normed(s, 0)
            s.step(nc.vector.memset(tiny[:], LOG_FLOOR))
            nc.vector.memset(unit[:], LN_SCALE)
            s.step(nc.vector.memset(undo[:], float(np.log(LN_SCALE))))
            nc.vector.memset(state[:], 0.0)
            nc.vector.memset(swv[:], 0.0)
            s.step(nc.vector.memset(swkT[:], 0.0))
            s.step(nc.vector.tensor_tensor(lmax, lb2[:, 0, :], lb2[:, 1, :], ALU.max))
            s.step(nc.vector.tensor_tensor(lb2[:], lb2[:], lmax.unsqueeze(1).broadcast_to([P, 2, HW]), ALU.subtract))
            dve.sem_inc(tab, 1)
            dve.wait_ge(lexp, 1)
            s.step(nc.vector.tensor_tensor(lmax, lb2[:, 0, :], lb2[:, 1, :], ALU.add))
            s.step(nc.vector.reciprocal(lmax, lmax))
            s.step(nc.vector.tensor_tensor(lb2[:], lb2[:], lmax.unsqueeze(1).broadcast_to([P, 2, HW]), ALU.mult))
            lb, omlb = lb2[:, 0, :], lb2[:, 1, :]
            dve.sem_inc(ready, 1)

            def caps(n, first):
                dve.wait_ge(S["ir"], n + 1)
                if not first:
                    dve.wait_ge(S["b"], n)
                nc.vector.tensor_scalar(ex[:, 0, :], qr[:], -ARG_CAP, -1.0, ALU.max, ALU.mult)
                nc.vector.tensor_scalar(ex[:, 1, :], gr[:], -ARG_CAP, -1.0, ALU.max, ALU.mult)
                nc.vector.tensor_scalar(ex[:, 2, :], zr[:], ARG_CAP, None, ALU.min).then_inc(S["e"], 1)

            def sigmoids(s, n, m, first):
                if not first:
                    dve.wait_ge(mix_out[0], n * 16)
                dve.wait_ge(S["ex"], n + 1)
                qg, ez = ex[:, 0:2, :], st_flat[:, 0:HW]
                nc.vector.scalar_tensor_tensor(qg, qg, 1.0, r_qg, ALU.add, ALU.mult)
                s.step(nc.vector.scalar_tensor_tensor(ez, ex[:, 2, :], 1.0, kk[:], ALU.add, ALU.mult))
                nc.vector.scalar_tensor_tensor(qg, qg, 2.0, r_qg, ALU.subtract, ALU.mult)
                s.step(nc.vector.scalar_tensor_tensor(kk[:], ez, 2.0, kk[:], ALU.subtract, ALU.mult))
                s.step(nc.vector.scalar_tensor_tensor(kk[:], kk[:], -1.0, omlb, ALU.mult, ALU.mult))
                nc.vector.scalar_tensor_tensor(qs, qs, -1.0, qr[:], ALU.mult, ALU.mult)
                s.step(nc.vector.tensor_tensor(ff, ff, kk[:], ALU.mult))
                nc.vector.scalar_tensor_tensor(gate[:, m], ex[:, 1, :], -1.0, gr[:], ALU.mult, ALU.mult)
                s.step(nc.vector.tensor_tensor(ff, ff, lb, ALU.add))
                dve.sem_inc(S["f"], 1)
                s.step(nc.vector.tensor_tensor(gate[:, m], gate[:, m], hgn[:], ALU.mult))

            def window_scores(s, n):
                nc.vector.tensor_copy(st[:, :, WIN:WIN + 1], sink[:].unsqueeze(2))
                dve.wait_ge(S["sc"], n + 1)
                for g in range(SW_KV):
                    hs = slice(g * GROUP, (g + 1) * GROUP)
                    s.step(nc.vector.scalar_tensor_tensor(st[:, hs, 0:WIN], bank(B_SW[g], 1, GROUP), HD ** -0.5,
                                                          alibi[:, hs, :], ALU.mult, ALU.add))
                s.step(nc.vector.tensor_copy(alibi[:CHUNK, :, CHUNK:], alibi_prev[:]))
                s.step(nc.vector.reduce_max(ssum[:, 0, :], st, AX_X))
                s.step(nc.vector.tensor_tensor(st, st, ssum[:, 0, :].unsqueeze(2).broadcast_to([P, SW_HEADS, WIN + 1]),
                                               ALU.subtract))
                dve.sem_inc(S["s"], 1)

            def window_probs(s, n):
                dve.wait_ge(S["p"], n + 1)
                s.step(nc.vector.reduce_sum(ssum[:, 0, :], st, AX_X))
                s.step(nc.vector.reciprocal(ssum[:, 1, :], ssum[:, 0, :]))
                s.step(nc.vector.tensor_tensor(st, st, ssum[:, 1, :].unsqueeze(2).broadcast_to([P, SW_HEADS, WIN + 1]),
                                               ALU.mult))
                dve.sem_inc(S["pn"], 1)

            def log_decays(s, b, k, h):
                if h >= 2:
                    dve.wait_ge(S["hs"], b * HG + h - 1)
                if h == 0:
                    dve.wait_ge(S["bS"], b + 1)
                    nc.vector.tensor_tensor(dlast[:], bT[:, k, :, P - 1:P].broadcast_to([P, HG, P]), bT[:, k], ALU.subtract)
                for n in range(LEVELS):
                    w = P >> (n + 1)
                    bv = bT[:, k, h, :].rearrange("p (m w) -> p m w", w=2 * w)
                    dv = dec[:, h % 2, n].rearrange("p (m w) -> p m w", w=2 * w)
                    ref = bv[:, :, w - 1:w].broadcast_to([P, P // (2 * w), w])
                    nc.vector.tensor_tensor(dv[:, :, w:], bv[:, :, w:], ref, ALU.subtract)
                    done = nc.vector.tensor_tensor(dv[:, :, :w], ref, bv[:, :, :w], ALU.subtract)
                done.then_inc(S["Dl"], 1)

            def decayed(s, b, k, h):
                dve.wait_ge(S["E"], b * HG + h + 1)
                if h == 0:
                    nc.vector.tensor_tensor(qb[:], qT[:, k], eb[:, k], ALU.mult)
                    nc.vector.tensor_tensor(kd[:], kT[:, k], dlast[:], ALU.mult)
                d = dec[:, h % 2]
                s.step(nc.vector.tensor_tensor(ke[:, h % 2], d, kT[:, k, h, :].unsqueeze(1).broadcast_to([P, LEVELS, P]), ALU.mult))
                nc.vector.tensor_tensor(d, d, qT[:, k, h, :].unsqueeze(1).broadcast_to([P, LEVELS, P]),
                                        ALU.mult).then_inc(S["QK"], 1)

            def weights(s, b, h):
                dve.wait_ge(S["hs"], b * HG + h + 1)
                s.step(nc.vector.tensor_tensor(pick[:], bank(B_LEVELS, 2, LEVELS + 1), level[:], ALU.mult))
                nc.vector.reduce_sum(attn[:, h, :], pick[:].rearrange("p l t -> p t l"), AX_X).then_inc(S["at"], 1)

            def outputs(s, b, k):
                dve.wait_ge(S["U"], b + 1)
                for h in range(HG):
                    done = nc.vector.scalar_tensor_tensor(state[:, h, :], state[:, h, :], eb[:, k, h, P - 1:P],
                                                          bank(B_U, 1, HG)[:, h, :], ALU.mult, ALU.add)
                s.step(done)
                dve.wait_ge(S["oS"], b + 1)
                sq = pick[:, 0:HG, :]
                s.step(nc.vector.tensor_tensor(sq, oS[:], oS[:], ALU.mult))
                s.step(nc.vector.reduce_sum(ostat[:, 0, :], sq, AX_X))
                s.step(nc.vector.tensor_scalar(ostat[:, 0, :], ostat[:, 0, :], 1.0 / P, EPS, ALU.mult, ALU.add))
                dve.sem_inc(S["oms"], 1)
                s.step(nc.vector.tensor_tensor(oS[:], oS[:], gate[:, k].rearrange("p (h t) -> p h t", h=HG), ALU.mult))
                dve.wait_ge(S["ors"], b + 1)
                inverse_root(nc, dve, s, ostat[:, 1, :], ostat[:, 0, :], ostat[:, 2, :])
                s.step(nc.vector.tensor_tensor(oS[:], oS[:], ostat[:, 1, :].unsqueeze(2).broadcast_to([P, HG, P]), ALU.mult))
                dve.sem_inc(S["on"], 1)

            def turn(c, k, norm=True, first=True, second=True, third=True, out=True):
                n, m = c + 1, 1 - k
                start = isinstance(c, int) and c < 0
                dve.sem_clear(dve_steps)
                s = Steps(dve, dve_steps)
                if start and second:
                    dve.wait_ge(consts, 16 * NCONST)
                    s.step(nc.vector.tensor_copy(level[:], pick[:]))
                if third:
                    log_decays(s, c, k, 0)
                if second:
                    caps(n, start)
                if third:
                    log_decays(s, c, k, 1)
                    decayed(s, c, k, 0)
                    decayed(s, c, k, 1)
                if second:
                    sigmoids(s, n, m, start)
                if third:
                    weights(s, c, 0)
                    log_decays(s, c, k, 2)
                    decayed(s, c, k, 2)
                    weights(s, c, 1)
                    log_decays(s, c, k, 3)
                if second:
                    window_scores(s, n)
                if third:
                    decayed(s, c, k, 3)
                    weights(s, c, 2)
                if norm:
                    normed(s, c + 3)
                if third:
                    weights(s, c, 3)
                if second:
                    window_probs(s, n)
                if third:
                    outputs(s, c, k)

            turns(turn, dve)

        @block.scalar
        def _(act):

            def decays(s, b, h):
                act.wait_ge(S["Dl"], b * HG + h + 1)
                if h == 0:
                    s.step(nc.scalar.activation(dlast[:], dlast[:], ACT.Exp))
                nc.scalar.activation(dec[:, h % 2], dec[:, h % 2], ACT.Exp).then_inc(S["E"], 1)

            def evacuate(to, frm, part, n):
                act.wait_ge(S[part + "_ps"], n + 1)
                return nc.scalar.copy(to, frm)

            def squares(n):
                act.wait_ge(x_in, n * 16 + 16)
                nc.scalar.activation(xn[:], xb[:], ACT.Square, accum_out=stat[:, 0:1]).then_inc(S["ss"], 1)

            def root(s, n):
                act.wait_ge(S["ms"], n + 1)
                s.step(nc.scalar.activation(stat[:, 2:3], stat[:, 1:2], ACT.Ln))
                nc.scalar.activation(stat[:, 2:3], stat[:, 2:3], ACT.Exp, scale=-0.5).then_inc(S["rs"], 1)

            def features(n):
                act.wait_ge(S["hT_ps"], n + 1)
                for c in range(2):
                    done = nc.scalar.copy(hT[:, 4 * c:4 * c + 4, :], bank(c, 1, 4))
                done.then_inc(S["hT"], 1)

            def turn(c, k, norm=True, first=True, second=True, third=True, out=True):
                p, n, m = c + 2, c + 1, 1 - k
                act.sem_clear(act_steps)
                s = Steps(act, act_steps)
                if third:
                    decays(s, c, 0)
                if second:
                    act.wait_ge(S["swT"], n + 1)
                    act.wait_ge(S["old"], n + 1)
                    nc.scalar.copy(swqT[:], bank(B_SWQT, 1, GROUP))
                    nc.scalar.copy(swkT[:], bank(B_SWKT)[:, 0:P]).then_inc(S["kqT"], 1)
                    act.wait_ge(S["e"], n + 1)
                    s.step(nc.scalar.activation(ex[:], ex[:], ACT.Exp))
                    nc.scalar.activation(r_qg, ex[:, 0:2, :], ACT.Ln, bias=unit[:], scale=LN_SCALE)
                    s.step(nc.scalar.activation(kk[:], ex[:, 2, :], ACT.Ln, bias=unit[:], scale=LN_SCALE))
                    nc.scalar.activation(r_qg, r_qg, ACT.Exp, bias=undo[:], scale=-1.0)
                    nc.scalar.activation(kk[:], kk[:], ACT.Exp, bias=undo[:], scale=-1.0).then_inc(S["ex"], 1)
                if third:
                    decays(s, c, 1)
                if out:
                    act.wait_ge(S["onT"], c)
                    nc.scalar.copy(mixH[:], bank(B_ONT, 1, 4)).then_inc(S["mixT"], 1)
                if third:
                    act.wait_ge(S["KDT"], c + 1)
                    nc.scalar.copy(kdT[:], bank(B_KDT, 1, HG)).then_inc(S["kdT"], 1)
                if first:
                    evacuate(swq[:].rearrange("p i g d -> p g i d"),
                             bank(B_SWQ).rearrange("p (g i d) -> p g i d", g=SW_KV, i=GROUP), "swq", p).then_inc(S["swq"], 1)
                    if second:
                        act.wait_ge(S["kept"], n + 1)
                    evacuate(swkv[:].rearrange("p n d -> p (n d)"), bank(B_SWKV)[:, 0:2 * SW_KV * HD], "swkv", p).then_inc(S["swkv"], 1)
                if third:
                    decays(s, c, 2)
                if second:
                    act.wait_ge(S["f"], n + 1)
                    nc.scalar.activation(ff, ff, ACT.Ln, bias=tiny[:]).then_inc(S["logf"], 1)
                if first:
                    evacuate(qr[:], bank(B_Q), "q", p).then_inc(S["qr"], 1)
                if third:
                    decays(s, c, 3)
                if first:
                    evacuate(zr[:], bank(B_Z), "z", p).then_inc(S["zr"], 1)
                if norm:
                    squares(c + 3)
                if second:
                    act.wait_ge(S["s"], n + 1)
                    nc.scalar.activation(st, st, ACT.Exp).then_inc(S["p"], 1)
                    act.wait_ge(S["qkT"], n + 1)
                    nc.scalar.copy(qT[:, m], bank(B_QT, 1, HG))
                    nc.scalar.copy(kT[:, m], bank(B_KT, 1, HG)).then_inc(S["qkTs"], 1)
                if norm:
                    root(s, c + 3)
                if first:
                    evacuate(gr[:], bank(B_GATE), "gate", p).then_inc(S["gr"], 1)
                if second:
                    act.wait_ge(S["b"], n + 1)
                    nc.scalar.copy(bT[:, m], bank(B_CUM, 1, HG))
                    nc.scalar.activation(eb[:, m], bank(B_CUM, 1, HG), ACT.Exp).then_inc(S["bS"], 1)
                if first:
                    evacuate(ir[:], bank(B_I), "i", p).then_inc(S["ir"], 1)
                if third:
                    if out:
                        act.wait_ge(mix_out[1], c * 16)
                    act.wait_ge(S["O"], c + 1)
                    nc.scalar.copy(oS[:], bank(B_O, 1, HG)).then_inc(S["oS"], 1)
                if second:
                    act.wait_ge(S["pT"], n + 1)
                    for g in range(2):
                        done = nc.scalar.copy(pT[:, 4 * g:4 * g + 4, :], bank(B_PT[g], 1, 4))
                    done.then_inc(S["pTs"], 1)
                if norm:
                    features(c + 3)
                if third:
                    act.wait_ge(S["oms"], c + 1)
                    s.step(nc.scalar.activation(ostat[:, 1, :], ostat[:, 0, :], ACT.Ln))
                    nc.scalar.activation(ostat[:, 1, :], ostat[:, 1, :], ACT.Exp, scale=-0.5).then_inc(S["ors"], 1)
                if second:
                    act.wait_ge(S["oT"], n + 1)
                    nc.scalar.copy(mixS, bank(B_OT, 1, 4)).then_inc(S["oTs"], 1)

            squares(0)
            root(Steps(act, act_steps), 0)
            features(0)
            act.wait_ge(tab, 1)
            nc.scalar.activation(lb2[:], lb2[:], ACT.Exp).then_inc(lexp, 1)
            act.wait_ge(ready, 1)
            turns(turn, act)

        @block.tensor
        def _(pe):
            mm, tr = nc.tensor.matmul, nc.tensor.transpose
            pe.wait_ge(tables, 64)

            def project(n, to, part):
                at, width = PARTS[part]
                if isinstance(n, int) and n == 0:
                    pe.wait_ge(w_part[part], 16)
                for c in range(DC):
                    done = mm(bank(to)[:, 0:width], hT[:, c, :], w_in[:, c, at:at + width],
                              start=(c == 0), stop=(c == DC - 1))
                done.then_inc(S[part + "_ps"], 1)

            def level_scores(b, k, h):
                pe.wait_ge(S["QK"], b * HG + h + 1)
                if h == 0:
                    for j in range(HG):
                        done = tr(bank(B_KDT, 1, HG)[:, j, :], kd[:, j, :], ident[:])
                    done.then_inc(S["KDT"], 1)
                else:
                    pe.wait_ge(S["at"], b * HG + h)
                sc = bank(B_LEVELS, 2, LEVELS + 1)
                for n in range(LEVELS):
                    mm(sc[:, n, :], ke[:, h % 2, n, :], dec[:, h % 2, n, :], start=True, stop=True)
                mm(sc[:, LEVELS, :], kT[:, k, h, :], qT[:, k, h, :], start=True, stop=True).then_inc(S["hs"], 1)

            def features(n):
                pe.wait_ge(S["xn"], n + 1)
                for c in range(DC):
                    done = tr(bank(c // 4, 1, 4)[:, c % 4, :], xn[:, c * P:(c + 1) * P], ident[:])
                done.then_inc(S["hT_ps"], 1)

            def turn(c, k, norm=True, first=True, second=True, third=True, out=True):
                p, n, m = c + 2, c + 1, 1 - k
                if second:
                    if isinstance(c, int) and c < 0:
                        pe.wait_ge(consts, 16 * NCONST)
                    else:
                        pe.wait_ge(S["oTs"], n)
                    pe.wait_ge(S["swkv"], n + 1)
                    for i in range(GROUP):
                        tr(bank(B_SWQT, 1, GROUP)[:, i, :], swq[:, i].rearrange("p g d -> p (g d)"), ident[:])
                    tr(bank(B_SWKT)[:, 0:P], swkv[:, 0], ident[:]).then_inc(S["swT"], 1)
                if first:
                    pe.wait_ge(S["hT"], p + 1)
                    project(p, B_SWQ, "swq")
                    project(p, B_SWKV, "swkv")
                if out:
                    pe.wait_ge(S["on"], c)
                    for h in range(HG):
                        done = tr(bank(B_ONT, 1, HG)[:, h, :], oS[:, h, :], ident[:])
                    done.then_inc(S["onT"], 1)
                if third:
                    level_scores(c, k, 0)
                if second:
                    pe.wait_ge(S["kqT"], n + 1)
                    pe.wait_ge(S["mix"], n + 1)
                    pe.sem_inc(passed, 1)
                    for g2 in range(2):
                        keys = swkT_mix if g2 == 0 else swkT
                        for i in range(GROUP):
                            for g in range(SW_KV):
                                done = mm(ps[g2 * CHUNK:(g2 + 1) * CHUNK, B_SW[g], i * WIN:(i + 1) * WIN],
                                          swqT[g * HD:(g + 1) * HD, i, g2 * CHUNK:(g2 + 1) * CHUNK],
                                          keys[g * HD:(g + 1) * HD, :], start=True, stop=True)
                    done.then_inc(S["sc"], 1)
                if first:
                    pe.wait_ge(S["swq"], p + 1)
                    project(p, B_Q, "q")
                if third:
                    level_scores(c, k, 1)
                if first:
                    pe.wait_ge(S["swkv"], p + 1)
                    project(p, B_Z, "z")
                if third:
                    level_scores(c, k, 2)
                if second:
                    pe.wait_ge(S["f"], n + 1)
                    pe.wait_ge(S["s"], n + 1)
                    for h in range(HG):
                        tr(bank(B_QT, 1, HG)[:, h, :], qs[:, h * P:(h + 1) * P], ident[:])
                    for h in range(HG):
                        done = tr(bank(B_KT, 1, HG)[:, h, :], kk[:, h * P:(h + 1) * P], ident[:])
                    done.then_inc(S["qkT"], 1)
                if first:
                    pe.wait_ge(S["qr"], p + 1)
                    project(p, B_GATE, "gate")
                if second:
                    pe.wait_ge(S["logf"], n + 1)
                    pe.wait_ge(S["qkTs"], n + 1)
                    for h in range(HG):
                        done = mm(bank(B_CUM, 1, HG)[:, h, :], ff[:, h * P:(h + 1) * P], upto[:], start=True, stop=True)
                    done.then_inc(S["b"], 1)
                if third:
                    level_scores(c, k, 3)
                if first:
                    pe.wait_ge(S["zr"], p + 1)
                    project(p, B_I, "i")
                if third:
                    pe.wait_ge(S["kdT"], c + 1)
                    pe.wait_ge(S["kept"], c + 1)
                    if out:
                        pe.wait_ge(S["mixT"], c)
                    o = bank(B_O, 1, HG)
                    for h in range(HG):
                        pe.wait_ge(S["at"], c * HG + h + 1)
                        mm(o[:, h, :], attn[:, h, :], vv[:, k, h * P:(h + 1) * P], start=True, stop=False)
                        done = mm(o[:, h, :], qb[:, h, :], state[:, h, :], start=False, stop=True)
                    done.then_inc(S["O"], 1)
                    for h in range(HG):
                        done = mm(bank(B_U, 1, HG)[:, h, :], kdT[:, h, :], vv[:, k, h * P:(h + 1) * P], start=True, stop=True)
                    done.then_inc(S["U"], 1)
                if second:
                    pe.wait_ge(S["pn"], n + 1)
                    pe.wait_ge(S["bS"], n + 1)
                    for h in range(SW_HEADS):
                        done = tr(bank(B_PT[h // 4], 1, 4)[:, h % 4, :], st[:, h, 0:WIN], ident[:])
                    done.then_inc(S["pT"], 1)
                if norm:
                    pe.wait_ge(S["gr"], p + 1)
                    pe.wait_ge(S["ir"], p + 1)
                    features(c + 3)
                if second:
                    pe.wait_ge(S["pTs"], n + 1)
                    for h in range(SW_HEADS):
                        g, half = h // GROUP, (h % 2) * HD
                        for g2 in range(2):
                            vals = swv_mix if g2 == 0 else swv
                            done = mm(ps[half:half + HD, B_OT, (h // 2) * P + g2 * CHUNK:(h // 2) * P + (g2 + 1) * CHUNK],
                                      vals[:, g * HD:(g + 1) * HD], pT[:, h, g2 * CHUNK:(g2 + 1) * CHUNK],
                                      start=True, stop=True)
                    done.then_inc(S["oT"], 1)

            features(0)
            turns(turn, pe)


def output_phase(nc, a, mix_dram, x1_dram, weights, w_out_in, wq_in, qq, g2, score_in):
    with ExitStack() as ctx:
        def sb(name, shape, dt=F32):
            return ctx.enter_context(nc.sbuf_tensor("o_" + name, shape, dt))

        def sem(name):
            return ctx.enter_context(nc.semaphore("o_" + name))

        w_raw = weights[:, :, OUT_AT:OUT_AT + D]
        w_hi = sb("w_hi", [P, DC, D], F32R)
        w_lo = sb("w_lo", [P, DC, D], F32R)
        xb = sb("xb", [P, 2, D])
        mixT = sb("mixT", [P, 2, D])
        m_hi = sb("m_hi", [P, 2, D], F32R)
        m_lo = sb("m_lo", [P, 2, D], F32R)
        ps = ctx.enter_context(nc.psum_tensor("o_ps", [P, 2, 2, 512], F32))
        m_in, x_in, x1_out = ([sem(f"{n}{k}") for k in range(2)] for n in ("m_in", "x_in", "x1_out"))
        S = {n: sem(n) for n in "w_hi w_lo m_hi m_lo out x1 stored".split()}
        block = ctx.enter_context(nc.Block())

        @block.sync
        def _(sp):
            x_h = a["x"][0].rearrange("(b p) d -> b p d", p=P)

            def load(b, k):
                sp.dma_start(mixT[:, k, :], mix_dram[b].rearrange("p c t -> p (c t)")).then_inc(m_in[k], 16)
                sp.dma_start(xb[:, k, :], x_h[b]).then_inc(x_in[k], 16)

            load(0, 0)
            load(1, 1)
            sp.dma_start(qq[:].rearrange("p j d -> p (j d)").rearrange("p (k d) -> p k d", d=P),
                         a["peer_subkeys"][0].rearrange("h c n d -> n (h c) d")).then_inc(score_in, 16)
            sp.dma_start(g2[:], row(a["norm2_g"][0], D)).then_inc(score_in, 16)
            sp.wait_ge(S["w_lo"], DC)
            sp.dma_start(weights[:, :, OUT_AT:PQ], a["peer_wq"][0].rearrange("(c p) n -> p c n", p=P)[:, :, OUT_AT:PQ]).then_inc(wq_in, 16)

            def turn(i, k, last=False):
                b = i * 2 + k
                sp.wait_ge(S["x1"], b + 1)
                sp.dma_start(x1_dram[b], xb[:, k, :]).then_inc(x1_out[k], 16)
                sp.wait_ge(x1_out[k], i * 16 + 16)
                sp.sem_inc(S["stored"], 1)
                if not last:
                    load(b + 2, k)

            with sp.Fori(0, NB // 2 - 1) as i:
                for k in range(2):
                    turn(i, k)
            for k in range(2):
                turn(NB // 2 - 1, k, last=True)

        @block.scalar
        def _(act):
            act.wait_ge(w_out_in, 16)
            act.sem_inc(S["out"], 2)

            def split(i, k):
                act.wait_ge(m_in[k], i * 16 + 16)
                act.wait_ge(S["out"], i * 2 + k + 1)
                nc.scalar.copy(m_hi[:, k, :], mixT[:, k, :]).then_inc(S["m_hi"], 1)

            for c in range(DC):
                nc.scalar.copy(w_hi[:, c, :], w_raw[:, c, :]).then_inc(S["w_hi"], 1)
                if c == 0:
                    split(0, 0)
            split(0, 1)
            with act.Fori(1, NB // 2) as i:
                for k in range(2):
                    split(i, k)

        @block.vector
        def _(dve):
            def split(b, k):
                dve.wait_ge(S["m_hi"], b + 1)
                nc.vector.tensor_tensor(m_lo[:, k, :], mixT[:, k, :], m_hi[:, k, :].bitcast(F32), ALU.subtract).then_inc(S["m_lo"], 1)

            for c in range(DC):
                if c == 1:
                    split(0, 0)
                dve.wait_ge(S["w_hi"], c + 1)
                nc.vector.tensor_tensor(w_lo[:, c, :], w_raw[:, c, :], w_hi[:, c, :].bitcast(F32), ALU.subtract).then_inc(S["w_lo"], 1)

            def add(i, k):
                dve.wait_ge(x_in[k], i * 16 + 16)
                dve.wait_ge(S["out"], i * 2 + k + 3)
                nc.vector.tensor_tensor(xb[:, k, :], xb[:, k, :], ps[:, k].rearrange("p a b -> p (a b)"),
                                        ALU.add).then_inc(S["x1"], 1)

            with dve.Fori(0, NB // 2 - 1) as i:
                for k in range(2):
                    split(i * 2 + k + 1, 1 - k)
                    add(i, k)
            split(NB - 1, 1)
            add(NB // 2 - 1, 0)
            add(NB // 2 - 1, 1)

        @block.tensor
        def _(pe):
            def turn(b, k, first=False):
                pe.wait_ge(S["m_lo"], b + 1)
                if not first:
                    pe.wait_ge(S["x1"], b - 1)
                for half in range(2):
                    for c in range(DC):
                        if isinstance(b, int) and b == 0 and half == 0:
                            pe.wait_ge(S["w_lo"], c + 1)
                        for m, (mv, wv) in enumerate(((m_hi, w_hi), (m_hi, w_lo), (m_lo, w_hi))):
                            done = nc.tensor.matmul(ps[:, k, half, :], mv[:, k, c * P:(c + 1) * P],
                                                    wv[:, c, half * 512:(half + 1) * 512],
                                                    start=(c == 0 and m == 0), stop=(c == DC - 1 and m == 2))
                done.then_inc(S["out"], 1)

            turn(0, 0, first=True)
            turn(1, 1, first=True)
            with pe.Fori(1, NB // 2) as i:
                for k in range(2):
                    turn(i * 2 + k, k)


def score_phase(nc, a, x1_dram, s_dram, ident, weights, wq_in, qq, g2, score_in, h_hi, h_lo, u_raw, u_in):
    with ExitStack() as ctx:
        def sb(name, shape, dt=F32):
            return ctx.enter_context(nc.sbuf_tensor("s_" + name, shape, dt))

        def sem(name):
            return ctx.enter_context(nc.semaphore("s_" + name))

        skT = sb("skT", [P, 2 * PH, NKEYS])
        wq = weights[:, :, 0:PQ]
        hT = weights[:, :, PQ:PQ + P]
        qT = [weights[:, :, PQ + (j + 1) * P:PQ + (j + 2) * P] for j in range(2)]
        xb = sb("xb", [P, D])
        xn = sb("xn", [P, D])
        squares = sb("squares", [P, D])
        stat = sb("stat", [P, 4])
        ss = sb("ss", [P, 2, D])
        ps = ctx.enter_context(nc.psum_tensor("s_ps", [P, 8, 512], F32))
        subkeys = qq[:].rearrange("p j d -> p (j d)").rearrange("p (k d) -> p k d", d=P)

        def bank(n, k=1, parts=None):
            v = ps[:, n:n + k, :].rearrange("p a b -> p (a b)")
            return v if parts is None else v.rearrange("p (h t) -> p h t", h=parts)

        Q_BANKS, H_BANKS, QT_BANKS = (0, 2), 4, 6
        names = "ss ms rs xn hT_ps hT h_hi h_lo q_ps q_sb qT_ps qT_sb s_ps s_sb skT_ps skT".split()
        S = {n: sem(n) for n in names}
        x1_in, s_out = sem("x1_in"), sem("s_out")
        act_steps, dve_steps = sem("act_steps"), sem("dve_steps")
        block = ctx.enter_context(nc.Block())

        def turns(turn, eng):
            with eng.Fori(0, NB - 1) as b:
                turn(b)
            turn(NB - 1, last=True)

        @block.sync
        def _(sp):
            sp.dma_start(xb[:], x1_dram[0]).then_inc(x1_in, 16)
            sp.wait_ge(S["xn"], 1)
            sp.dma_start(xb[:], x1_dram[1]).then_inc(x1_in, 16)

            def store(b):
                sp.wait_ge(S["s_sb"], b * 2 + 4)
                sp.dma_start(s_dram[b], ss[:]).then_inc(s_out, 16)

            with sp.Fori(0, NB - 2) as b:
                sp.wait_ge(S["xn"], b + 2)
                sp.dma_start(xb[:], x1_dram[b + 2]).then_inc(x1_in, 16)
                store(b)
            store(NB - 2)
            store(NB - 1)
            sp.wait_ge(s_out, NB * 16 + 1)

        @block.gpsimd
        def _(pool):
            for k in range(2):
                pool.dma_start(u_raw[:, k, :], a["peer_u"][0].rearrange("(e p) d -> e p d", p=P)[k]).then_inc(u_in[k], 16)

        @block.vector
        def _(dve):
            dve.wait_ge(score_in, 32)

            def norm(b):
                s = Steps(dve, dve_steps)
                dve.wait_ge(S["ss"], b + 1)
                s.step(nc.vector.tensor_scalar(stat[:, 1:2], stat[:, 0:1], 1.0 / D, EPS, ALU.mult, ALU.add))
                dve.sem_inc(S["ms"], 1)
                dve.wait_ge(S["rs"], b + 1)
                inverse_root(nc, dve, s, stat[:, 2:3], stat[:, 1:2], stat[:, 3:4])
                nc.vector.scalar_tensor_tensor(xn[:], xb[:], stat[:, 2:3], g2[:], ALU.mult, ALU.mult).then_inc(S["xn"], 1)

            def split(b):
                dve.wait_ge(S["h_hi"], b + 1)
                at = bass.ds(b * P, P)
                nc.vector.tensor_tensor(h_lo[:, :, at], bank(H_BANKS, 2, DC), h_hi[:, :, at].bitcast(F32),
                                        ALU.subtract).then_inc(S["h_lo"], 1)

            norm(0)
            split(0)
            with dve.Fori(0, NB - 1) as b:
                dve.sem_clear(dve_steps)
                norm(b + 1)
                split(b + 1)

        @block.scalar
        def _(act):
            act.sem_inc(s_out, 1)
            act.wait_ge(S["skT_ps"], 1)
            for c in range(4):
                done = nc.scalar.copy(skT[:, 4 * c:4 * c + 4, :], bank(c, 1, 4))
            done.then_inc(S["skT"], 1)
            act.sem_inc(S["s_sb"], 2)

            def norm(b):
                s = Steps(act, act_steps)
                act.wait_ge(x1_in, b * 16 + 16)
                nc.scalar.activation(squares[:], xb[:], ACT.Square, accum_out=stat[:, 0:1]).then_inc(S["ss"], 1)
                act.wait_ge(S["ms"], b + 1)
                s.step(nc.scalar.activation(stat[:, 2:3], stat[:, 1:2], ACT.Ln))
                nc.scalar.activation(stat[:, 2:3], stat[:, 2:3], ACT.Exp, scale=-0.5).then_inc(S["rs"], 1)

            def features(b):
                act.wait_ge(S["hT_ps"], b + 1)
                nc.scalar.copy(hT, bank(H_BANKS, 2, DC)).then_inc(S["hT"], 1)
                nc.scalar.copy(h_hi[:, :, bass.ds(b * P, P)], bank(H_BANKS, 2, DC)).then_inc(S["h_hi"], 1)

            def q_features(b, j):
                act.wait_ge(S["qT_ps"], b * 2 + j + 1)
                nc.scalar.copy(qT[j], bank(QT_BANKS, 2, DC)).then_inc(S["qT_sb"], 1)

            def scores(b, j):
                act.wait_ge(S["s_ps"], b * 2 + j + 1)
                nc.scalar.copy(ss[:, j, :], bank(Q_BANKS[j], 2)).then_inc(S["s_sb"], 1)

            def turn(b, last=False):
                if not last:
                    act.sem_clear(act_steps)
                    norm(b + 1)
                for j in range(2):
                    act.wait_ge(S["q_ps"], b * 2 + j + 1)
                    nc.scalar.copy(qq[:, j, :], bank(Q_BANKS[j], 2)).then_inc(S["q_sb"], 1)
                q_features(b, 0)
                if not last:
                    features(b + 1)
                act.wait_ge(s_out, b * 16 + 1)
                scores(b, 0)
                q_features(b, 1)
                scores(b, 1)

            norm(0)
            features(0)
            turns(turn, act)

        @block.tensor
        def _(pe):
            mm, tr = nc.tensor.matmul, nc.tensor.transpose
            pe.wait_ge(score_in, 32)
            for c in range(2 * PH):
                done = tr(bank(c // 4, 1, 4)[:, c % 4, :], subkeys[:, c, :], ident[:])
            done.then_inc(S["skT_ps"], 1)

            def features(b):
                pe.wait_ge(S["xn"], b + 1)
                for c in range(DC):
                    done = tr(bank(H_BANKS, 2, DC)[:, c, :], xn[:, c * P:(c + 1) * P], ident[:])
                done.then_inc(S["hT_ps"], 1)

            def q_features(b, j):
                pe.wait_ge(S["q_sb"], b * 2 + j + 1)
                for c in range(DC):
                    done = tr(bank(QT_BANKS, 2, DC)[:, c, :], qq[:, j, c * P:(c + 1) * P], ident[:])
                done.then_inc(S["qT_ps"], 1)

            def scores(b, j):
                pe.wait_ge(S["qT_sb"], b * 2 + j + 1)
                for c in range(DC):
                    done = mm(bank(Q_BANKS[j], 2, DC)[:, c, :], qT[j][:, c, :], skT[:, j * DC + c, :],
                              start=True, stop=True)
                done.then_inc(S["s_ps"], 1)

            def turn(b, last=False):
                pe.wait_ge(S["hT"], b + 1)
                for j in range(2):
                    pe.wait_ge(S["s_sb"], b * 2 + j + 1)
                    for n in range(2):
                        for c in range(DC):
                            at = (2 * j + n) * 512
                            done = mm(bank(Q_BANKS[j] + n), hT[:, c, :], wq[:, c, at:at + 512], start=(c == 0), stop=(c == DC - 1))
                    done.then_inc(S["q_ps"], 1)
                q_features(b, 0)
                if not last:
                    pe.wait_ge(S["h_lo"], b + 1)
                    features(b + 1)
                scores(b, 0)
                q_features(b, 1)
                scores(b, 1)

            features(0)
            pe.wait_ge(S["skT"], 1)
            pe.wait_ge(wq_in, 32)
            turns(turn, pe)


def choose_phase(nc, a, s_dram, act_dram, g_dram, ident, h_hi, h_lo, u_raw, u_in, passed):
    with ExitStack() as ctx:
        def sb(name, shape, dt=F32):
            return ctx.enter_context(nc.sbuf_tensor("k_" + name, shape, dt))

        def sem(name):
            return ctx.enter_context(nc.semaphore("k_" + name))

        SLOTS = NKEYS // NB
        SET = P // SLOTS
        SPH = HALF // SET
        START = 10
        STORED = SLOTS // 2
        uT_hi = sb("uT_hi", [P, 2, DC, P], F32R)
        uT_lo = sb("uT_lo", [P, 2, DC, P], F32R)
        ga = sb("ga", [P, 2, SEQ])
        iota = sb("iota", [P, P])
        ss = sb("ss", [P, 2, D])
        v12 = sb("v12", [P, 2, PH, TOPK])
        i12 = sb("i12", [P, 2, PH, TOPK], U32)
        i12f = sb("i12f", [P, 2, PH, TOPK])
        cand = sb("cand", [P, PH, TOPK * TOPK])
        onehot = sb("onehot", [P, NHK, TOPK])
        zsum = sb("zsum", [P, 2, PH])
        eg = sb("eg", [P, 3, PH, TOPK])
        egT = sb("egT", [P, 3, P])
        g_hi = sb("g_hi", [P, P], F32R)
        oh1 = sb("oh1", [P, SET, P])
        oh2 = sb("oh2", [P, SET, P], F32R)
        w_hi = sb("w_hi", [P, SET, P], F32R)
        w_lo = sb("w_lo", [P, SET, P], F32R)
        gs = sb("gs", [P, 2, NKEYS, HALF])
        ps = ctx.enter_context(nc.psum_tensor("k_ps", [P, 8, 512], F32))
        rest = onehot[:].rearrange("p a b -> p (a b)")[:, 0:4 * P].rearrange("p (n w) -> p n w", n=2)

        sc, ci = v12[:, 0], v12[:, 1].bitcast(U32)
        c12 = i12
        c12f = cand[:, 0, :].rearrange("p (c h k) -> p c h k", c=2, h=PH)

        def bank(n, k=1, parts=None):
            v = ps[:, n:n + k, :].rearrange("p a b -> p (a b)")
            return v if parts is None else v.rearrange("p (h t) -> p h t", h=parts)

        TPS, UPS, GPS = 0, 2, 6
        names = ("uT_ps uT_hi uT_lo act_ps ga ss_read sx gx eg egT_ps egT oh w_hi w_lo g_ps gs_sb").split()
        S = {n: sem(n) for n in names}
        consts, ss_in = sem("consts"), sem("ss_in")
        act_out, g_out = ([sem(f"{n}{k}") for k in range(2)] for n in ("act_out", "g_out"))
        dve_steps = sem("dve_steps")
        block = ctx.enter_context(nc.Block())

        def turns(turn, eng):
            turn(0)
            with eng.Fori(1, NB - 1) as b:
                turn(b)
            turn(NB - 1)
            turn(NB)

        def plan(b):
            if isinstance(b, int) and b == 0:
                return [(START + n, parts, ()) for n, parts in
                        enumerate(((0, 1, 2), (3, 4, 5), (6, 7, 8), (9, 10, 11), (12, 13), (14, 15)))]
            if isinstance(b, int) and b == NB:
                return [(j, (), (2 * j, 2 * j + 1) if j < STORED else ()) for j in range(START)]
            return [(j, (j,), (j,)) for j in range(SLOTS)]

        def slice_of(b, j):
            return b * SLOTS + (j - START)

        def is_last(e):
            return isinstance(e, int) and e == NKEYS - 1

        @block.sync
        def _(sp):
            for k in range(2):
                sp.sem_inc(act_out[k], 1)
                sp.sem_inc(g_out[k], 1)
            sp.dma_start(iota[:], a["c_iota"]).then_inc(consts, 16)

            def store_gates(b, half):
                sp.wait_ge(S["gs_sb"], (b - 1) * SLOTS + (half + 1) * SPH)
                sp.dma_start(g_dram[(b - 1) * 2 + half], gs[:, half]).then_inc(g_out[half], 16)

            def turn(b):
                for j, _, sets in plan(b):
                    e = slice_of(b, j)
                    sp.wait_ge(S["ga"], e + 1)
                    sp.dma_start(act_dram[e], ga[:, j % 2, :]).then_inc(act_out[j % 2], 16)
                    if SPH in sets:
                        store_gates(b, 0)
                    if j == STORED and isinstance(b, int) and b == NB:
                        store_gates(b, 1)
                if sets:
                    store_gates(b, 1)

            turns(turn, sp)
            for k in range(2):
                sp.wait_ge(act_out[k], NKEYS // 2 * 16 + 1)
                sp.wait_ge(g_out[k], NB * 16 + 1)

        @block.gpsimd
        def _(pool):
            u_h = a["peer_u"][0].rearrange("(e p) d -> e p d", p=P)
            pool.dma_start(ss[:], s_dram[0]).then_inc(ss_in, 16)

            def weigh(b, j):
                pool.wait_ge(S["oh"], (b - 1) * SLOTS + j + 1)
                rests = egT[:, 2, j * SET:(j + 1) * SET]
                nc.gpsimd.tensor_tensor(w_lo[:], oh1[:], rests.unsqueeze(2).broadcast_to([P, SET, P]),
                                        ALU.mult).then_inc(S["w_lo"], 1)

            def turn(b):
                for j, parts, sets in plan(b):
                    e = slice_of(b, j)
                    if not (isinstance(e, int) and e + 2 >= NKEYS):
                        pool.wait_ge(S["uT_ps"], e + 1)
                        pool.dma_start(u_raw[:, j % 2, :], u_h[e + 2]).then_inc(u_in[j % 2], 16)
                    if PH in parts and not (isinstance(b, int) and b == NB - 1):
                        pool.wait_ge(S["ss_read"], b + 1)
                        pool.dma_start(ss[:], s_dram[b + 1]).then_inc(ss_in, 16)
                    for n in sets:
                        weigh(b, n)

            turns(turn, pool)

        @block.vector
        def _(dve):
            dve.wait_ge(consts, 16)

            def u_lo(e, k):
                dve.wait_ge(S["uT_hi"], e + 1)
                nc.vector.tensor_tensor(uT_lo[:, k].rearrange("p c t -> p (c t)"), bank(TPS, 2),
                                        uT_hi[:, k].rearrange("p c t -> p (c t)").bitcast(F32),
                                        ALU.subtract).then_inc(S["uT_lo"], 1)

            def rows(b, j):
                if j == 0:
                    dve.wait_ge(S["egT"], b)
                    nc.vector.tensor_tensor(egT[:, 2], bank(GPS, 1, 4)[:, 2, :], g_hi[:].bitcast(F32), ALU.subtract)
                dve.wait_ge(S["g_ps"], (b - 1) * SLOTS + j + 1)
                ts = slice(j * SET, (j + 1) * SET)
                for n, oh in ((1, oh2), (0, oh1)):
                    made = nc.vector.tensor_tensor(
                        oh[:], iota[:].unsqueeze(1).broadcast_to([P, SET, P]),
                        egT[:, n, ts].unsqueeze(2).broadcast_to([P, SET, P]), ALU.is_equal)
                made.then_inc(S["oh"], 1)

            def top16(s, pair, width):
                scr = [rest[:, n, 0:width] for n in range(2)]
                first = [s.mark(nc.vector.max(vals[:, 0:8], src)) for src, vals, _ in pair]
                replaced = []
                for n, (src, vals, idx) in enumerate(pair):
                    s.until(first[n])
                    nc.vector.max_index(idx[:, 0:8], vals[:, 0:8], src)
                    replaced.append(s.mark(nc.vector.match_replace(scr[n], vals[:, 0:8], src, NEG)))
                second = []
                for n, (src, vals, idx) in enumerate(pair):
                    s.until(replaced[n])
                    second.append(s.mark(nc.vector.max(vals[:, 8:16], scr[n])))
                for n, (src, vals, idx) in enumerate(pair):
                    s.until(second[n])
                    found = s.mark(nc.vector.max_index(idx[:, 8:16], vals[:, 8:16], scr[n]))
                s.until(found)

            def best_keys(s, h):
                keys = ss[:, h // 4, (h % 4) * 2 * P:((h % 4) * 2 + 2) * P].rearrange("p (c n) -> p c n", c=2)
                top16(s, [(keys[:, c, :], v12[:, c, h, :], i12[:, c, h, :]) for c in range(2)], NKEYS)

            def sums(s):
                s.step(nc.vector.tensor_copy(i12f[:], i12[:]))
                s.step(nc.vector.tensor_tensor(
                    cand[:].rearrange("p h (m n) -> p h m n", m=TOPK),
                    v12[:, 0].unsqueeze(3).broadcast_to([P, PH, TOPK, TOPK]),
                    v12[:, 1].unsqueeze(2).broadcast_to([P, PH, TOPK, TOPK]), ALU.add))

            def best_sums(s, h):
                top16(s, [(cand[:, n, :], sc[:, n, :], ci[:, n, :]) for n in (h, h + 1)], TOPK * TOPK)

            def shifted(s):
                s.step(nc.vector.tensor_tensor(eg[:, 2], sc, sc[:, :, 0:1].broadcast_to([P, PH, TOPK]), ALU.subtract))
                dve.sem_inc(S["sx"], 1)
                nc.vector.tensor_scalar(c12[:, 0], ci, 4, None, ALU.logical_shift_right)
                s.step(nc.vector.tensor_scalar(c12[:, 1], ci, TOPK - 1, None, ALU.bitwise_and))
                s.step(nc.vector.tensor_copy(c12f, c12[:]))

            def keys_of(s, c):
                s.step(nc.vector.tensor_tensor(
                    onehot[:], c12f[:, c].rearrange("p h k -> p (h k)").unsqueeze(2).broadcast_to([P, NHK, TOPK]),
                    iota[:, 0:TOPK].unsqueeze(1).broadcast_to([P, NHK, TOPK]), ALU.is_equal))
                oh4 = onehot[:].rearrange("p (h k) j -> p h k j", h=PH)
                s.step(nc.vector.tensor_tensor(
                    oh4, oh4, i12f[:, c].unsqueeze(2).broadcast_to([P, PH, TOPK, TOPK]), ALU.mult))
                s.step(nc.vector.reduce_sum(eg[:, c].rearrange("p h k -> p (h k)"), onehot[:], AX_X))

            def normalised(s, b):
                dve.wait_ge(S["gx"], b + 1)
                s.step(nc.vector.reduce_sum(zsum[:, 0, :], eg[:, 2], AX_X))
                s.step(nc.vector.reciprocal(zsum[:, 1, :], zsum[:, 0, :]))
                s.step(nc.vector.tensor_tensor(eg[:, 2], eg[:, 2], zsum[:, 1, :].unsqueeze(2).broadcast_to([P, PH, TOPK]), ALU.mult))
                dve.sem_inc(S["eg"], 1)

            def choose(s, b, j):
                if j == 0:
                    dve.wait_ge(ss_in, b * 16 + 16)
                    dve.sem_inc(passed, 1)
                if j < PH:
                    best_keys(s, j)
                    if j == PH - 1:
                        dve.sem_inc(S["ss_read"], 1)
                elif j == PH:
                    sums(s)
                elif j <= PH + PH // 2:
                    best_sums(s, 2 * (j - PH - 1))
                elif j == PH + PH // 2 + 1:
                    shifted(s)
                    keys_of(s, 0)
                elif j == PH + PH // 2 + 2:
                    keys_of(s, 1)
                elif j == PH + PH // 2 + 3:
                    normalised(s, b)

            def turn(b):
                dve.sem_clear(dve_steps)
                s = Steps(dve, dve_steps)
                for j, parts, sets in plan(b):
                    e = slice_of(b, j)
                    for n in sets:
                        rows(b, n)
                        if n == sets[0] and not is_last(e):
                            u_lo(e + 1, (j + 1) % 2)
                    if not sets and not is_last(e):
                        u_lo(e + 1, (j + 1) % 2)
                    for n in parts:
                        choose(s, b, n)

            u_lo(0, 0)
            turns(turn, dve)

        @block.scalar
        def _(act):
            def u_hi(e, k):
                act.wait_ge(S["uT_ps"], e + 1)
                act.wait_ge(S["act_ps"], e + 1)
                nc.scalar.copy(uT_hi[:, k].rearrange("p c t -> p (c t)"), bank(TPS, 2)).then_inc(S["uT_hi"], 1)

            def weigh(b, j):
                act.wait_ge(S["oh"], (b - 1) * SLOTS + j + 1)
                for t in range(SET):
                    done = nc.scalar.activation(w_hi[:, t, :], oh1[:, t, :], ACT.Copy,
                                                scale=g_hi[:, j * SET + t:j * SET + t + 1].bitcast(F32))
                done.then_inc(S["w_hi"], 1)

            def stage(b, j):
                half, at = j // SPH, j % SPH * SET
                if j % SPH == 0:
                    act.wait_ge(g_out[half], (b - 1) * 16 + 1)
                act.wait_ge(S["g_ps"], (b - 1) * SLOTS + j + 2)
                for n in range(2):
                    done = nc.scalar.copy(gs[:, half, :, at + n * 4:at + n * 4 + 4],
                                          bank(GPS + n, 1, 4).rearrange("p t e -> p e t"))
                done.then_inc(S["gs_sb"], 1)

            def turn(b):
                for j, parts, sets in plan(b):
                    e = slice_of(b, j)
                    if not is_last(e):
                        u_hi(e + 1, (j + 1) % 2)
                    for n in sets:
                        if n > 0:
                            stage(b, n - 1)
                        else:
                            act.wait_ge(S["egT_ps"], b)
                            nc.scalar.copy(egT[:, 0:2], bank(GPS, 1, 4)[:, 0:2, :])
                            nc.scalar.copy(g_hi[:], bank(GPS, 1, 4)[:, 2, :]).then_inc(S["egT"], 1)
                        weigh(b, n)
                    if j == STORED and isinstance(b, int) and b == NB:
                        stage(b, SLOTS - 1)
                    if SLOTS - 2 in parts:
                        act.wait_ge(S["sx"], b + 1)
                        nc.scalar.activation(eg[:, 2], eg[:, 2], ACT.Exp).then_inc(S["gx"], 1)
                    act.wait_ge(S["act_ps"], e + 3)
                    act.wait_ge(act_out[j % 2], (b * (SLOTS // 2) + (j - START) // 2) * 16 + 1)
                    nc.scalar.activation(ga[:, j % 2, :], bank(UPS + 2 * (j % 2), 2), ACT.Gelu).then_inc(S["ga"], 1)
                if sets:
                    stage(b, SLOTS - 1)

            u_hi(0, 0)
            turns(turn, act)

        @block.tensor
        def _(pe):
            mm, tr = nc.tensor.matmul, nc.tensor.transpose
            pe.sem_inc(S["g_ps"], 1)
            pe.sem_inc(S["act_ps"], 2)

            def transpose_u(e, k, loads):
                pe.wait_ge(u_in[k], loads * 16 + 16)
                for c in range(DC):
                    last = tr(bank(TPS, 2, DC)[:, c, :], u_raw[:, k, c * P:(c + 1) * P], ident[:])
                last.then_inc(S["uT_ps"], 1)

            def product_h(k, half):
                ts = slice(half * 512, (half + 1) * 512)
                for c in range(DC):
                    for m, (uv, hv) in enumerate(((uT_hi, h_hi), (uT_hi, h_lo), (uT_lo, h_hi))):
                        done = mm(bank(UPS + 2 * k + half), uv[:, k, c, :], hv[:, c, ts],
                                  start=(c == 0 and m == 0), stop=(c == DC - 1 and m == 2))
                return done

            def by_rank(b):
                pe.wait_ge(S["eg"], b)
                if not (isinstance(b, int) and b < 2):
                    pe.wait_ge(S["gs_sb"], (b - 1) * SLOTS)
                for c in range(3):
                    done = tr(bank(GPS, 1, 4)[:, c, :], eg[:, c].rearrange("p h k -> p (h k)"), ident[:])
                done.then_inc(S["egT_ps"], 1)

            def gate_products(b, j):
                pe.wait_ge(S["w_hi"], (b - 1) * SLOTS + j + 1)
                pe.wait_ge(S["w_lo"], (b - 1) * SLOTS + j + 1)
                if j > 0:
                    pe.wait_ge(S["gs_sb"], (b - 1) * SLOTS + j)
                for t in range(SET):
                    out = bank(GPS + t // 4, 1, 4)[:, t % 4, :]
                    mm(out, oh2[:, t, :], w_hi[:, t, :], start=True, stop=False)
                    done = mm(out, oh2[:, t, :], w_lo[:, t, :], start=False, stop=True)
                done.then_inc(S["g_ps"], 1)

            def turn(b):
                last = isinstance(b, int) and b == NB
                for j, _, sets in plan(b):
                    e, k = slice_of(b, j), j % 2
                    pe.wait_ge(S["uT_lo"], e + 1)
                    if not is_last(e):
                        transpose_u(e + 1, 1 - k, b * (SLOTS // 2) + (j + 1 - START) // 2)
                    if not (isinstance(e, int) and e < 2):
                        pe.wait_ge(S["ga"], e - 1)
                    if 0 in sets and last:
                        by_rank(b)
                    product_h(k, 0)
                    if last and sets:
                        gate_products(b, sets[0])
                    elif 0 in sets:
                        by_rank(b)
                    product_h(k, 1).then_inc(S["act_ps"], 1)
                    if sets:
                        gate_products(b, sets[-1])

            transpose_u(0, 0, 0)
            turns(turn, pe)


def value_phase(nc, a, x1_dram, act_dram, g_dram):
    with ExitStack() as ctx:
        def sb(name, shape, dt=F32):
            return ctx.enter_context(nc.sbuf_tensor("v_" + name, shape, dt))

        def sem(name):
            return ctx.enter_context(nc.semaphore("v_" + name))

        GR = 4
        NGR = NKEYS // GR
        y = sb("y", [P, NB, D])
        v_raw = sb("v_raw", [P, 2, D])
        ga = sb("ga", [P, GR, SEQ])
        g_raw = sb("g_raw", [P, 2, NG, 2, HALF])
        a_hi = sb("a_hi", [P, 2, GR, SEQ], F32R)
        a_lo = sb("a_lo", [P, 2, GR, SEQ], F32R)
        v_hi = sb("v_hi", [P, 2, GR, D], F32R)
        v_lo = sb("v_lo", [P, 2, GR, D], F32R)
        stat = sb("stat", [P, 4, NB])
        ps = ctx.enter_context(nc.psum_tensor("v_ps", [P, 8, 512], F32))
        grow = ga[:, 0, :]
        YS = 4
        x1_in, out_sem, gf_in = sem("x1_in"), sem("out"), sem("gf_in")
        v_in, g_in = ([sem(f"{n}_in{k}") for k in range(2)] for n in "vg")
        a_in = [sem(f"a_in{j}") for j in range(GR)]
        names = "am a_hi a_lo v_hi v_lo y_ps y_ad ss2 ms2 rs2 fin".split()
        S = {n: sem(n) for n in names}
        act_steps, dve_steps = sem("act_steps"), sem("dve_steps")
        block = ctx.enter_context(nc.Block())

        def groups(body, eng):
            for s in range(2):
                body(0, s, first=True)
            with eng.Fori(1, NGR // 2 - 1) as i:
                for s in range(2):
                    body(i, s)
            for s in range(2):
                body(NGR // 2 - 1, s, last=True)

        @block.sync
        def _(sp):
            g_h = g_dram.rearrange("j p e t -> p j e t")

            def body(i, s, first=False, last=False):
                for j in range(GR):
                    e = (i * 2 + s) * GR + j
                    if j % 2 == 0:
                        if not (first and s == 0):
                            sp.wait_ge(S["am"], e - 2)
                        sp.dma_start(g_raw[:, j // 2], g_h[:, :, bass.ds(e, 2), :]).then_inc(g_in[j // 2], 16)
                    if not (first and s == 0):
                        sp.wait_ge(S["a_lo"], e - GR + 1)
                    sp.dma_start(ga[:, j, :], act_dram[e]).then_inc(a_in[j], 16)
                if first and s == 0:
                    sp.dma_start(y[:], x1_dram.rearrange("b p d -> p b d")).then_inc(x1_in, 16)

            groups(body, sp)
            sp.wait_ge(S["a_lo"], NKEYS)
            sp.dma_start(grow, row(a["final_norm_g"], D)).then_inc(gf_in, 16)
            out_h = a["out"][0].rearrange("(b p) d -> b p d", p=P)
            with sp.Fori(0, NB) as b:
                sp.wait_ge(S["fin"], b + 1)
                sp.dma_start(out_h[b], y[:, b, :]).then_inc(out_sem, 16)
            sp.wait_ge(out_sem, 16 * NB)

        @block.gpsimd
        def _(pool):
            v_h = a["peer_v"][0].rearrange("(e p) d -> e p d", p=P)

            def body(i, s, first=False, last=False):
                for j in range(GR):
                    e = (i * 2 + s) * GR + j
                    if not (first and s == 0 and j < 2):
                        pool.wait_ge(S["v_lo"], e - 1)
                    pool.dma_start(v_raw[:, j % 2, :], v_h[e]).then_inc(v_in[j % 2], 16)

            groups(body, pool)

        @block.tensor
        def _(pe):
            def products(s, j, b, half):
                ds = slice(half * 512, (half + 1) * 512)
                ts = slice(b * P, (b + 1) * P)
                for m, (av, vv) in enumerate(((a_hi, v_hi), (a_hi, v_lo), (a_lo, v_hi))):
                    done = nc.tensor.matmul(ps[:, 2 * (b % YS) + half, :], av[:, s, j, ts], vv[:, s, j, ds],
                                            start=(j == 0 and m == 0), stop=(j == GR - 1 and m == 2))
                return done

            def body(i, s, first=False, last=False):
                g = i * 2 + s
                opening = first and s == 0
                if opening:
                    for j in range(GR):
                        pe.wait_ge(S["a_lo"], j + 1)
                        pe.wait_ge(S["v_lo"], j + 1)
                        for b in range(YS):
                            for half in range(2):
                                done = products(s, j, b, half)
                            if j == GR - 1:
                                done.then_inc(S["y_ps"], 1)
                else:
                    pe.wait_ge(S["a_lo"], g * GR + GR)
                    pe.wait_ge(S["v_lo"], g * GR + GR)
                for b in range(YS if opening else 0, NB):
                    pe.wait_ge(S["y_ad"], g * NB + b - YS + 1)
                    for half in range(2):
                        for j in range(GR):
                            done = products(s, j, b, half)
                    done.then_inc(S["y_ps"], 1)

            groups(body, pe)

        @block.scalar
        def _(act):
            def body(i, s, first=False, last=False):
                g = i * 2 + s
                for j in range(GR):
                    e = g * GR + j
                    if j == 0 and not first:
                        act.wait_ge(S["y_ps"], g * NB - NB)
                    act.wait_ge(v_in[j % 2], g * (GR // 2) * 16 + (j // 2) * 16 + 16)
                    nc.scalar.copy(v_hi[:, s, j, :], v_raw[:, j % 2, :]).then_inc(S["v_hi"], 1)
                    act.wait_ge(S["am"], e + 1)
                    nc.scalar.copy(a_hi[:, s, j, :], ga[:, j, :]).then_inc(S["a_hi"], 1)

            groups(body, act)
            for b in range(NB):
                if b == 0:
                    act.wait_ge(S["a_lo"], NKEYS)
                act.wait_ge(S["y_ad"], (NGR - 1) * NB + b + 1)
                nc.scalar.activation(ga[:, 1, :], y[:, b, :], ACT.Square, accum_out=stat[:, 0, b:b + 1]).then_inc(S["ss2"], 1)
                act.wait_ge(S["ms2"], b + 1)
                root = stat[:, 2, b:b + 1]
                Steps(act, act_steps, 1, b).step(nc.scalar.activation(root, stat[:, 1, b:b + 1], ACT.Ln))
                nc.scalar.activation(root, root, ACT.Exp, scale=-0.5).then_inc(S["rs2"], 1)

        @block.vector
        def _(dve):
            def prepare(i, s, j):
                g = i * 2 + s
                e = g * GR + j
                if j % 2 == 0:
                    dve.wait_ge(g_in[j // 2], g * 16 + 16)
                dve.wait_ge(a_in[j], g * 16 + 16)
                v = ga[:, j, :].rearrange("p (j t) -> p j t", j=NG)
                nc.vector.tensor_tensor(v, v, g_raw[:, j // 2, :, j % 2, :], ALU.mult).then_inc(S["am"], 1)
                dve.wait_ge(S["v_hi"], e + 1)
                nc.vector.tensor_tensor(v_lo[:, s, j, :], v_raw[:, j % 2, :], v_hi[:, s, j, :].bitcast(F32),
                                        ALU.subtract).then_inc(S["v_lo"], 1)

            def rest_of_a(i, s, j):
                e = (i * 2 + s) * GR + j
                dve.wait_ge(S["a_hi"], e + 1)
                nc.vector.tensor_tensor(a_lo[:, s, j, :], ga[:, j, :], a_hi[:, s, j, :].bitcast(F32),
                                        ALU.subtract).then_inc(S["a_lo"], 1)

            def add(g, b):
                dve.wait_ge(S["y_ps"], g * NB + b + 1)
                nc.vector.tensor_tensor(y[:, b, :], y[:, b, :],
                                        ps[:, 2 * (b % YS):2 * (b % YS) + 2, :].rearrange("p a b -> p (a b)"),
                                        ALU.add).then_inc(S["y_ad"], 1)

            def body(i, s, first=False, last=False):
                g = i * 2 + s
                for j in range(GR):
                    prepare(i, s, j)
                    if not (first and s == 0):
                        for b in (2 * j, 2 * j + 1):
                            add(g - 1, b)
                            if b == 2 * j:
                                rest_of_a(i, s, j)
                    else:
                        rest_of_a(i, s, j)
                        if j == 0:
                            dve.wait_ge(x1_in, 16)

            groups(body, dve)
            dve.wait_ge(gf_in, 16)
            st = Steps(dve, dve_steps)
            for b in range(NB):
                add(NGR - 1, b)
                mean, root = stat[:, 1, b:b + 1], stat[:, 2, b:b + 1]
                dve.wait_ge(S["ss2"], b + 1)
                st.step(nc.vector.tensor_scalar(mean, stat[:, 0, b:b + 1], 1.0 / D, EPS, ALU.mult, ALU.add))
                dve.sem_inc(S["ms2"], 1)
                dve.wait_ge(S["rs2"], b + 1)
                inverse_root(nc, dve, st, root, mean, stat[:, 3, b:b + 1])
                nc.vector.scalar_tensor_tensor(y[:, b, :], y[:, b, :], root, grow, ALU.mult, ALU.mult).then_inc(S["fin"], 1)


def build(nc, a):
    x1_dram = nc.dram_tensor("x1_scratch", [NB, P, D], F32).ap()
    g_dram = nc.dram_tensor("g_scratch", [NG, P, NKEYS, HALF], F32).ap()
    mix_dram = nc.dram_tensor("mix_scratch", [NB, P, DC, P], F32).ap()
    s_dram = nc.dram_tensor("score_scratch", [NB, P, 2, D], F32).ap()
    act_dram = nc.dram_tensor("act_scratch", [NKEYS, P, SEQ], F32).ap()
    with ExitStack() as across, ExitStack() as signals:
        ident = across.enter_context(nc.sbuf_tensor("ident", [P, P], F32))
        w_out_in, wq_in, score_in, passed, *u_in = (signals.enter_context(nc.semaphore(n)) for n in ("w_out_in", "wq_in", "score_in", "passed", "u_in0", "u_in1"))
        with nc.sbuf_tensor("weights", [P, DC, IN_COLS], F32, side="right") as weights:
            mixer_phase(nc, a, mix_dram, ident, weights, w_out_in, wq_in, passed)
            with (nc.sbuf_tensor("qq", [P, 2, D], F32, side="right") as qq,
                  nc.sbuf_tensor("g2", [P, D], F32, side="right") as g2):
                output_phase(nc, a, mix_dram, x1_dram, weights, w_out_in, wq_in, qq, g2, score_in)
                u_raw = across.enter_context(nc.sbuf_tensor("u_raw", [P, 2, D], F32))
                h_hi, h_lo = (across.enter_context(nc.sbuf_tensor(n, [P, DC, SEQ], F32R)) for n in ("h_hi", "h_lo"))
                score_phase(nc, a, x1_dram, s_dram, ident, weights, wq_in, qq, g2, score_in, h_hi, h_lo, u_raw, u_in)
        choose_phase(nc, a, s_dram, act_dram, g_dram, ident, h_hi, h_lo, u_raw, u_in, passed)
        across.close()
        value_phase(nc, a, x1_dram, act_dram, g_dram)


def kernel(**inputs):
    import concourse.bacc as bacc
    from concourse.bass_utils import run_bass_kernel_spmd

    nc = bacc.Bacc("TRN2", target_bir_lowering=False, num_devices=1)
    arrays = {name: np.ascontiguousarray(inputs[name]) for name in INPUTS}
    arrays.update(shape_constants())
    a = {name: nc.dram_tensor(name, v.shape, mybir.dt.from_np(v.dtype), kind="ExternalInput").ap()
         for name, v in arrays.items()}
    a["out"] = nc.dram_tensor("out", (1, SEQ, D), F32, kind="ExternalOutput").ap()
    build(nc, a)
    result = run_bass_kernel_spmd(nc, [arrays], core_ids=[0])
    return result.results[0]["out"]
```
